# Optimizing a Trainium2 kernel written in Bass

```python
import math
import jax, jax.numpy as jnp
from jax import lax
import numpy as np

D_MODEL = 1024
BATCH = 1
SEQ = 512
DEPTH = 2

MIX_WIDTH = D_MODEL
HEAD_DIM = 64
N_HEADS_DIFF = MIX_WIDTH // (4 * HEAD_DIM)
N_HEADS_FOX = MIX_WIDTH // (2 * HEAD_DIM)
DIFF_WIDTH = N_HEADS_DIFF * 2 * HEAD_DIM
FOX_WIDTH = N_HEADS_FOX * HEAD_DIM
IN_WIDTH = 3 * DIFF_WIDTH + 3 * FOX_WIDTH + N_HEADS_FOX
ROT_DIM = HEAD_DIM // 4
ROPE_THETA = 500000.0
Q_BLOCK = 128
D_FF = ((8 * D_MODEL // 3 + 255) // 256) * 256
EPS = 1e-6
NEG_INF = -1e30


def rms_norm(x, g):
    xf = x.astype(jnp.float32)
    y = xf * lax.rsqrt(jnp.mean(xf * xf, axis=-1, keepdims=True) + EPS)
    return (y * g.astype(jnp.float32)).astype(x.dtype)

def rotary_tables(positions, dtype):
    inv_freq = 1.0 / (ROPE_THETA ** (jnp.arange(0, ROT_DIM, 2, dtype=jnp.float32) / ROT_DIM))
    ang = positions.astype(jnp.float32)[..., None] * inv_freq
    cos = jnp.cos(ang)[:, :, None, :].astype(dtype)
    sin = jnp.sin(ang)[:, :, None, :].astype(dtype)
    return cos, sin

def partial_rotary(t, cos, sin):
    half = ROT_DIM // 2
    t1, t2, rest = t[..., :half], t[..., half:ROT_DIM], t[..., ROT_DIM:]
    return jnp.concatenate([t1 * cos - t2 * sin, t2 * cos + t1 * sin, rest], axis=-1)

def diff_attention(q, k, v, lam):
    b, s = q.shape[0], q.shape[1]
    nb = s // Q_BLOCK
    scale = HEAD_DIM ** -0.5
    q_blocks = q.reshape(b, nb, Q_BLOCK, N_HEADS_DIFF, 2, HEAD_DIM).swapaxes(0, 1)
    k_pos = jnp.arange(s)

    def block(args):
        i, qi = args
        q_pos = i * Q_BLOCK + jnp.arange(Q_BLOCK)
        causal = q_pos[:, None] >= k_pos[None, :]
        logits = jnp.einsum('bqhmd,bkhmd->bhmqk', qi, k).astype(jnp.float32) * scale
        logits = jnp.where(causal, logits, NEG_INF)
        p = jax.nn.softmax(logits, axis=-1)
        p = p[:, :, 0] - lam * p[:, :, 1]
        return jnp.einsum('bhqk,bkhe->bqhe', p.astype(v.dtype), v)

    o = lax.map(block, (jnp.arange(nb), q_blocks))
    return o.swapaxes(0, 1).reshape(b, s, N_HEADS_DIFF, 2 * HEAD_DIM)

def forgetting_attention(q, k, v, log_f):
    b, s = q.shape[0], q.shape[1]
    nb = s // Q_BLOCK
    scale = HEAD_DIM ** -0.5
    c = jnp.cumsum(log_f, axis=1)
    c_k = c.transpose(0, 2, 1)[:, :, None, :]
    q_blocks = q.reshape(b, nb, Q_BLOCK, N_HEADS_FOX, HEAD_DIM).swapaxes(0, 1)
    c_blocks = c.reshape(b, nb, Q_BLOCK, N_HEADS_FOX).swapaxes(0, 1)
    k_pos = jnp.arange(s)

    def block(args):
        i, qi, ci = args
        q_pos = i * Q_BLOCK + jnp.arange(Q_BLOCK)
        causal = q_pos[:, None] >= k_pos[None, :]
        decay = ci.transpose(0, 2, 1)[..., None] - c_k
        logits = jnp.einsum('bqhd,bkhd->bhqk', qi, k).astype(jnp.float32) * scale + decay
        logits = jnp.where(causal, logits, NEG_INF)
        p = jax.nn.softmax(logits, axis=-1)
        return jnp.einsum('bhqk,bkhd->bqhd', p.astype(v.dtype), v)

    o = lax.map(block, (jnp.arange(nb), q_blocks, c_blocks))
    return o.swapaxes(0, 1).reshape(b, s, N_HEADS_FOX, HEAD_DIM)

def first_inputs(seed: int = 0) -> dict:
    key = jax.random.key(seed)
    ks = jax.random.split(key, 16)
    f32 = jnp.float32

    def nrm(k, shape, scale):
        return jax.random.normal(k, shape, f32) * scale

    def gain(k, n):
        return 1.0 + 0.05 * jax.random.normal(k, (DEPTH, n), f32)

    return {
        "x": nrm(ks[0], (BATCH, SEQ, D_MODEL), 1.0),
        "positions": jnp.broadcast_to(jnp.arange(SEQ, dtype=jnp.int32), (BATCH, SEQ)),
        "attn_pre_g": gain(ks[1], D_MODEL),
        "w_in": nrm(ks[2], (DEPTH, D_MODEL, IN_WIDTH), D_MODEL ** -0.5),
        "forget_bias": jax.random.uniform(ks[3], (DEPTH, N_HEADS_FOX), f32, 1.0, 6.0),
        "lam_q1": nrm(ks[4], (DEPTH, HEAD_DIM), 0.1),
        "lam_k1": nrm(ks[5], (DEPTH, HEAD_DIM), 0.1),
        "lam_q2": nrm(ks[6], (DEPTH, HEAD_DIM), 0.1),
        "lam_k2": nrm(ks[7], (DEPTH, HEAD_DIM), 0.1),
        "diff_sub_g": gain(ks[8], 2 * HEAD_DIM),
        "w_out": nrm(ks[9], (DEPTH, MIX_WIDTH, D_MODEL), MIX_WIDTH ** -0.5),
        "attn_post_g": gain(ks[10], D_MODEL),
        "ffn_pre_g": gain(ks[11], D_MODEL),
        "w_gate": nrm(ks[12], (DEPTH, D_MODEL, D_FF), D_MODEL ** -0.5),
        "w_up": nrm(ks[13], (DEPTH, D_MODEL, D_FF), D_MODEL ** -0.5),
        "w_down": nrm(ks[14], (DEPTH, D_FF, D_MODEL), D_FF ** -0.5),
        "ffn_post_g": gain(ks[15], D_MODEL),
    }

def first_block(x, positions, attn_pre_g, w_in, forget_bias, lam_q1, lam_k1, lam_q2, lam_k2,
              diff_sub_g, w_out, attn_post_g, ffn_pre_g, w_gate, w_up, w_down, ffn_post_g):
    b, s, _ = x.shape
    f32 = jnp.float32
    cos, sin = rotary_tables(positions, x.dtype)
    split_at = [DIFF_WIDTH, 2 * DIFF_WIDTH, 3 * DIFF_WIDTH,
                3 * DIFF_WIDTH + FOX_WIDTH, 3 * DIFF_WIDTH + 2 * FOX_WIDTH,
                3 * DIFF_WIDTH + 3 * FOX_WIDTH]
    for l in range(DEPTH):
        h = rms_norm(x, attn_pre_g[l])
        proj = h @ w_in[l]
        qa, ka, va, qb, kb, vb, f_logit = jnp.split(proj, split_at, axis=-1)

        qa = partial_rotary(qa.reshape(b, s, 2 * N_HEADS_DIFF, HEAD_DIM), cos, sin)
        ka = partial_rotary(ka.reshape(b, s, 2 * N_HEADS_DIFF, HEAD_DIM), cos, sin)
        qa = qa.reshape(b, s, N_HEADS_DIFF, 2, HEAD_DIM)
        ka = ka.reshape(b, s, N_HEADS_DIFF, 2, HEAD_DIM)
        va = va.reshape(b, s, N_HEADS_DIFF, 2 * HEAD_DIM)
        lam_init = 0.8 - 0.6 * math.exp(-0.3 * l)
        lam = (jnp.exp(jnp.sum(lam_q1[l].astype(f32) * lam_k1[l].astype(f32)))
               - jnp.exp(jnp.sum(lam_q2[l].astype(f32) * lam_k2[l].astype(f32)))
               + lam_init)
        oa = diff_attention(qa, ka, va, lam)
        oa = rms_norm(oa, diff_sub_g[l]) * (1.0 - lam_init)

        log_f = jax.nn.log_sigmoid(f_logit.astype(f32) + forget_bias[l].astype(f32))
        ob = forgetting_attention(qb.reshape(b, s, N_HEADS_FOX, HEAD_DIM),
                                  kb.reshape(b, s, N_HEADS_FOX, HEAD_DIM),
                                  vb.reshape(b, s, N_HEADS_FOX, HEAD_DIM), log_f)

        mixed = jnp.concatenate([oa.reshape(b, s, DIFF_WIDTH), ob.reshape(b, s, FOX_WIDTH)], axis=-1)
        x = x + rms_norm(mixed @ w_out[l], attn_post_g[l])

        h = rms_norm(x, ffn_pre_g[l])
        y = (jax.nn.silu(h @ w_gate[l]) * (h @ w_up[l])) @ w_down[l]
        x = x + rms_norm(y, ffn_post_g[l])
    return x


N_MIXERS = 2
SB_HEADS = 16
SB_HEAD_DIM = D_MODEL // SB_HEADS
HG_EXPAND = 128
HG_HEADS = D_MODEL // HG_EXPAND
HG_KEY_DIM = HG_EXPAND
HG_VAL_DIM = D_MODEL // HG_HEADS
HG_CHUNK = 64
D_FF_2 = 4 * D_MODEL
N_SB = (DEPTH + N_MIXERS - 1) // N_MIXERS
N_HG = DEPTH // N_MIXERS


def rmsnorm(x, gain):
    xf = x.astype(jnp.float32)
    y = xf * lax.rsqrt(jnp.mean(xf * xf, axis=-1, keepdims=True) + EPS)
    return (y * gain.astype(jnp.float32)).astype(x.dtype)

def stick_breaking_attention(q, k, v):
    seq = q.shape[2]
    scale = 1.0 / math.sqrt(q.shape[-1])
    outs = []
    for t0 in range(0, seq, Q_BLOCK):
        t1 = t0 + Q_BLOCK
        z = jnp.einsum('bhqd,bhkd->bhqk', q[:, :, t0:t1], k[:, :, :t1]).astype(jnp.float32) * scale
        causal = jnp.arange(t1)[None, :] < (t0 + jnp.arange(Q_BLOCK))[:, None]
        log_stay = jnp.where(causal, jax.nn.log_sigmoid(-z), 0.0)
        log_between = lax.cumsum(log_stay, axis=3, reverse=True) - log_stay
        weights = jnp.where(causal, jnp.exp(jax.nn.log_sigmoid(z) + log_between), 0.0)
        outs.append(jnp.einsum('bhqk,bhkd->bhqd', weights.astype(v.dtype), v[:, :, :t1]))
    return jnp.concatenate(outs, axis=2)

def stick_breaking_mixer(h, w_qkv, q_gain, k_gain, w_o):
    bsz, seq, _ = h.shape
    qkv = h @ w_qkv
    q, k, v = jnp.split(qkv, 3, axis=-1)
    q = rmsnorm(q.reshape(bsz, seq, SB_HEADS, SB_HEAD_DIM), q_gain)
    k = rmsnorm(k.reshape(bsz, seq, SB_HEADS, SB_HEAD_DIM), k_gain)
    v = v.reshape(bsz, seq, SB_HEADS, SB_HEAD_DIM)
    q, k, v = (jnp.transpose(a, (0, 2, 1, 3)) for a in (q, k, v))
    o = stick_breaking_attention(q, k, v)
    o = jnp.transpose(o, (0, 2, 1, 3)).reshape(bsz, seq, D_MODEL)
    return o @ w_o

def hgrn2_chunk_scan(q, k, v, log_f):
    bsz, nh, seq, dk = q.shape
    dv = v.shape[-1]
    n_chunks = seq // HG_CHUNK

    def to_chunks(a):
        return jnp.moveaxis(a.astype(jnp.float32).reshape(bsz, nh, n_chunks, HG_CHUNK, a.shape[-1]), 2, 0)

    incl = jnp.tril(jnp.ones((HG_CHUNK, HG_CHUNK), dtype=bool))

    def step(state, inp):
        qc, kc, vc, lfc = inp
        b = jnp.cumsum(lfc, axis=2)
        inter = jnp.einsum('bhck,bhkv->bhcv', qc * jnp.exp(b), state)
        diff = b[:, :, :, None, :] - b[:, :, None, :, :]
        decay = jnp.where(incl[:, :, None], jnp.exp(jnp.minimum(diff, 0.0)), 0.0)
        scores = jnp.einsum('bhtk,bhsk,bhtsk->bhts', qc, kc, decay)
        intra = jnp.einsum('bhts,bhsv->bhtv', scores, vc)
        b_last = b[:, :, -1:, :]
        new_state = (jnp.exp(b_last[:, :, 0, :])[..., None] * state
                     + jnp.einsum('bhsk,bhsv->bhkv', kc * jnp.exp(b_last - b), vc))
        return new_state, inter + intra

    init = jnp.zeros((bsz, nh, dk, dv), jnp.float32)
    _, ys = lax.scan(step, init, (to_chunks(q), to_chunks(k), to_chunks(v), to_chunks(log_f)))
    return jnp.moveaxis(ys, 0, 2).reshape(bsz, nh, seq, dv)

def hgrn2_mixer(h, w_in, lower_bound, norm_gain, w_o):
    bsz, seq, _ = h.shape
    proj = h @ w_in
    q, f, i, g = jnp.split(proj, 4, axis=-1)
    q = jax.nn.silu(q)
    lb = lower_bound.astype(jnp.float32)
    forget = lb + (1.0 - lb) * jax.nn.sigmoid(f.astype(jnp.float32))
    log_f = jnp.log(forget)
    k = -jnp.expm1(log_f)

    def heads(a, d):
        return jnp.transpose(a.reshape(bsz, seq, HG_HEADS, d), (0, 2, 1, 3))

    o = hgrn2_chunk_scan(heads(q, HG_KEY_DIM), heads(k, HG_KEY_DIM),
                         heads(i, HG_VAL_DIM), heads(log_f, HG_KEY_DIM))
    o = jnp.transpose(o, (0, 2, 1, 3)).astype(h.dtype)
    o = rmsnorm(o, norm_gain).reshape(bsz, seq, D_MODEL)
    o = o * jax.nn.sigmoid(g)
    return o @ w_o

def squared_relu_mlp(h, w1, w2):
    a = jax.nn.relu(h @ w1)
    return (a * a) @ w2

def second_inputs(seed: int = 0) -> dict:
    key = jax.random.key(seed)
    ks = jax.random.split(key, 12)
    d_in = D_MODEL ** -0.5
    res = (2 * DEPTH) ** -0.5
    nrm = jax.random.normal
    return {
        "x": nrm(ks[0], (BATCH, SEQ, D_MODEL), jnp.float32),
        "norm_gains": 1.0 + 0.02 * nrm(ks[1], (DEPTH, 2, D_MODEL), jnp.float32),
        "sb_w_qkv": nrm(ks[2], (N_SB, D_MODEL, 3 * D_MODEL), jnp.float32) * d_in,
        "sb_q_gain": 1.0 + 0.02 * nrm(ks[3], (N_SB, SB_HEAD_DIM), jnp.float32),
        "sb_k_gain": 1.0 + 0.02 * nrm(ks[4], (N_SB, SB_HEAD_DIM), jnp.float32),
        "sb_w_o": nrm(ks[5], (N_SB, D_MODEL, D_MODEL), jnp.float32) * d_in * res,
        "hg_w_in": nrm(ks[6], (N_HG, D_MODEL, 4 * D_MODEL), jnp.float32) * d_in,
        "hg_lb_logits": 0.5 * nrm(ks[7], (N_HG, D_MODEL), jnp.float32),
        "hg_norm_gain": 1.0 + 0.02 * nrm(ks[8], (N_HG, HG_VAL_DIM), jnp.float32),
        "hg_w_o": nrm(ks[9], (N_HG, D_MODEL, D_MODEL), jnp.float32) * d_in * res,
        "mlp_w1": nrm(ks[10], (DEPTH, D_MODEL, D_FF_2), jnp.float32) * d_in,
        "mlp_w2": nrm(ks[11], (DEPTH, D_FF_2, D_MODEL), jnp.float32) * (D_FF_2 ** -0.5) * res,
    }

def second_block(x, norm_gains, sb_w_qkv, sb_q_gain, sb_k_gain, sb_w_o,
              hg_w_in, hg_lb_logits, hg_norm_gain, hg_w_o, mlp_w1, mlp_w2):
    p = jax.nn.softmax(hg_lb_logits.astype(jnp.float32), axis=0)
    lower_bounds = jnp.cumsum(p, axis=0) - p[0:1]
    for layer in range(DEPTH):
        j = layer // N_MIXERS
        h = rmsnorm(x, norm_gains[layer, 0])
        if layer % N_MIXERS == 0:
            x = x + stick_breaking_mixer(h, sb_w_qkv[j], sb_q_gain[j], sb_k_gain[j], sb_w_o[j])
        else:
            x = x + hgrn2_mixer(h, hg_w_in[j], lower_bounds[j], hg_norm_gain[j], hg_w_o[j])
        h = rmsnorm(x, norm_gains[layer, 1])
        x = x + squared_relu_mlp(h, mlp_w1[layer], mlp_w2[layer])
    return x


def setup_inputs(seed=0):
    out = dict(first_inputs(seed))
    for name, value in second_inputs(seed + 1).items():
        if name != "x":
            out[name + "_2"] = value
    return out


def reference(
    x, positions, attn_pre_g, w_in, forget_bias, lam_q1, lam_k1, lam_q2, lam_k2, diff_sub_g,
    w_out, attn_post_g, ffn_pre_g, w_gate, w_up, w_down, ffn_post_g, norm_gains_2, sb_w_qkv_2,
    sb_q_gain_2, sb_k_gain_2, sb_w_o_2, hg_w_in_2, hg_lb_logits_2, hg_norm_gain_2, hg_w_o_2,
    mlp_w1_2, mlp_w2_2,
):
    x = first_block(
        x, positions, attn_pre_g, w_in, forget_bias, lam_q1, lam_k1, lam_q2, lam_k2, diff_sub_g,
        w_out, attn_post_g, ffn_pre_g, w_gate, w_up, w_down, ffn_post_g,
    )
    return second_block(
        x, norm_gains_2, sb_w_qkv_2, sb_q_gain_2, sb_k_gain_2, sb_w_o_2, hg_w_in_2,
        hg_lb_logits_2, hg_norm_gain_2, hg_w_o_2, mlp_w1_2, mlp_w2_2,
    )


_drawn_inputs = setup_inputs


def setup_inputs(seed=0):
    import zlib

    import numpy as np

    out = dict(_drawn_inputs(seed))
    spreads = {}
    factors = {'norm_gains_2': 5.861, 'sb_q_gain_2': 8.0, 'sb_k_gain_2': 8.0, 'hg_norm_gain_2': 8.0}
    for name, (base, spread) in spreads.items():
        noise = np.random.default_rng([zlib.crc32(name.encode()), seed]).standard_normal(out[name].shape)
        drawn = base * np.exp(spread * noise) if base else spread * noise
        out[name] = __import__('jax').numpy.asarray(drawn.astype(out[name].dtype))
    for name, factor in factors.items():
        out[name] = (out[name] * factor).astype(out[name].dtype)
    return out
```

```python
import math
from contextlib import ExitStack

import numpy as np
import concourse.bass as bass
from concourse import mybir

F32 = mybir.dt.float32
F32R = mybir.dt.float32r
I32 = mybir.dt.int32
ALU = mybir.AluOpType
ACT = mybir.ActivationFunctionType
AX_X = mybir.AxisListType.X
ds = bass.ds

P = 128
S = 512
D = 1024
KD = D // P
NB = S // P
LAYERS = 2
HD = 64
DIFF_W = 512
FOX_W = 512
FF1 = 2816
FF2 = 4096
EPS = 1e-6
NEG = -1e30
ROT_HALF = 8
THETA = 500000.0

FF1_CHUNKS = [(0, 8), (8, 8), (16, 6)]
FF1_TILES = FF1 // P
FF2_CHUNKS = [(0, 8), (8, 8), (16, 8), (24, 8)]
U_ATT, U_OUT, U_GU0, U_GU1, U_D0, U_GU2, U_D1, U_D2, U_LAYER = 0, 24, 32, 48, 64, 72, 84, 92, 100
FFN_ORDER = [("gu", 0, U_GU0), ("gu", 1, U_GU1), ("down", 0, U_D0), ("gu", 2, U_GU2), ("down", 1, U_D1),
             ("down", 2, U_D2)]
PAIRS = 8
NDIFF = 4
SLOTS = 12
HEAD_TILES = 8
T_OF = [4 if p < NDIFF else 8 for p in range(PAIRS)]
T_BASE = [sum(T_OF[:p]) for p in range(PAIRS + 1)]
LAM_INIT = [0.8 - 0.6 * math.exp(-0.3 * l) for l in range(LAYERS)]

G_ATT_PRE, G_B2, G_ATT_POST, G_FFN_PRE, G_FFN_POST, G_LB, G_DIFF, G_HG, G_SBQ, G_SBK, G_ROWS = (
    0, 16, 48, 64, 80, 96, 104, 106, 107, 108, 109)


def aux_uses():
    uses = []
    for p in range(-1, PAIRS):
        for k in range(SLOTS):
            if p == -1 and k == 3:
                uses.append("norm_att")
            if k == 1 and p >= 0:
                uses.append(("v", p))
            if k == 4 and 0 <= p - 1 < NDIFF:
                uses.append(("o_norm", p - 1))
            if k == 6 and p + 1 < NDIFF:
                uses.append(("rot_q", p + 1))
            if k == 9 and p + 1 < NDIFF:
                uses.append(("rot_k", p + 1))
    uses += ["norm_att_post", "norm_ffn", "norm_ffn_post"]
    return {u: i for i, u in enumerate(uses)}


AUX = aux_uses()
A_LAYER = len(AUX)

U2 = LAYERS * U_LAYER
U_SB, U_SBO, U_M1 = U2, U2 + 24, U2 + 32
U_HG = U_M1 + 64
U_HGO, U_M2 = U_HG + 32, U_HG + 40
U_END = U_M2 + 64
MLP_ORDER = [("up", 0), ("up", 1), ("down", 0), ("up", 2), ("down", 1), ("up", 3), ("down", 2), ("down", 3)]
MLP_UNITS = [(kind, c, 8 * i) for i, (kind, c) in enumerate(MLP_ORDER)]
Z_AT = [0, 512, 896, 1152]
Z_N = [512, 384, 256, 128]
Z_W = 1280
Z_BANK = [(0, 0), (1, 0), (2, 0), (2, 256)]
Z_PARTS = [(2, (2, 3), 896, 384), (1, (1,), 512, 384), (0, (0,), 0, 512)]
A_SB = LAYERS * A_LAYER
A_M1 = A_SB + 3 * PAIRS + 1
MID1 = LAYERS * FF1_TILES
A_HG = A_M1 + 1
A_M2 = A_HG + 17
U_LAST = U_END
HG_SLOTS = 16
HALVES = [64, 32, 16, 8, 4, 2, 1]


def a_hgv(i, first=False):
    return A_HG + 1 if first else A_HG + 2 * i



def added_base(n):
    return 2 + KD * n


def block2_norm(i):
    return KD * (2 * LAYERS + i), KD * (4 * LAYERS + i), added_base(2 * LAYERS + i - 1)


VEC_STEPS_LAYER = 93
SB_STEPS = 40
SB_ACT_STEPS = 24
HG_STEPS = 6
HG_ACT_STEPS = 14
ACT_STEPS_LAYER = 46


class Steps:

    def __init__(self, engine, sem):
        self.engine, self.sem, self.base, self.n, self.outer = engine, sem, 0, 0, []

    def __call__(self, instruction):
        instruction.then_inc(self.sem, 1)
        self.n += 1

    def wait(self):
        self.engine.wait_ge(self.sem, self.base + self.n)

    def enter(self, i, per):
        self.outer.append((self.base, self.n, per))
        self.base, self.n = self.base + self.n + i * per, 0

    def leave(self, times):
        base, n, per = self.outer.pop()
        assert self.n == per, (self.n, per)
        self.base, self.n = base, n + times * per


def two_blocks(nc, x, positions, attn_pre_g, w_in, forget_bias, lam_q1, lam_k1, lam_q2, lam_k2, diff_sub_g,
               w_out, attn_post_g, ffn_pre_g, w_gate, w_up, w_down, ffn_post_g, norm_gains_2, sb_w_qkv_2,
               sb_q_gain_2, sb_k_gain_2, sb_w_o_2, hg_w_in_2, hg_lb_logits_2, hg_norm_gain_2, hg_w_o_2,
               mlp_w1_2, mlp_w2_2, out):
    with ExitStack() as ctx:
        def sb(name, shape, dt=F32):
            return ctx.enter_context(nc.sbuf_tensor(name, shape, dt))

        def sem(name):
            return ctx.enter_context(nc.semaphore(name))

        xT = sb("xT", [P, KD, S])
        h_hi = sb("h_hi", [P, KD, S], F32R)
        h_lo = sb("h_lo", [P, KD, S], F32R)
        mid_hi = sb("mid_hi", [P, 2, HEAD_TILES, S], F32R)
        mid_lo = sb("mid_lo", [P, 2, HEAD_TILES, S], F32R)
        yT = sb("yT", [P, KD, S])
        w_raw = sb("w_raw", [P, 2, 8, P])
        w_hi = sb("w_hi", [P, 2, 8, P], F32R)
        w_lo = sb("w_lo", [P, 2, 8, P], F32R)
        scratch = sb("scratch", [P, 6144])
        rstd = sb("rstd", [P, S])
        ident = sb("ident", [P, P])
        ident_r = sb("ident_r", [P, P], F32R)
        mask_r = sb("mask_r", [P, P], F32R)
        ones = sb("ones", [P, S])
        rotT = sb("rotT", [P, P])
        cosT = sb("cosT", [P, S])
        sinT = sb("sinT", [P, S])
        gains = sb("gains", [P, G_ROWS])
        layer_gain = sb("layer_gain", [P, 4, KD])
        lconst = sb("lconst", [P, LAYERS, 4])
        lcur = sb("lcur", [P, 4])
        eps_col = sb("eps_col", [P, 1])
        neg_incl_r = sb("neg_incl_r", [P, P], F32R)
        neg_ones_r = sb("neg_ones_r", [P, P], F32R)
        mask_sb_r = sb("mask_sb_r", [P, P], F32R)
        before01 = sb("before01", [P, P])
        head_ones = sb("head_ones", [P, P])
        sb_gain = sb("sb_gain", [P, 2])
        hdiag_t = sb("hdiag_t", [P, S])
        hoff_t = sb("hoff_t", [P, 768])
        lower = sb("lower", [P, 4, KD])
        hg_col = sb("hg_col", [P, 1])
        level_mask = sb("level_mask", [P, len(HALVES), NB * HD], mybir.dt.uint8)
        same_mask = sb("same_mask", [P, NB * P], mybir.dt.uint8)
        stat = sb("stat", [P, 16])
        sel_r = sb("sel_r", [P, 8, P], F32R)

        def part(a, n, *shape):
            t = yT.rearrange("p a b -> p (a b)")[:, a:a + n] if a < KD * S else scratch[:, a - KD * S:a - KD * S + n]
            return t

        wf_raw = sb("wf_raw", [P, 8, P])
        wf_flat = wf_raw.rearrange("p k c -> p (k c)")
        negc = sb("negc", [P, S])
        raw = part(0, 512)
        vraw = part(512, 512)
        vtok = part(1024, 512).rearrange("p (j c) -> p j c", j=NB)
        rcos = part(1536, 512)
        rsin = part(2048, 512)
        orow = part(2560, 512)
        osq = part(3072, 512)
        onrm = part(3584, 512)
        qT = [part(4096 + 512 * i, 512) for i in range(2)]
        kT = [part(5120 + 512 * i, 512) for i in range(2)]
        prob = [part(6144 + 512 * i, 512) for i in range(4)]
        probT = [part(8192 + 512 * i, 512) for i in range(2)]
        ologs = part(9216, 512)
        raw_f, ologs_f = osq, orow
        logs = part(9728, 512)
        square = [part(4096 + 512 * i, 512) for i in range(2)]
        square_sum = part(5120, 512)
        gate = part(5632, 512)
        gate_t = part(6144, 512)
        gate_t2 = part(6656, 512)
        up = part(7168, 512)
        hid = part(7680, 512)
        sb_orow = part(1536, 512)
        sb_sq = part(2048, 512)
        sb_logs = part(2560, 512)
        sb_log = part(4096, Z_W)
        sb_stay = part(4096 + Z_W, Z_W)
        sb_w = part(4096 + 2 * Z_W, Z_W)
        sqT = [part(7936 + 512 * i, 512) for i in range(2)]
        skT = [part(8960 + 512 * i, 512) for i in range(2)]
        stay_hi = mid_hi[:, 1].rearrange("p a b -> p (a b)")[:, 0:Z_W]
        stay_lo = mid_lo[:, 1].rearrange("p a b -> p (a b)")[:, 0:Z_W]
        tile_of = [part(512 * i, 512) for i in range(20)] + [cosT[:], sinT[:], negc[:], wf_flat[:, 0:512], wf_flat[:, 512:1024]]
        hq, hk, hb = tile_of[0:2], tile_of[2:4], tile_of[4:6]
        hvraw, hvtok, hgraw, hgsig = tile_of[6], tile_of[7].rearrange("p (j c) -> p j c", j=NB), tile_of[11], tile_of[12]
        horow, hosq, hors = tile_of[13:16]
        hraw, ht1, ht2, hfd = tile_of[16:20]
        hx = tile_of[20:23]
        hx128, hx256 = tile_of[23], tile_of[24]
        hdiag = hdiag_t[:]
        hoff = hoff_t[:]
        decay_r = mid_lo[:, 1, 0:2]
        wf_hi = mid_hi[:, 1].rearrange("p a b -> p (a b)")[:, 0:1024].rearrange("p (k c) -> p k c", k=8)
        wf_lo = mid_hi[:, 1].rearrange("p a b -> p (a b)")[:, 1024:2048].rearrange("p (k c) -> p k c", k=8)

        def psum(name):
            return ctx.enter_context(nc.psum_tensor(name, [P, S], F32))

        acc = [psum("acc0"), psum("acc1")]
        sc = [psum("sc0"), psum("sc1")]
        tp = [psum("tp0"), psum("tp1")]
        po = psum("po")
        aux = psum("aux")

        consts_in = sem("consts_in")
        x_in = sem("x_in")
        w_landed = [sem("w_landed0"), sem("w_landed1")]
        w_split = sem("w_split")
        unit_done = sem("unit_done")
        load_turn = sem("load_turn")
        split_turn = sem("split_turn")
        pred_turn = sem("pred_turn")
        evacuated = [sem("evacuated0"), sem("evacuated1")]
        pool_consts = sem("pool_consts")
        pool_step = sem("pool_step")
        vec_consts = sem("vec_consts")
        vec_step = sem("vec_step")
        act_step = sem("act_step")
        act_consts = sem("act_consts")
        pre_pe = sem("pre_pe")
        pre_taken = sem("pre_taken")
        x_ready = sem("x_ready")
        h_hi_ready = sem("h_hi_ready")
        h_ready = sem("h_ready")
        square_ready = sem("square_ready")
        square_added = sem("square_added")
        square_summed = sem("square_summed")
        y_scaled = sem("y_scaled")
        rstd_ready = sem("rstd_ready")
        layer_const = sem("layer_const")
        aux_done = sem("aux_done")
        aux_free = sem("aux_free")
        qk_ready = sem("qk_ready")
        score_done = sem("score_done")
        max_done = sem("max_done")
        exp_done = sem("exp_done")
        p_ready = sem("p_ready")
        t_done = sem("t_done")
        t_taken = sem("t_taken")
        pv_done = sem("pv_done")
        po_taken = sem("po_taken")
        o_square = sem("o_square")
        o_rstd = sem("o_rstd")
        o_normed = sem("o_normed")
        o_hi_ready = sem("o_hi_ready")
        o_ready = sem("o_ready")
        wf_landed = sem("wf_landed")
        wf_split = sem("wf_split")
        wf_done = sem("wf_done")
        f_taken = sem("f_taken")
        f_ready = sem("f_ready")
        f_log = sem("f_log")
        decay_ready = sem("decay_ready")
        gate_log = sem("gate_log")
        raw_square = sem("raw_square")
        hg_fm = sem("hg_fm")
        hg_flog = sem("hg_flog")
        hg_flb = sem("hg_flb")
        hg_fd = sem("hg_fd")
        hg_fexp = sem("hg_fexp")
        hg_k = sem("hg_k")
        hg_qlog = sem("hg_qlog")
        hg_qls = sem("hg_qls")
        hg_qsig = sem("hg_qsig")
        hg_q = sem("hg_q")
        hg_glog = sem("hg_glog")
        hg_gls = sem("hg_gls")
        hg_gsig = sem("hg_gsig")
        hg_sub = sem("hg_sub")
        hg_exp = sem("hg_exp")
        hg_mul = sem("hg_mul")
        hg_mm = sem("hg_mm")
        hg_pred = sem("hg_pred")
        hg_offexp = sem("hg_offexp")
        hg_offmul = sem("hg_offmul")
        hg_offmm = sem("hg_offmm")
        hg_offtaken = sem("hg_offtaken")
        hg_bias = sem("hg_bias")
        hg_pv = sem("hg_pv")
        hg_otaken = sem("hg_otaken")
        hg_osq = sem("hg_osq")
        hg_ors = sem("hg_ors")
        hg_on = sem("hg_on")
        hg_ohi = sem("hg_ohi")
        hg_oready = sem("hg_oready")
        hg_b = sem("hg_b")
        hg_graw = sem("hg_graw")
        lb_step = sem("lb_step")
        raw_rstd = sem("raw_rstd")
        sbqk_ready = sem("sbqk_ready")
        z_done = sem("z_done")
        z_log = sem("z_log")
        stay_ready = sem("stay_ready")
        logw_done = sem("logw_done")
        w_ready = sem("w_ready")
        sbpv_done = sem("sbpv_done")
        sbo_taken = sem("sbo_taken")
        sbo_hi = sem("sbo_hi")
        sbo_ready = sem("sbo_ready")
        gate_ls = sem("gate_ls")
        gate_sig = sem("gate_sig")
        gu_done = sem("gu_done")
        hid_ready = sem("hid_ready")
        mid_hi_ready = sem("mid_hi_ready")
        mid_ready = sem("mid_ready")
        out_ready = sem("out_ready")
        out_stored = sem("out_stored")

        def tiles(w):
            return w.rearrange("l (k p) c -> p (l k) c", p=P)

        w_in_t, w_out_t, w_gate_t, w_up_t, w_down_t = map(tiles, (w_in, w_out, w_gate, w_up, w_down))
        sb_qkv_t, sb_o_t, hg_in_t, hg_o_t, w1_t, w2_t = map(
            tiles, (sb_w_qkv_2, sb_w_o_2, hg_w_in_2, hg_w_o_2, mlp_w1_2, mlp_w2_2))
        x_rows = x.rearrange("b (t p) d -> p (b t) d", p=P)
        out_rows = out.rearrange("b (t p) d -> p (b t) d", p=P)
        x_tok = yT.rearrange("p a b -> p (a b)").rearrange("p (t d) -> p t d", t=NB)
        grow = scratch[:, 0:128]
        lam_in = scratch[:, 5568:5568 + 4 * LAYERS * HD].rearrange("p (v l c) -> p v l c", v=4, l=LAYERS)
        pos_i = scratch[:, 1024:1536].bitcast(I32)
        ang = scratch[:, 1536:2048]
        turn = scratch[:, 2048:2560]
        red = scratch[:, 2560:3072]
        inv_row = scratch[:, 3072:3200]
        inv_col = scratch[:, 3200:3201]
        lam_p = scratch[:, 3264:3264 + 2 * LAYERS * HD].rearrange("p (v l c) -> p v l c", v=2, l=LAYERS)
        lam_s = scratch[:, 3584:3584 + 2 * LAYERS]
        lam_e = scratch[:, 3600:3600 + 2 * LAYERS]
        mask_f = scratch[:, 3712:3840]
        neg_incl_f = scratch[:, 3840:3968]
        mask_sb_f = scratch[:, 3968:4096]
        sel_f = scratch[:, 4096:5120].rearrange("p (h c) -> p h c", h=8)
        level_f = scratch[:, 5120:5120 + len(HALVES) * HD].rearrange("p (i q) -> p i q", i=len(HALVES))
        N_CONSTS = 14 + 4

        block = ctx.enter_context(nc.Block())

        @block.sync
        def _(sp):
            for t in range(NB):
                sp.dma_start(x_tok[:, t], x_rows[:, t]).then_inc(x_in, 16)

            def load(half, slot, w, row, k, col):
                sp.wait_ge(w_split, 2 * half + slot + 1)
                sp.sem_inc(load_turn, 1)
                sp.dma_start(w_raw[:, slot, 0:k], w[:, ds(row, k), ds(col, P)]).then_inc(w_landed[slot], 16)

            def load_wf(l):
                sp.wait_ge(wf_split, l + 1)
                sp.sem_inc(load_turn, 1)
                sp.dma_start(wf_raw[:], w_in_t[:, ds(l * KD, KD), w_in.shape[2] - P:w_in.shape[2]]).then_inc(wf_landed, 16)

            with sp.Fori(0, LAYERS) as l:
                load_wf(l)
                for p in range(PAIRS):
                    q_col = p * P if p < NDIFF else 3 * DIFF_W + (p - NDIFF) * P
                    for i in range(3):
                        n = 3 * p + i
                        load(l * (U_LAYER // 2) + n // 2, n % 2, w_in_t, l * KD, KD, q_col + i * DIFF_W)
                with sp.Fori(0, KD // 2) as m:
                    for i in range(2):
                        load(l * (U_LAYER // 2) + U_OUT // 2 + m, i, w_out_t, l * KD, KD, m * 2 * P + i * P)
                for kind, c, u in FFN_ORDER:
                    first, n = FF1_CHUNKS[c]
                    half = l * (U_LAYER // 2) + u // 2
                    if kind == "gu":
                        with sp.Fori(0, n) as j:
                            load(half + j, 0, w_gate_t, l * KD, KD, j * P + first * P)
                            load(half + j, 1, w_up_t, l * KD, KD, j * P + first * P)
                    else:
                        with sp.Fori(0, KD // 2) as m:
                            for i in range(2):
                                load(half + m, i, w_down_t, l * FF1_TILES + first, n, m * 2 * P + i * P)
            def load_square(u, w):
                with sp.Fori(0, KD // 2) as m:
                    for i in range(2):
                        load(u // 2 + m, i, w, 0, KD, m * 2 * P + i * P)

            def load_mlp(mlp, u0):
                for kind, c, u in MLP_UNITS:
                    with sp.Fori(0, KD // 2) as m:
                        for i in range(2):
                            col = m * 2 * P + i * P
                            if kind == "up":
                                load((u0 + u) // 2 + m, i, w1_t, mlp * KD, KD, col + c * D)
                            else:
                                load((u0 + u) // 2 + m, i, w2_t, mlp * (FF2 // P) + c * 8, 8, col)

            with sp.Fori(0, PAIRS // 2) as pp:
                for par in range(2):
                    for i in range(3):
                        u = 3 * par + i
                        load(U_SB // 2 + 3 * pp + u // 2, u % 2, sb_qkv_t, 0, KD, pp * 2 * P + par * P + i * D)
            load_square(U_SBO, sb_o_t)
            load_mlp(0, U_M1)
            with sp.Fori(0, KD) as i:
                for n, which in enumerate((1, 0, 2, 3)):
                    load(U_HG // 2 + 2 * i + n // 2, n % 2, hg_in_t, 0, KD, i * P + which * D)
            load_square(U_HGO, hg_o_t)
            load_mlp(1, U_M2)
            for t in range(NB):
                sp.wait_ge(out_ready, t + 1)
                sp.dma_start(out_rows[:, t], x_tok[:, t]).then_inc(out_stored, 16)
            sp.wait_ge(out_stored, 16 * NB)

        @block.gpsimd
        def _(pool):
            steps = Steps(pool, pool_step)
            steps(nc.gpsimd.memset(ident[:], 0.0))
            steps(nc.gpsimd.memset(rotT[:], 0.0))
            steps(nc.gpsimd.memset(mask_f, 0.0))
            steps(nc.gpsimd.memset(sel_f, 0.0))
            steps(nc.gpsimd.memset(neg_incl_f, -1.0))
            steps(nc.gpsimd.memset(mask_sb_f, NEG))
            steps(nc.gpsimd.memset(before01[:], 1.0))
            steps(nc.gpsimd.memset(level_f, 1.0))
            steps.wait()
            nc.gpsimd.affine_select(out=ident[:], in_=ident[:], compare_op=ALU.not_equal, fill=1.0, base=0,
                                    pattern=[[-1, P]], channel_multiplier=1).then_inc(pool_consts, 1)
            nc.gpsimd.affine_select(out=mask_f, in_=mask_f, compare_op=ALU.is_ge, fill=NEG, base=0,
                                    pattern=[[-1, P]], channel_multiplier=1).then_inc(pool_consts, 1)
            heads = rotT[:].rearrange("p (b c) -> p b c", b=2)
            lower, upper = heads[:, :, 0:ROT_HALF], heads[:, :, ROT_HALF:2 * ROT_HALF]
            nc.gpsimd.affine_select(out=lower, in_=lower, compare_op=ALU.not_equal, fill=-1.0, base=-ROT_HALF,
                                    pattern=[[-HD, 2], [-1, ROT_HALF]], channel_multiplier=1).then_inc(pool_consts, 1)
            nc.gpsimd.affine_select(out=upper, in_=upper, compare_op=ALU.not_equal, fill=1.0, base=0,
                                    pattern=[[-HD, 2], [-1, ROT_HALF]], channel_multiplier=1).then_inc(pool_consts, 1)
            nc.gpsimd.affine_select(out=sel_f, in_=sel_f, compare_op=ALU.not_equal, fill=1.0, base=-120,
                                    pattern=[[-1, 8], [0, P]], channel_multiplier=1).then_inc(pool_consts, 1)
            for t in (neg_incl_f, mask_sb_f):
                nc.gpsimd.affine_select(out=t, in_=t, compare_op=ALU.is_ge, fill=0.0, base=0,
                                        pattern=[[-1, P]], channel_multiplier=1).then_inc(pool_consts, 1)
            nc.gpsimd.affine_select(out=before01[:], in_=before01[:], compare_op=ALU.is_ge, fill=0.0, base=-1,
                                    pattern=[[1, P]], channel_multiplier=-1).then_inc(pool_consts, 1)
            for i, h in enumerate(HALVES):
                m = level_f[:, i].rearrange("p (n j) -> p n j", j=h)
                steps(nc.gpsimd.affine_select(out=m, in_=m, compare_op=ALU.is_ge, fill=0.0, base=0,
                                              pattern=[[-2 * h, HD // h], [0, h]], channel_multiplier=1))
            steps.wait()
            for i, h in enumerate(HALVES):
                m = level_f[:, i].rearrange("p (n j) -> p n j", j=h)
                nc.gpsimd.affine_select(out=m, in_=m, compare_op=ALU.is_ge, fill=0.0, base=h - 1,
                                        pattern=[[2 * h, HD // h], [0, h]], channel_multiplier=-1).then_inc(pool_consts, 1)

            def split(half, slot, k):
                pool.wait_ge(w_landed[slot], 16 * half + 16)
                pool.wait_ge(unit_done, 2 * half + slot + 1)
                pool.sem_inc(split_turn, 1)
                steps(nc.gpsimd.tensor_scalar(w_hi[:, slot, 0:k], w_raw[:, slot, 0:k], 1.0, 1.0, ALU.mult, ALU.mult))
                steps.wait()
                nc.gpsimd.tensor_tensor(w_lo[:, slot, 0:k], w_raw[:, slot, 0:k], w_hi[:, slot, 0:k].bitcast(F32),
                                        ALU.subtract).then_inc(w_split, 1)

            def split_units(first_half, halves, k):
                if halves == 1:
                    split(first_half, 0, k)
                    split(first_half, 1, k)
                    return
                with pool.Fori(0, halves) as i:
                    steps.enter(i, 2)
                    split(first_half + i, 0, k)
                    split(first_half + i, 1, k)
                    steps.leave(halves)

            def scale_y(l, si):
                for j in range(KD):
                    if j == 0:
                        pool.wait_ge(rstd_ready, l * 4 + si + 1)
                    nc.gpsimd.tensor_tensor(yT[:, j], yT[:, j], rstd[:], ALU.mult).then_inc(y_scaled, 1)

            pool.sem_inc(w_split, 2)
            pool.sem_inc(wf_split, 1)
            split_units(0, 1, 8)
            with pool.Fori(0, LAYERS) as l:
                steps.enter(l, 1 + U_LAYER)
                pool.wait_ge(wf_landed, 16 * l + 16)
                pool.wait_ge(wf_done, l + 1)
                pool.sem_inc(split_turn, 1)
                steps(nc.gpsimd.tensor_scalar(wf_hi, wf_raw[:], 1.0, 1.0, ALU.mult, ALU.mult))
                steps.wait()
                nc.gpsimd.tensor_tensor(wf_lo, wf_raw[:], wf_hi.bitcast(F32), ALU.subtract).then_inc(wf_split, 1)
                half = l * (U_LAYER // 2)
                split_units(half + 1, U_GU0 // 2, 8)
                scale_y(l, 1)
                split_units(half + 1 + U_GU0 // 2, (U_D2 - U_GU0) // 2 - 1, 8)
                split_units(half + U_D2 // 2, KD // 2, FF1_CHUNKS[2][1])
                split_units(half + U_LAYER // 2, 1, 8)
                scale_y(l, 3)
                steps.leave(LAYERS)
            split_units(U2 // 2 + 1, (U_LAST - U2) // 2 - 1, 8)

        @block.tensor
        def _(pe):
            pe.sem_inc(unit_done, 2)
            pe.sem_inc(wf_done, 1)

            def products(bank, hi, lo, w_hi_, w_lo_, k_tiles, done, before=None, after=None):
                ops = []
                for k in range(k_tiles):
                    for i, (w, r) in enumerate(((w_hi_, hi), (w_hi_, lo), (w_lo_, hi))):
                        def issue(k=k, i=i, w=w, r=r):
                            if i == 0 and before is not None:
                                before(k)
                            mm = pe.matmul(bank[:], w[:, k], r[:, k], start=(k == 0 and i == 0),
                                           stop=(k == k_tiles - 1 and i == 2))
                            if k == k_tiles - 1 and i == 2:
                                mm.then_inc(done, 1)
                            if i == 2 and after is not None:
                                after(k)
                        ops.append(issue)
                return ops

            def unit(half, slot, hi, lo, k_tiles=8, ready=None, base=0, fresh=False, squares=None):
                def before(k):
                    if k == 0:
                        pe.wait_ge(w_split, 2 * half + slot + 3)
                        if not fresh:
                            pe.wait_ge(evacuated[slot], half)
                    if ready is not None:
                        pe.wait_ge(ready, base + k + 1)

                def after(k):
                    pe.wait_ge(square_ready, squares + k + 1)
                    pe.matmul(aux[:], ones[:, 0:P], square[k % 2], start=(k == 0),
                              stop=(k == KD - 1)).then_inc(square_summed if k < KD - 1 else aux_done, 1)
                return products(acc[slot], hi, lo, w_hi[:, slot], w_lo[:, slot], k_tiles, unit_done, before,
                                None if squares is None else after)

            def early_output(half, ready, base):
                both = [unit(half, i, mid_hi[:, 0], mid_lo[:, 0], ready=ready, base=base) for i in range(2)]
                return sum((ops[:3 * KD - 3] for ops in both), []), sum((ops[3 * KD - 3:] for ops in both), [])

            def share(work, k, n):
                run(work[k * len(work) // n:(k + 1) * len(work) // n])

            def run(ops):
                for op in ops:
                    op()

            def sum_squares(added, a):
                pe.wait_ge(square_added, added + KD)
                pe.wait_ge(aux_free, a)
                pe.matmul(aux[:], ones[:, 0:P], square_sum, start=True, stop=True).then_inc(aux_done, 1)

            pe.wait_ge(pool_consts, 1)
            pe.wait_ge(consts_in, 16 * N_CONSTS)
            pe.wait_ge(vec_consts, 3)
            pe.transpose(sc[0][:, 0:G_ROWS], grow[0:G_ROWS, :], ident[0:G_ROWS, 0:G_ROWS]).then_inc(pre_pe, 1)
            pe.matmul(sc[1][:, 0:1], inv_row[0:1, :], ones[0:1, 0:1], start=True, stop=True).then_inc(pre_pe, 1)
            for j in range(KD):
                if j == 0:
                    pe.wait_ge(x_in, 16 * NB)
                if j >= 2:
                    pe.wait_ge(x_ready, j - 1)
                for t in range(NB):
                    mm = pe.transpose(tp[j % 2][:, t * P:t * P + P], x_tok[:, t, j * P:j * P + P], ident[:])
                mm.then_inc(pre_pe, 1)

            with pe.Fori(0, LAYERS) as l:
                A = l * A_LAYER
                half0 = l * (U_LAYER // 2)

                def score(p, s):
                    t, m = s // 2, s % 2
                    bank, n = sc[s % 2], (t + 1) * P
                    if s == 0:
                        if p == 0:
                            pe.wait_ge(f_taken, l + 1)
                        if p < NDIFF:
                            pe.wait_ge(qk_ready, l * 2 * NDIFF + 2 * p + 2)
                        else:
                            for u in (3 * p, 3 * p + 1):
                                pe.wait_ge(evacuated[u % 2], half0 + u // 2 + 1)
                            if p == NDIFF:
                                pe.wait_ge(decay_ready, l + 1)
                    if p * 8 + s >= 2:
                        pe.wait_ge(exp_done, l * 64 + p * 8 + s - 1)
                    r = slice(HD * m, HD * m + HD)
                    pe.matmul(bank[:, 0:n], qT[p % 2][r, t * P:t * P + P], kT[p % 2][r, 0:n], start=True, stop=False)
                    if p >= NDIFF:
                        h = 2 * (p - NDIFF) + m
                        for i in range(2):
                            pe.matmul(bank[:, 0:n], sel_r[96:128, h, :], decay_r[96:128, i, 0:n], start=False, stop=False)
                    pe.matmul(bank[:, t * P:n], ident_r[:], mask_r[:], start=False, stop=True).then_inc(score_done, 1)

                def transpose_p(p, i):
                    ti = T_BASE[p] + i
                    t = i if p < NDIFF else i // 2
                    src = prob[(2 * i) % 4] if p < NDIFF else prob[i % 4]
                    pe.wait_ge(p_ready, l * T_BASE[PAIRS] + ti + 1)
                    if ti >= 2:
                        pe.wait_ge(t_taken, l * T_BASE[PAIRS] + ti - 1)
                    for j in range(t + 1):
                        mm = pe.transpose(tp[ti % 2][:, j * P:j * P + P], src[:, j * P:j * P + P], ident[:])
                    mm.then_inc(t_done, 1)

                def pv(p, i):
                    ti = T_BASE[p] + i
                    t = i if p < NDIFF else i // 2
                    r = slice(0, P) if p < NDIFF else slice(HD * (i % 2), HD * (i % 2) + HD)
                    if i == 0:
                        pe.wait_ge(aux_free, A + AUX[("v", p)] + 1)
                        if p >= 1:
                            pe.wait_ge(po_taken, l * PAIRS + p)
                    pe.wait_ge(t_taken, l * T_BASE[PAIRS] + ti + 1)
                    for j in range(t + 1):
                        mm = pe.matmul(po[r, t * P:t * P + P], vtok[:, j, r], probT[ti % 2][:, j * P:j * P + P],
                                       start=(j == 0), stop=(j == t))
                    mm.then_inc(pv_done, 1)

                def use_aux(name):
                    if AUX[name]:
                        pe.wait_ge(aux_free, A + AUX[name])

                for p in range(-1, PAIRS):
                    work = []
                    if p + 1 < PAIRS:
                        for i in range(3):
                            u = 3 * (p + 1) + i
                            first = p == -1 and i == 0
                            work += unit(half0 + u // 2, u % 2, h_hi, h_lo, 8, ready=h_ready if first else None,
                                         base=l * 16, fresh=(u < 2), squares=l * 32 if first else None)
                    else:
                        work, rest = early_output(half0 + U_OUT // 2, o_ready, l * PAIRS)
                    for k in range(SLOTS):
                        if p >= 0 and k < 8:
                            score(p, k)
                        share(work, k, SLOTS)
                        if p >= 0 and k == 1:
                            use_aux(("v", p))
                            pe.wait_ge(evacuated[(3 * p + 2) % 2], half0 + (3 * p + 2) // 2 + 1)
                            for j in range(NB):
                                mm = pe.transpose(aux[:, j * P:j * P + P], vraw[:, j * P:j * P + P], ident[:])
                            mm.then_inc(aux_done, 1)
                        if k == 4 and 0 <= p - 1 < NDIFF:
                            use_aux(("o_norm", p - 1))
                            pe.wait_ge(o_square, l * NDIFF + p)
                            pe.matmul(aux[:], ones[:, 0:P], osq, start=True, stop=True).then_inc(aux_done, 1)
                        for slot, name, i in ((6, "rot_q", 0), (9, "rot_k", 1)):
                            if k == slot and p + 1 < NDIFF:
                                u = 3 * (p + 1) + i
                                use_aux((name, p + 1))
                                pe.wait_ge(evacuated[u % 2], half0 + u // 2 + 1)
                                pe.matmul(aux[:], rotT[:], raw, start=True, stop=True).then_inc(aux_done, 1)
                        if p >= 0 and p < NDIFF:
                            if k >= 3 and k % 2 == 1 and (k - 3) // 2 < 4:
                                transpose_p(p, (k - 3) // 2)
                            if k >= 4 and k % 2 == 0 and (k - 4) // 2 < 4:
                                pv(p, (k - 4) // 2)
                        elif p >= NDIFF:
                            if 2 <= k < 10:
                                transpose_p(p, k - 2)
                            if 3 <= k < 11:
                                pv(p, k - 3)
                    if p == -1:
                        pe.wait_ge(wf_split, l + 2)
                        run(products(sc[0], h_hi, h_lo, wf_hi, wf_lo, 8, wf_done))

                run(rest)
                with pe.Fori(1, KD // 2) as m:
                    for i in range(2):
                        run(unit(half0 + U_OUT // 2 + m, i, mid_hi[:, 0], mid_lo[:, 0]))
                sum_squares(added_base(2 * l), A + AUX["norm_att_post"])

                def gate_up(half, **kw):
                    run(unit(half, 0, h_hi, h_lo, **kw))
                    run(unit(half, 1, h_hi, h_lo))

                for kind, c, u in FFN_ORDER:
                    first, n = FF1_CHUNKS[c]
                    half = half0 + u // 2
                    if kind == "gu":
                        if c == 0:
                            gate_up(half, ready=h_ready, base=l * 16 + 8, squares=l * 32 + 16)
                            with pe.Fori(1, n) as j:
                                gate_up(half + j)
                        else:
                            with pe.Fori(0, n) as j:
                                gate_up(half + j)
                    else:
                        with pe.Fori(0, KD // 2) as m:
                            pe.wait_ge(mid_ready, l * FF1_TILES + first + n)
                            for i in range(2):
                                run(unit(half + m, i, mid_hi[:, c % 2], mid_lo[:, c % 2], n))
                sum_squares(added_base(2 * l + 1), A + AUX["norm_ffn_post"])

            def sb_pair(pp, par, current=True, following=True, work=()):
                p = 2 * pp + par
                aux_n = A_SB + 3 + 3 * p
                if following:
                    work = []
                    for i in range(3):
                        u = 3 * (par + 1) + i
                        first = par == -1 and i == 0
                        h_base, squares, _ = block2_norm(0)
                        work += unit(U_SB // 2 + 3 * pp + u // 2, u % 2, h_hi, h_lo, 8, ready=h_ready if first else None,
                                     base=h_base, squares=squares if first else None)

                def scores(m):
                    if m == 0:
                        pe.wait_ge(sbqk_ready, 2 * p + 2)
                    pe.wait_ge(w_ready, 2 * p + m + 1)
                    r = slice(HD * m, HD * m + HD)
                    for bank, blocks, _, _ in Z_PARTS:
                        for b in blocks:
                            at = Z_BANK[b][1]
                            mm = pe.matmul(z[bank][:, at:at + Z_N[b]], skT[par % 2][r, b * P:b * P + P],
                                           sqT[par % 2][r, b * P:S], start=(b < 3), stop=True, skip_group_check=True)
                        mm.then_inc(z_done, 1)

                def log_weights(m):
                    for i, (bank, blocks, _, _) in enumerate(Z_PARTS):
                        pe.wait_ge(stay_ready, 6 * p + 3 * m + i + 1)
                        for b in blocks:
                            at = Z_BANK[b][1]
                            pe.matmul(z[bank][:, at:at + P], ident_r[:], mask_sb_r[:], start=False, stop=False,
                                      skip_group_check=True)
                            for c in range(b, NB):
                                lhs = neg_incl_r if c == b else neg_ones_r
                                for part_ in (stay_hi, stay_lo):
                                    mm = pe.matmul(z[bank][:, at + (c - b) * P:at + Z_N[b]], lhs[:],
                                                   part_[:, Z_AT[c]:Z_AT[c] + Z_N[c]], start=False,
                                                   stop=(c == NB - 1), skip_group_check=True)
                        mm.then_inc(logw_done, 1)

                def sb_pv(m, p_, first):
                    r = slice(HD * m, HD * m + HD)
                    pe.wait_ge(w_ready, 2 * p_ + m + 2)
                    if m == 0:
                        pe.wait_ge(aux_free, aux_n + 1)
                        pe.wait_ge(sbo_taken, p_ + 1)
                    for b in range(NB):
                        mm = pe.matmul(po[r, b * P:S], vtok[:, b, r], sb_w[:, Z_AT[b]:Z_AT[b] + Z_N[b]],
                                       start=(b == 0), stop=(b == NB - 1), skip_group_check=True)
                    mm.then_inc(sbpv_done, 1)

                for k in range(SLOTS):
                    if current:
                        if k in (0, 6):
                            scores(k // 6)
                        if k == 1 and prev_pv:
                            prev_pv[0](pp, par)
                        if k == 7:
                            sb_pv(0, p, False)
                        if k in (5, 11):
                            log_weights(k // 6)
                    share(work, k, SLOTS)
                    if current and k == 2:
                        pe.wait_ge(aux_free, aux_n)
                        u = 3 * par + 2
                        pe.wait_ge(evacuated[u % 2], U_SB // 2 + 3 * pp + u // 2 + 1)
                        for j in range(NB):
                            mm = pe.transpose(aux[:, j * P:j * P + P], vraw[:, j * P:j * P + P], ident[:])
                        mm.then_inc(aux_done, 1)
                    for i, at in ((0, 6), (1, 10)):
                        if following and k == at:
                            pe.wait_ge(aux_free, aux_n + 1 + i)
                            pe.wait_ge(raw_square, 2 * p + 2 + i + 1)
                            pe.matmul(aux[:], head_ones[:], sb_sq, start=True, stop=True).then_inc(aux_done, 1)

            def last_pv(p_):
                pe.wait_ge(w_ready, 2 * p_ + 3)
                r = slice(HD, 2 * HD)
                for b in range(NB):
                    mm = pe.matmul(po[r, b * P:S], vtok[:, b, r], sb_w[:, Z_AT[b]:Z_AT[b] + Z_N[b]],
                                   start=(b == 0), stop=(b == NB - 1), skip_group_check=True)
                mm.then_inc(sbpv_done, 1)

            z = [sc[0], sc[1], tp[0]]
            pe.sem_inc(sbpv_done, 1)
            prev_pv = []
            sb_pair(0, -1, current=False)
            sb_pair(0, 0)
            prev_pv = [lambda pp, par: last_pv(2 * pp + par - 1)]
            sb_pair(0, 1)
            with pe.Fori(1, PAIRS // 2 - 1) as pp:
                sb_pair(pp, 0)
                sb_pair(pp, 1)
            sb_pair(PAIRS // 2 - 1, 0)
            work, rest = early_output(U_SBO // 2, sbo_ready, 0)
            sb_pair(PAIRS // 2 - 1, 1, following=False, work=work)
            last_pv(PAIRS - 1)

            def square_matrix(u, rest):
                run(rest)
                with pe.Fori(1, KD // 2) as m:
                    for i in range(2):
                        run(unit(u // 2 + m, i, mid_hi[:, 0], mid_lo[:, 0]))

            def mlp_products(i_mlp, u0, norm, a_n):
                for kind, c, u in MLP_UNITS:
                    half = (u0 + u) // 2
                    if kind == "up":
                        first = 0
                        if c == 0:
                            h_base, _, added = block2_norm(norm)
                            run(unit(half, 0, h_hi, h_lo, ready=h_ready, base=h_base))
                            run(unit(half, 1, h_hi, h_lo))
                            sum_squares(added, a_n)
                            first = 1
                        with pe.Fori(first, KD // 2) as m:
                            for i in range(2):
                                run(unit(half + m, i, h_hi, h_lo))
                    else:
                        with pe.Fori(0, KD // 2) as m:
                            pe.wait_ge(mid_ready, MID1 + i_mlp * (FF2 // P) + 8 * c + 8)
                            for i in range(2):
                                run(unit(half + m, i, mid_hi[:, c % 2], mid_lo[:, c % 2]))

            square_matrix(U_SBO, rest)
            mlp_products(0, U_M1, 1, A_M1)

            def hg_head(pp, par, current=True, following=True, previous=True, first=False, work=()):
                i = 2 * pp + par
                half = U_HG // 2 + 2 * i
                if following:
                    work = []
                    for n in range(4):
                        work += unit(half + 2 + n // 2, n % 2, h_hi, h_lo, 8,
                                     ready=h_ready if par == -1 and n == 0 else None, base=block2_norm(2)[0])
                for k in range(HG_SLOTS):
                    if current and k == 0:
                        pe.wait_ge(hg_k, i + 1)
                        pe.wait_ge(hg_q, i + 1)
                        if not first:
                            pe.wait_ge(hg_pred, 8 * i)
                        for b in range(NB):
                            c = slice(b * P, b * P + P)
                            mm = pe.matmul(sc[1][:, c], hk[par % 2][:, c], hq[par % 2][:, c], start=True, stop=True)
                        mm.then_inc(hg_mm, 1)
                    if current and 3 <= k < 3 + len(HALVES):
                        lv = k - 3
                        h = HALVES[lv]
                        x = hx[lv % 3]
                        pe.wait_ge(hg_mul, 7 * i + lv + 1)
                        pe.wait_ge(hg_pred, 8 * i + lv)
                        for b in range(NB):
                            right = x[:, b * P:b * P + P].rearrange("p (n e j) -> p n e j", e=2, j=h)[:, :, 1]
                            mm = pe.matmul(sc[lv % 2][:, b * HD:b * HD + HD], x[:, b * P:b * P + P], right,
                                           start=True, stop=True)
                        mm.then_inc(hg_mm, 1)
                    if current and k == 12:
                        pe.wait_ge(hg_offmul, i + 1)
                        if not first:
                            pe.wait_ge(hg_offtaken, i)
                        pe.matmul(tp[0][:, 0:P], hx128[:, 0:P], hx128[:, P:2 * P], start=True, stop=True)
                        pe.matmul(tp[0][:, P:2 * P], hx128[:, 2 * P:3 * P], hx128[:, 3 * P:S], start=True, stop=True)
                        pe.matmul(tp[0][:, 2 * P:S], hx256[:, 0:P], hx256[:, 2 * P:S], start=True, stop=True)
                        pe.matmul(tp[1][:, 0:2 * P], hx256[:, P:2 * P], hx256[:, 2 * P:S], start=True,
                                  stop=True).then_inc(hg_offmm, 1)
                    if current and k == 14:
                        pe.wait_ge(aux_free, a_hgv(i, first) + 1)
                        pe.wait_ge(hg_pred, 8 * i + 8)
                        pe.wait_ge(hg_offtaken, i + 1)
                        if not first:
                            pe.wait_ge(hg_otaken, i)
                        for b in range(NB):
                            pe.matmul(po[:, b * P:b * P + P], hvtok[:, b], hdiag[:, b * P:b * P + P], start=(b == 0),
                                      stop=False, skip_group_check=True)
                        for b, c, n, at in ((0, 1, P, 0), (2, 3, P, P), (0, 2, 2 * P, 2 * P), (1, 2, 2 * P, S)):
                            mm = pe.matmul(po[:, c * P:c * P + n], hvtok[:, b], hoff[:, at:at + n], start=False,
                                           stop=True, skip_group_check=True)
                        mm.then_inc(hg_pv, 1)
                    share(work, k, HG_SLOTS)
                    if par == -1 and k == 3:
                        sum_squares(block2_norm(2)[2], A_HG)
                    if current and k == 1:
                        pe.wait_ge(evacuated[0], half + 2)
                        pe.wait_ge(aux_free, a_hgv(i, first))
                        for j in range(NB):
                            mm = pe.transpose(aux[:, j * P:j * P + P], hvraw[:, j * P:j * P + P], ident[:])
                        mm.then_inc(aux_done, 1)
                    if current and previous and k == 2:
                        hg_norm(i - 1)

            def hg_norm(i, last=False):
                pe.wait_ge(hg_osq, i + 1)
                pe.wait_ge(aux_free, a_hgv(i + 1) + (0 if last else 1))
                pe.matmul(aux[:], ones[:, 0:P], hosq, start=True, stop=True).then_inc(aux_done, 1)

            hg_head(0, -1, current=False)
            hg_head(0, 0, previous=False, first=True)
            hg_head(0, 1)
            with pe.Fori(1, KD // 2 - 1) as pp:
                hg_head(pp, 0)
                hg_head(pp, 1)
            hg_head(KD // 2 - 1, 0)
            work, rest = early_output(U_HGO // 2, hg_oready, 0)
            hg_head(KD // 2 - 1, 1, following=False, work=work)
            hg_norm(KD - 1, last=True)
            square_matrix(U_HGO, rest)
            mlp_products(1, U_M2, 3, A_M2)
            for i in range(2):
                pe.wait_ge(evacuated[i], U_LAST // 2)
            for t in range(NB):
                for g in range(2):
                    i = 2 * t + g
                    if i >= 2:
                        pe.wait_ge(out_ready, t)
                    for j in range(4):
                        mm = pe.transpose(tp[g][:, j * P:j * P + P], xT[:, 4 * g + j, t * P:t * P + P], ident[:])
                    mm.then_inc(pre_pe, 1)

        @block.vector
        def _(v):
            steps = Steps(v, vec_step)
            TT, TS, STT, COPY = v.tensor_tensor, v.tensor_scalar, v.scalar_tensor_tensor, v.tensor_copy

            v.memset(lconst[:], 0.0).then_inc(vec_consts, 1)
            v.memset(ones[:], 1.0)
            v.memset(eps_col[:], EPS).then_inc(vec_consts, 1)
            steps(v.memset(inv_row[0:1, :], 0.0))
            steps.wait()
            by_head = inv_row[0:1, :].rearrange("p (b q) -> p b q", b=2)[:, :, 0:2 * ROT_HALF].rearrange(
                "p b (e d) -> p b e d", e=2)
            inv_freq = 1.0 / (np.float32(THETA) ** (np.arange(0, 2 * ROT_HALF, 2, dtype=np.float32) / np.float32(2 * ROT_HALF)))
            for d in range(ROT_HALF):
                last = v.memset(by_head[:, :, :, d], float(inv_freq[d]))
            last.then_inc(vec_consts, 1)
            v.wait_ge(pre_pe, 1)
            steps(COPY(gains[:], sc[0][:, 0:G_ROWS]))
            v.wait_ge(pre_pe, 2)
            steps(COPY(inv_col, sc[1][:, 0:1]))
            for j in range(KD):
                v.wait_ge(pre_pe, 3 + j)
                COPY(xT[:, j], tp[j % 2][:]).then_inc(x_ready, 1)
            def add_square(n, added, j, i):
                v.wait_ge(square_ready, n + j + 1)
                v.wait_ge(square_added, added + j)
                TT(square_sum, square_sum, square[i], ALU.add).then_inc(square_added, 1)

            def low_part(hi_n, j, gain):
                v.wait_ge(h_hi_ready, hi_n + j + 1)
                STT(h_lo[:, ds(j, 1)], xT[:, ds(j, 1)], gain, h_hi[:, ds(j, 1)].bitcast(F32), ALU.mult,
                    ALU.subtract).then_inc(h_ready, 1)

            v.sem_inc(square_added, 2)
            for j in range(KD):
                low_part(0, j, gains[:, G_ATT_PRE + j:G_ATT_PRE + j + 1])
            v.wait_ge(pool_consts, 8)
            COPY(ident_r[:], ident[:])
            COPY(mask_r[:], mask_f)
            COPY(sel_r[:], sel_f)
            COPY(neg_incl_r[:], neg_incl_f)
            COPY(mask_sb_r[:], mask_sb_f)
            TS(neg_ones_r[:], ones[:, 0:P], -1.0, None, ALU.mult)
            steps(v.memset(head_ones[:], 0.0))
            steps.wait()
            for m in range(2):
                v.memset(head_ones[HD * m:HD * m + HD, HD * m:HD * m + HD], 1.0)
            v.wait_ge(pool_consts, 8 + len(HALVES))
            for b in range(NB):
                COPY(level_mask[:, :, b * HD:b * HD + HD], level_f)
                COPY(same_mask[:, b * P:b * P + P], ident[:])
            TS(sb_gain[:, 0:1], gains[:, G_SBQ:G_SBQ + 1], HD ** -0.5, None, ALU.mult)
            COPY(sb_gain[:, 1:2], gains[:, G_SBK:G_SBK + 1])
            v.wait_ge(consts_in, 16 * N_CONSTS)
            steps(TT(lam_p, lam_in[:, 0:4:2], lam_in[:, 1:4:2], ALU.mult))
            steps.wait()
            v.reduce_sum(lam_s.rearrange("p (v l) -> p v l", v=2), lam_p, AX_X).then_inc(vec_consts, 1)
            big = 1.5 * 2.0 ** 23
            c1, c2 = 6.28125, 0.0019350051879882812
            c3 = 2 * math.pi - c1 - c2
            pi_in = float(np.nextafter(np.float32(math.pi), np.float32(0)))
            steps(TS(ang, pos_i, inv_col, None, ALU.mult))
            steps.wait()
            for shift, offset, dst in ((0.0, 0.0, 0), (0.25, math.pi / 2, 1)):
                if dst:
                    v.wait_ge(act_consts, 1)
                steps(TS(turn, ang, 1 / (2 * math.pi), shift, ALU.mult, ALU.add))
                steps.wait()
                steps(TS(turn, turn, big, None, ALU.add))
                steps.wait()
                steps(TS(turn, turn, -big, None, ALU.add))
                steps.wait()
                steps(STT(red, turn, -c1, ang, ALU.mult, ALU.add))
                steps.wait()
                steps(STT(red, turn, -c2, red, ALU.mult, ALU.add))
                steps.wait()
                steps(STT(red, turn, -c3, red, ALU.mult, ALU.add))
                steps.wait()
                steps(TS(red, red, offset, pi_in, ALU.add, ALU.min))
                steps.wait()
                TS(red, red, -pi_in, None, ALU.max).then_inc(vec_consts, 1)
            v.wait_ge(act_consts, 3)
            for l in range(LAYERS):
                steps(TT(lconst[:, l, 0:1], lam_e[:, LAYERS + l:LAYERS + l + 1], lam_e[:, l:l + 1], ALU.subtract))
                steps(TS(lconst[:, l, 1:2], gains[:, G_DIFF + l:G_DIFF + l + 1], 1.0 - LAM_INIT[l], None, ALU.mult))
            steps.wait()
            for l in range(LAYERS):
                steps(TS(lconst[:, l, 0:1], lconst[:, l, 0:1], -LAM_INIT[l], None, ALU.add))
            steps.wait()

            def take(half, slot):
                v.wait_ge(unit_done, 2 * half + slot + 3)

            with v.Fori(0, LAYERS) as l:
                steps.enter(l, VEC_STEPS_LAYER)
                A = l * A_LAYER
                half0 = l * (U_LAYER // 2)
                v.wait_ge(h_ready, l * 16 + KD)
                COPY(layer_gain[:, 0:3], gains[:, G_ATT_POST:G_ATT_POST + 6 * KD].rearrange(
                    "p (g l j) -> p g l j", g=3, l=LAYERS)[:, :, ds(l, 1)])
                COPY(layer_gain[:, 3], gains[:, ds(l * KD + KD, KD)])
                COPY(lcur[:], lconst[:, ds(l, 1)]).then_inc(layer_const, 1)
                v.wait_ge(layer_const, l + 1)
                def probabilities(p, i):
                    t = i if p < NDIFF else i // 2
                    n = (t + 1) * P
                    if p < NDIFF:
                        s, a = 2 * i, (2 * i) % 4
                        v.wait_ge(exp_done, l * 64 + p * 8 + s + 2)
                        steps(v.reciprocal(stat[:, 8 + a:10 + a], stat[:, 4 + a:6 + a]))
                        steps.wait()
                        steps(TT(stat[:, 12:13], stat[:, 9 + a:10 + a], lcur[:, 0:1], ALU.mult))
                        steps(TS(prob[a][:, 0:n], prob[a][:, 0:n], stat[:, 8 + a:9 + a], None, ALU.mult))
                        steps.wait()
                        STT(prob[a][:, 0:n], prob[a + 1][:, 0:n], stat[:, 12:13], prob[a][:, 0:n],
                            ALU.mult, ALU.add).then_inc(p_ready, 1)
                    else:
                        a = i % 4
                        v.wait_ge(exp_done, l * 64 + p * 8 + i + 1)
                        steps(v.reciprocal(stat[:, 8 + a:9 + a], stat[:, 4 + a:5 + a]))
                        steps.wait()
                        TS(prob[a][:, 0:n], prob[a][:, 0:n], stat[:, 8 + a:9 + a], None, ALU.mult).then_inc(p_ready, 1)

                def take_qk(p, i):
                    u = 3 * p + i
                    take(half0 + u // 2, u % 2)
                    dst = raw if p < NDIFF else (qT, kT)[i][p % 2]
                    STT(dst, acc[u % 2][:], (HD ** -0.5, 1.0)[i], rstd[:], ALU.mult, ALU.mult).then_inc(evacuated[u % 2], 1)

                def rotate(p, i):
                    a = AUX[(("rot_q", "rot_k")[i], p)]
                    v.wait_ge(aux_done, A + a + 1)
                    TT(rsin, aux[:], sinT[:], ALU.mult).then_inc(aux_free, 1)
                    steps(TT(rcos, raw, cosT[:], ALU.mult))
                    steps.wait()
                    v.wait_ge(aux_free, A + a + 1)
                    TT((qT, kT)[i][p % 2], rcos, rsin, ALU.add).then_inc(qk_ready, 1)

                def low_output(p):
                    v.wait_ge(o_hi_ready, l * PAIRS + p + 1)
                    src = onrm if p < NDIFF else orow
                    TT(mid_lo[:, 0, p], src, mid_hi[:, 0, p].bitcast(F32), ALU.subtract).then_inc(o_ready, 1)

                for p in range(-1, PAIRS):
                    for k in range(SLOTS):
                        if k == 0 and p >= 0:
                            u = 3 * p + 2
                            take(half0 + u // 2, u % 2)
                            TT(vraw, acc[u % 2][:], rstd[:], ALU.mult).then_inc(evacuated[u % 2], 1)
                        if p >= 0 and k < 8:
                            n = (k // 2 + 1) * P
                            v.wait_ge(score_done, l * 64 + p * 8 + k + 1)
                            v.tensor_reduce(stat[:, k % 4:k % 4 + 1], sc[k % 2][:, 0:n], AX_X, ALU.max,
                                            negate=True).then_inc(max_done, 1)
                        if p >= 0 and p < NDIFF and k >= 2 and k % 2 == 0 and k <= 8:
                            probabilities(p, (k - 2) // 2)
                        if p >= NDIFF and 1 <= k <= 8:
                            probabilities(p, k - 1)
                        if k == 4 and p + 1 < PAIRS:
                            if p == -1:
                                v.wait_ge(rstd_ready, l * 4 + 1)
                            take_qk(p + 1, 0)
                        if k == 8 and p + 1 < PAIRS:
                            take_qk(p + 1, 1)
                        if p + 1 < NDIFF and k == 7:
                            rotate(p + 1, 0)
                        if p + 1 < NDIFF and k == 10:
                            rotate(p + 1, 1)
                        if k == 2 and p - 1 >= NDIFF:
                            low_output(p - 1)
                        if k == 6 and 0 <= p - 1 < NDIFF:
                            v.wait_ge(o_rstd, l * NDIFF + p)
                            STT(onrm, orow, lcur[:, 1:2], ologs, ALU.mult, ALU.mult).then_inc(o_normed, 1)
                        if k == 8 and 0 <= p - 1 < NDIFF:
                            low_output(p - 1)
                        if p == 0 and k == 9:
                            v.wait_ge(f_log, l + 1)
                            f = slice(96, P)
                            steps(STT(raw_f[f], raw_f[f], 0.0, ologs_f[f], ALU.min, ALU.subtract))
                            steps.wait()
                            steps(v.tensor_tensor_scan(negc[f], ones[f], raw_f[f], 0.0, ALU.mult, ALU.subtract))
                            steps.wait()
                            steps(COPY(decay_r[f, 0], negc[f]))
                            steps.wait()
                            TT(decay_r[f, 1], negc[f], decay_r[f, 0].bitcast(F32), ALU.subtract).then_inc(decay_ready, 1)
                        if k == 11 and p >= 0:
                            v.wait_ge(pv_done, l * T_BASE[PAIRS] + T_BASE[p + 1])
                            COPY(orow, po[:]).then_inc(po_taken, 1)
                    if p == -1:
                        v.wait_ge(wf_done, l + 2)
                        TT(raw_f[96:P], sc[0][96:P], rstd[96:P], ALU.mult).then_inc(f_taken, 1)
                        v.wait_ge(f_taken, l + 1)
                        TS(raw_f[96:P], raw_f[96:P], lcur[96:P, 2:3], None, ALU.add).then_inc(f_ready, 1)
                low_output(PAIRS - 1)

                def update_x(g, x_n, scaled):
                    for j in range(KD + 1):
                        if j < KD:
                            v.wait_ge(y_scaled, scaled + j + 1)
                            STT(xT[:, j], yT[:, j], layer_gain[:, g, j:j + 1], xT[:, j], ALU.mult,
                                ALU.add).then_inc(x_ready, 1)
                        if j >= 1:
                            v.wait_ge(x_ready, x_n + j)
                            low_part(x_n, j - 1, layer_gain[:, g + 1, j - 1:j])

                def take_y(half, slot, j, kind, n):
                    take(half, slot)
                    dst = yT[:, ds(j, 1)]
                    if kind == "first":
                        COPY(dst, acc[slot][:]).then_inc(evacuated[slot], 1)
                    else:
                        TT(dst, dst, acc[slot][:], ALU.add).then_inc(evacuated[slot], 1)

                steps(v.memset(square_sum, 0.0))
                with v.Fori(0, KD // 2) as m:
                    steps.wait()
                    for i in range(2):
                        take_y(half0 + U_OUT // 2 + m, i, 2 * m + i, "first", 0)
                        add_square(l * 32 + 8, added_base(2 * l), 2 * m + i, i)
                update_x(0, l * 16 + 8, l * 16)
                for kind, c, u in FFN_ORDER:
                    first, n = FF1_CHUNKS[c]
                    half = half0 + u // 2
                    if kind == "gu":
                        with v.Fori(0, n) as j:
                            g = l * FF1_TILES + first + j
                            v.wait_ge(rstd_ready, l * 4 + 3)
                            take(half + j, 0)
                            TT(gate, acc[0][:], rstd[:], ALU.mult).then_inc(evacuated[0], 1)
                            v.wait_ge(gate_log, g + 1)
                            STT(gate_t, gate, 0.0, gate_t2, ALU.min, ALU.subtract).then_inc(gate_ls, 1)
                            take(half + j, 1)
                            TT(up, acc[1][:], rstd[:], ALU.mult).then_inc(evacuated[1], 1)
                            v.wait_ge(evacuated[1], half + j + 1)
                            TT(up, gate, up, ALU.mult).then_inc(gu_done, 1)
                            v.wait_ge(gate_sig, g + 1)
                            v.wait_ge(gu_done, g + 1)
                            TT(hid, up, gate_t2, ALU.mult).then_inc(hid_ready, 1)
                            v.wait_ge(mid_hi_ready, g + 1)
                            TT(mid_lo[:, c % 2, ds(j, 1)], hid, mid_hi[:, c % 2, ds(j, 1)].bitcast(F32),
                               ALU.subtract).then_inc(mid_ready, 1)
                    else:
                        if c == 2:
                            steps(v.memset(square_sum, 0.0))
                        with v.Fori(0, KD // 2) as m:
                            if c == 2:
                                steps.wait()
                            for i in range(2):
                                take_y(half + m, i, 2 * m + i, "first" if c == 0 else "more", 0)
                                if c == 2:
                                    add_square(l * 32 + 24, added_base(2 * l + 1), 2 * m + i, i)
                update_x(2, l * 16 + 16, l * 16 + 8)
                steps.leave(LAYERS)

            def sb_pair(pp, par, current=True, following=True, previous=True):
                p = 2 * pp + par
                half = U_SB // 2 + 3 * pp
                aux_n = A_SB + 3 + 3 * p

                def stay(m):
                    for i, (bank, blocks, at, n) in enumerate(Z_PARTS):
                        c = slice(at, at + n)
                        v.wait_ge(z_log, 6 * p + 3 * m + i + 1)
                        steps(STT(sb_stay[:, c], z[bank][:, 0:n], 0.0, sb_log[:, c], ALU.max, ALU.add))
                        steps.wait()
                        for b in blocks:
                            d = sb_stay[:, Z_AT[b]:Z_AT[b] + P]
                            steps(TT(d, d, before01[:], ALU.mult))
                        steps.wait()
                        steps(COPY(stay_hi[:, c], sb_stay[:, c]))
                        steps.wait()
                        TT(stay_lo[:, c], sb_stay[:, c], stay_hi[:, c].bitcast(F32), ALU.subtract).then_inc(stay_ready, 1)

                def take_raw(i):
                    u = 3 * (par + 1) + i
                    if par >= 0 or i:
                        v.wait_ge(sbqk_ready, 2 * p + 2 + i)
                    take(half + u // 2, u % 2)
                    TT(raw, acc[u % 2][:], rstd[:], ALU.mult).then_inc(evacuated[u % 2], 1)

                def normed(i):
                    v.wait_ge(raw_rstd, 2 * p + 2 + i + 1)
                    dst = (sqT, skT)[i][(par + 1) % 2]
                    STT(dst, raw, sb_gain[:, i:i + 1], sb_logs, ALU.mult, ALU.mult).then_inc(sbqk_ready, 1)

                for k in range(SLOTS):
                    if current and k == 0:
                        u = 3 * par + 2
                        take(half + u // 2, u % 2)
                        TT(vraw, acc[u % 2][:], rstd[:], ALU.mult).then_inc(evacuated[u % 2], 1)
                        stay(0)
                    if current and k == 6:
                        stay(1)
                    if current and previous and k == 3:
                        sb_output(p - 1)
                    if following and k == 4:
                        if par == -1:
                            v.wait_ge(rstd_ready, 4 * LAYERS + 1)
                        take_raw(0)
                    if following and k == 7:
                        normed(0)
                    if following and k == 8:
                        take_raw(1)
                    if following and k == 11:
                        normed(1)

            def sb_output(p):
                v.wait_ge(sbpv_done, 2 * p + 3)
                COPY(sb_orow, po[:]).then_inc(sbo_taken, 1)
                v.wait_ge(sbo_hi, p + 1)
                TT(mid_lo[:, 0, ds(p, 1)], sb_orow, mid_hi[:, 0, ds(p, 1)].bitcast(F32), ALU.subtract).then_inc(sbo_ready, 1)

            z = [sc[0], sc[1], tp[0]]
            v.sem_inc(sbo_taken, 1)
            sb_pair(0, -1, current=False)
            sb_pair(0, 0, previous=False)
            sb_pair(0, 1)
            with v.Fori(1, PAIRS // 2 - 1) as pp:
                steps.enter(pp - 1, SB_STEPS)
                sb_pair(pp, 0)
                sb_pair(pp, 1)
                steps.leave(PAIRS // 2 - 2)
            sb_pair(PAIRS // 2 - 1, 0)
            sb_pair(PAIRS // 2 - 1, 1, following=False)
            sb_output(PAIRS - 1)

            def add_x(half, slot, j):
                take(half, slot)
                v.wait_ge(evacuated[slot], half)
                dst = xT[:, ds(j, 1)]
                TT(dst, dst, acc[slot][:], ALU.add).then_inc(evacuated[slot], 1)

            def add_matrix(u, norm=None):
                if norm is not None:
                    steps(v.memset(square_sum, 0.0))
                with v.Fori(0, KD // 2) as m:
                    if norm is not None:
                        steps.wait()
                    for i in range(2):
                        j = 2 * m + i
                        add_x(u // 2 + m, i, j)
                        if norm is not None:
                            h_base, squares, added = block2_norm(norm)
                            low_part(h_base, j, gains[:, ds(j + (G_B2 + norm * KD), 1)])
                            add_square(squares, added, j, i)

            def mlp(i_mlp, u0, i_norm):
                for kind, c, u in MLP_UNITS:
                    half = (u0 + u) // 2
                    if kind == "down":
                        add_matrix(u0 + u, norm=2 if i_mlp == 0 and c == 3 else None)
                        continue
                    with v.Fori(0, KD // 2) as m:
                        for i in range(2):
                            g = MID1 + i_mlp * (FF2 // P) + 8 * c + 2 * m + i
                            v.wait_ge(rstd_ready, 4 * LAYERS + i_norm + 1)
                            take(half + m, i)
                            TT(gate, acc[i][:], rstd[:], ALU.mult).then_inc(evacuated[i], 1)
                            v.wait_ge(evacuated[i], half + m + 1)
                            STT(hid, gate, 0.0, gate, ALU.max, ALU.mult).then_inc(hid_ready, 1)
                            v.wait_ge(mid_hi_ready, g + 1)
                            TT(mid_lo[:, c % 2, ds(2 * m + i, 1)], hid, mid_hi[:, c % 2, ds(2 * m + i, 1)].bitcast(F32),
                               ALU.subtract).then_inc(mid_ready, 1)

            add_matrix(U_SBO, norm=1)
            mlp(0, U_M1, 1)

            low, ex, lb, rest = (lower[:, n] for n in range(4))
            logits = gains[:, G_LB:G_LB + KD]
            steps(COPY(low, logits))
            steps.wait()
            TT(low, logits, low, ALU.subtract).then_inc(lb_step, 1)
            v.wait_ge(lb_step, 2)
            steps(v.reciprocal(low, ex))
            steps.wait()
            steps(TT(low, ex, low, ALU.mult))
            steps.wait()
            steps(TT(lb, low, low, ALU.subtract))
            steps(v.memset(hdiag, 0.0))
            steps.wait()
            TS(rest, lb, -1.0, 1.0, ALU.mult, ALU.add).then_inc(lb_step, 1)
            v.wait_ge(lb_step, 3)

            def nodes(t, h):
                return t.rearrange("p (n e j) -> p n e j", e=2, j=h)

            def hg_head(pp, par, current=True, following=True, previous=True, first=False):
                i = 2 * pp + par
                j = i + 1
                half = U_HG // 2 + 2 * i
                q, kk, b_ = hq[par % 2], hk[par % 2], hb[par % 2]
                q1, k1, b1 = hq[(par + 1) % 2], hk[(par + 1) % 2], hb[(par + 1) % 2]

                def sub(lv):
                    x, b = nodes(hx[lv % 3], HALVES[lv]), nodes(b_, HALVES[lv])
                    h = HALVES[lv]
                    mid = b[:, :, 0, h - 1:h].broadcast_to([P, S // (2 * h), h])
                    if lv == 0:
                        v.wait_ge(hg_b, i + 1)
                    if lv >= 3 or not first:
                        v.wait_ge(hg_mm, 8 * i + 1 + lv - 2)
                    TT(x[:, :, 1], b[:, :, 1], mid, ALU.subtract)
                    TT(x[:, :, 0], mid, b[:, :, 0], ALU.subtract).then_inc(hg_sub, 1)

                def mul(lv):
                    x = nodes(hx[lv % 3], HALVES[lv])
                    v.wait_ge(hg_exp, 7 * i + lv + 1)
                    TT(x[:, :, 1], x[:, :, 1], nodes(q, HALVES[lv])[:, :, 1], ALU.mult)
                    TT(x[:, :, 0], x[:, :, 0], nodes(kk, HALVES[lv])[:, :, 0], ALU.mult).then_inc(hg_mul, 1)

                def pred(lv):
                    v.wait_ge(hg_mm, 8 * i + 2 + lv)
                    v.wait_ge(hg_pred, 8 * i + 1 + lv)
                    v.sem_inc(pred_turn, 1)
                    v.copy_predicated(nodes(hdiag, HALVES[lv])[:, :, 1],
                                      level_mask[:, lv].rearrange("p (n j) -> p n j", j=HALVES[lv]),
                                      sc[lv % 2][:, 0:NB * HD].rearrange("p (n j) -> p n j", j=HALVES[lv])).then_inc(hg_pred, 1)

                for k in range(HG_SLOTS):
                    if current:
                        if k == 0:
                            take(half + 1, 1)
                            TT(hgraw, acc[1][:], rstd[:], ALU.mult).then_inc(evacuated[1], 1)
                            v.wait_ge(hg_mm, 8 * i + 1)
                            if not first:
                                v.wait_ge(hg_pv, i)
                            v.sem_inc(pred_turn, 1)
                            v.copy_predicated(hdiag, same_mask[:], sc[1][:]).then_inc(hg_pred, 1)
                        if 1 <= k < 8:
                            sub(k - 1)
                        if 2 <= k < 9:
                            mul(k - 2)
                        if 3 <= k < 10:
                            pred(k - 3)
                        if k == 7:
                            if not first:
                                v.wait_ge(hg_offexp, i)
                            TT(hg_col[:], b_[:, P - 1:P], b_[:, 2 * P - 1:2 * P], ALU.add).then_inc(hg_bias, 1)
                        if k == 11:
                            v.wait_ge(hg_offexp, i + 1)
                            for x, h in ((hx128, P), (hx256, 2 * P)):
                                x, q_, k_ = nodes(x, h), nodes(q, h), nodes(kk, h)
                                TT(x[:, :, 1], x[:, :, 1], q_[:, :, 1], ALU.mult)
                                last = TT(x[:, :, 0], x[:, :, 0], k_[:, :, 0], ALU.mult)
                            last.then_inc(hg_offmul, 1)
                        if k == 10:
                            v.wait_ge(hg_glog, i + 1)
                            STT(hgraw, hgraw, 0.0, hgsig, ALU.min, ALU.subtract).then_inc(hg_gls, 1)
                    if current and previous and k == 3:
                        hg_normed(i - 1)
                    if current and previous and k == 5:
                        hg_low(i - 1)
                    if following:
                        if k == 4:
                            if par == -1:
                                v.wait_ge(rstd_ready, 4 * LAYERS + 3)
                            take(half + 2, 0)
                            TT(hraw, acc[0][:], rstd[:], ALU.mult).then_inc(evacuated[0], 1)
                            v.wait_ge(evacuated[0], half + 3)
                            TS(ht2, hraw, -1.0, 80.0, ALU.mult, ALU.min).then_inc(hg_fm, 1)
                        if k == 6:
                            v.wait_ge(hg_flog, j + 1)
                            steps(STT(ht1, hraw, 0.0, ht1, ALU.min, ALU.subtract))
                            steps.wait()
                            TT(hfd, ht1, hraw, ALU.subtract).then_inc(hg_fd, 1)
                        if k == 7:
                            v.wait_ge(hg_fexp, j + 1)
                            TS(k1, hfd, rest[:, ds(j, 1)], None, ALU.mult).then_inc(hg_k, 1)
                        if k == 8:
                            take(half + 2, 1)
                            TT(hraw, acc[1][:], rstd[:], ALU.mult).then_inc(evacuated[1], 1)
                        if k == 9:
                            v.wait_ge(hg_flb, j + 1)
                            steps(TT(ht2, ht1, ht2, ALU.add))
                            steps.wait()
                            for b in range(NB):
                                c = slice(b * P, b * P + P)
                                scan = v.tensor_tensor_scan(b1[:, c], ones[:, c], ht2[:, c], 0.0, ALU.mult, ALU.add)
                            scan.then_inc(hg_b, 1)
                        if k == 11:
                            v.wait_ge(hg_qlog, j + 1)
                            STT(ht1, hraw, 0.0, ht1, ALU.min, ALU.subtract).then_inc(hg_qls, 1)
                        if k == 12:
                            v.wait_ge(hg_qsig, j + 1)
                            TT(q1, hraw, ht1, ALU.mult).then_inc(hg_q, 1)
                        if k == 12:
                            take(half + 3, 0)
                            TT(hvraw, acc[0][:], rstd[:], ALU.mult).then_inc(evacuated[0], 1)

            def hg_normed(i):
                v.wait_ge(hg_ors, i + 1)
                steps(STT(horow, horow, gains[:, G_HG:G_HG + 1], hors, ALU.mult, ALU.mult))
                steps.wait()
                v.wait_ge(hg_gsig, i + 1)
                TT(horow, horow, hgsig, ALU.mult).then_inc(hg_on, 1)

            def hg_low(i):
                v.wait_ge(hg_ohi, i + 1)
                TT(mid_lo[:, 0, ds(i, 1)], horow, mid_hi[:, 0, ds(i, 1)].bitcast(F32), ALU.subtract).then_inc(hg_oready, 1)

            hg_head(0, -1, current=False)
            hg_head(0, 0, previous=False, first=True)
            hg_head(0, 1)
            with v.Fori(1, KD // 2 - 1) as pp:
                steps.enter(pp - 1, HG_STEPS)
                hg_head(pp, 0)
                hg_head(pp, 1)
                steps.leave(KD // 2 - 2)
            hg_head(KD // 2 - 1, 0)
            hg_head(KD // 2 - 1, 1, following=False)
            hg_normed(KD - 1)
            hg_low(KD - 1)
            add_matrix(U_HGO, norm=3)
            mlp(1, U_M2, 3)
            for t in range(NB):
                v.wait_ge(pre_pe, 2 + KD + 2 * t + 1)
                COPY(x_tok[:, t, 0:512], tp[0][:])
                v.wait_ge(pre_pe, 2 + KD + 2 * t + 2)
                COPY(x_tok[:, t, 512:1024], tp[1][:]).then_inc(out_ready, 1)

        @block.scalar
        def _(a):
            steps = Steps(a, act_step)
            ACTV = a.activation
            for i, g in ((G_ATT_PRE, attn_pre_g), (G_ATT_POST, attn_post_g), (G_FFN_PRE, ffn_pre_g), (G_FFN_POST, ffn_post_g)):
                a.dma_start(grow[i:i + 16, :], g.rearrange("l (j c) -> (l j) c", c=P)).then_inc(consts_in, 16)
            a.dma_start(grow[G_B2:G_B2 + 32, :], norm_gains_2.rearrange("l w (j c) -> (l w j) c", c=P)).then_inc(consts_in, 16)
            a.dma_start(grow[G_LB:G_LB + 8, :], hg_lb_logits_2.rearrange("l (j c) -> (l j) c", c=P)).then_inc(consts_in, 16)
            a.dma_start(grow[G_DIFF:G_DIFF + LAYERS, :], diff_sub_g).then_inc(consts_in, 16)
            a.dma_start(grow[G_HG:G_HG + 1, :], hg_norm_gain_2).then_inc(consts_in, 16)
            for i in range(2):
                a.dma_start(grow[G_SBQ:G_SBQ + 1, i * HD:i * HD + HD], sb_q_gain_2).then_inc(consts_in, 16)
                a.dma_start(grow[G_SBK:G_SBK + 1, i * HD:i * HD + HD], sb_k_gain_2).then_inc(consts_in, 16)
            for i, w in enumerate((lam_q1, lam_k1, lam_q2, lam_k2)):
                a.dma_start(lam_in[:, i], w.partition_broadcast(P)).then_inc(consts_in, 16)
            a.dma_start(pos_i, positions.rearrange("b s -> (b s)").partition_broadcast(P)).then_inc(consts_in, 16)
            a.wait_ge(vec_consts, 1)
            with nc.allow_non_contiguous_dma(reason="16 words"):
                a.dma_start(lconst[120:P, :, 2], forget_bias.rearrange("l h -> h l")).then_inc(consts_in, 16)
            def high_part(x_n, j, gain):
                a.wait_ge(x_ready, x_n + j + 1)
                ACTV(h_hi[:, j], xT[:, j], ACT.Identity, scale=gain).then_inc(h_hi_ready, 1)

            def square_of(src, i):
                ACTV(square[i], src, ACT.Square).then_inc(square_ready, 1)

            def inv_rms(a_n, width):
                a.wait_ge(aux_done, a_n + 1)
                ACTV(logs, aux[:], ACT.Ln, bias=eps_col[:, 0:1], scale=1.0 / width).then_inc(aux_free, 1)
                a.wait_ge(aux_free, a_n + 1)
                ACTV(rstd[:], logs, ACT.Exp, scale=-0.5).then_inc(rstd_ready, 1)

            def pre_norm(x_n, n, gain_of):
                for j in range(KD):
                    high_part(x_n, j, gain_of(j))
                    if j >= 2:
                        a.wait_ge(square_summed, n * (KD - 1) + j - 1)
                    square_of(xT[:, j], j % 2)

            pre_norm(0, 0, lambda j: gains[:, G_ATT_PRE + j:G_ATT_PRE + j + 1])
            a.wait_ge(vec_consts, 5)
            ACTV(sinT[:], red, ACT.Sin).then_inc(act_consts, 1)
            a.wait_ge(vec_consts, 6)
            ACTV(cosT[:], red, ACT.Sin).then_inc(act_consts, 1)
            a.wait_ge(vec_consts, 4)
            a.preload_act_table_set("natural_log_exp_and_others")
            ACTV(lam_e, lam_s, ACT.Exp).then_inc(act_consts, 1)

            with a.Fori(0, LAYERS) as l:
                steps.enter(l, ACT_STEPS_LAYER)
                A = l * A_LAYER
                half0 = l * (U_LAYER // 2)
                a.wait_ge(layer_const, l + 1)
                inv_rms(A + AUX["norm_att"], D)

                def take_t(p, i):
                    ti = T_BASE[p] + i
                    t = i if p < NDIFF else i // 2
                    a.wait_ge(t_done, l * T_BASE[PAIRS] + ti + 1)
                    ACTV(probT[ti % 2][:, 0:(t + 1) * P], tp[ti % 2][:, 0:(t + 1) * P], ACT.Copy).then_inc(t_taken, 1)

                def high_output(p):
                    if p < NDIFF:
                        a.wait_ge(o_normed, l * NDIFF + p + 1)
                        src = onrm
                    else:
                        a.wait_ge(po_taken, l * PAIRS + p + 1)
                        src = orow
                    ACTV(mid_hi[:, 0, p], src, ACT.Copy).then_inc(o_hi_ready, 1)

                for p in range(-1, PAIRS):
                    for k in range(SLOTS):
                        if p == -1:
                            continue
                        if k == 0 and 0 <= p - 1 < NDIFF:
                            a.wait_ge(po_taken, l * PAIRS + p)
                            ACTV(osq, orow, ACT.Square).then_inc(o_square, 1)
                        if k == 0 and p - 1 >= NDIFF:
                            high_output(p - 1)
                        if k < 8:
                            n = (k // 2 + 1) * P
                            a.wait_ge(max_done, l * 64 + p * 8 + k + 1)
                            ACTV(prob[k % 4][:, 0:n], sc[k % 2][:, 0:n], ACT.Exp, bias=stat[:, k % 4:k % 4 + 1],
                                 accum_out=stat[:, 4 + k % 4:5 + k % 4]).then_inc(exp_done, 1)
                        if k == 1:
                            v_use = AUX[("v", p)]
                            a.wait_ge(aux_done, A + v_use + 1)
                            ACTV(vtok.rearrange("p j c -> p (j c)"), aux[:], ACT.Copy).then_inc(aux_free, 1)
                        if k == 5 and 0 <= p - 1 < NDIFF:
                            n = AUX[("o_norm", p - 1)]
                            a.wait_ge(aux_done, A + n + 1)
                            ACTV(ologs, aux[:], ACT.Ln, bias=eps_col[:, 0:1], scale=1.0 / (2 * HD)).then_inc(aux_free, 1)
                            a.wait_ge(aux_free, A + n + 1)
                            ACTV(ologs, ologs, ACT.Exp, scale=-0.5).then_inc(o_rstd, 1)
                        if k == 7 and 0 <= p - 1 < NDIFF:
                            high_output(p - 1)
                        if p < NDIFF and k >= 3 and k % 2 == 1 and (k - 3) // 2 < 4:
                            take_t(p, (k - 3) // 2)
                        if p >= NDIFF and 2 <= k < 10:
                            take_t(p, k - 2)
                    if p == -1:
                        f = slice(96, P)
                        a.wait_ge(f_ready, l + 1)
                        steps(ACTV(ologs_f[f], raw_f[f], ACT.Abs))
                        steps.wait()
                        steps(ACTV(ologs_f[f], ologs_f[f], ACT.Exp, scale=-1.0))
                        steps.wait()
                        ACTV(ologs_f[f], ologs_f[f], ACT.Ln, bias=1.0).then_inc(f_log, 1)
                high_output(PAIRS - 1)

                def square_loop(half, added):
                    with a.Fori(0, KD // 2) as m:
                        for i in range(2):
                            a.wait_ge(evacuated[i], half + m + 1)
                            a.wait_ge(square_added, added + 2 * m + i - 1)
                            square_of(yT[:, ds(2 * m + i, 1)], i)

                square_loop(half0 + U_OUT // 2, added_base(2 * l))
                inv_rms(A + AUX["norm_att_post"], D)
                pre_norm(l * 16 + 8, 2 * l + 1, lambda j: layer_gain[:, 1, j:j + 1])
                inv_rms(A + AUX["norm_ffn"], D)
                for kind, c, u in FFN_ORDER:
                    first, n = FF1_CHUNKS[c]
                    half = half0 + u // 2
                    if kind == "gu":
                        with a.Fori(0, n) as j:
                            steps.enter(j, 2)
                            g = l * FF1_TILES + first + j
                            a.wait_ge(evacuated[0], half + j + 1)
                            steps(ACTV(gate_t, gate, ACT.Abs))
                            steps.wait()
                            steps(ACTV(gate_t2, gate_t, ACT.Exp, scale=-1.0))
                            steps.wait()
                            ACTV(gate_t2, gate_t2, ACT.Ln, bias=1.0).then_inc(gate_log, 1)
                            a.wait_ge(gate_ls, g + 1)
                            ACTV(gate_t2, gate_t, ACT.Exp).then_inc(gate_sig, 1)
                            a.wait_ge(hid_ready, g + 1)
                            ACTV(mid_hi[:, c % 2, ds(j, 1)], hid, ACT.Copy).then_inc(mid_hi_ready, 1)
                            steps.leave(n)
                    elif c == 2:
                        square_loop(half, added_base(2 * l + 1))
                inv_rms(A + AUX["norm_ffn_post"], D)
                pre_norm(l * 16 + 16, 2 * l + 2, lambda j: layer_gain[:, 3, j:j + 1])
                steps.leave(LAYERS)

            def pre_norm2(norm, u):
                added = block2_norm(norm)[2]
                for j in range(KD):
                    gain = G_B2 + norm * KD + j
                    a.wait_ge(evacuated[j % 2], u // 2 + j // 2 + 1)
                    ACTV(h_hi[:, j], xT[:, j], ACT.Identity, scale=gains[:, gain:gain + 1]).then_inc(h_hi_ready, 1)
                    a.wait_ge(square_added, added + j - 1)
                    square_of(xT[:, j], j % 2)

            def sb_pair(pp, par, current=True, following=True, previous=True):
                p = 2 * pp + par
                half = U_SB // 2 + 3 * pp
                aux_n = A_SB + 3 + 3 * p

                def softplus_log(m):
                    parts = [sb_log[:, at:at + n] for _, _, at, n in Z_PARTS]

                    def magnitude(i):
                        a.wait_ge(z_done, 6 * p + 3 * m + i + 1)
                        steps(ACTV(parts[i], z[Z_PARTS[i][0]][:, 0:Z_PARTS[i][3]], ACT.Abs))

                    magnitude(0)
                    magnitude(1)
                    steps.wait()
                    steps(ACTV(parts[0], parts[0], ACT.Exp, scale=-1.0))
                    magnitude(2)
                    steps.wait()
                    ACTV(parts[0], parts[0], ACT.Ln, bias=1.0).then_inc(z_log, 1)
                    for i in (1, 2):
                        steps(ACTV(parts[i], parts[i], ACT.Exp, scale=-1.0))
                        steps.wait()
                        ACTV(parts[i], parts[i], ACT.Ln, bias=1.0).then_inc(z_log, 1)

                def weights(m):
                    for i, (bank, _, at, n) in enumerate(Z_PARTS):
                        a.wait_ge(logw_done, 6 * p + 3 * m + i + 1)
                        e = ACTV(sb_w[:, at:at + n], z[bank][:, 0:n], ACT.Exp)
                    e.then_inc(w_ready, 1)

                def raw_norm(i, k, first, last):
                    u = 3 * (par + 1) + i
                    if k == first:
                        a.wait_ge(evacuated[u % 2], half + u // 2 + 1)
                        ACTV(sb_sq, raw, ACT.Square).then_inc(raw_square, 1)
                    if k == last:
                        a.wait_ge(aux_done, aux_n + 2 + i)
                        ACTV(sb_logs, aux[:], ACT.Ln, bias=eps_col[:, 0:1], scale=1.0 / HD).then_inc(aux_free, 1)
                        a.wait_ge(aux_free, aux_n + 2 + i)
                        ACTV(sb_logs, sb_logs, ACT.Exp, scale=-0.5).then_inc(raw_rstd, 1)

                for k in range(SLOTS):
                    if current and k in (0, 6):
                        softplus_log(k // 6)
                    if current and previous and k == 3:
                        sb_high(p - 1)
                    if current and k == 2:
                        a.wait_ge(aux_done, aux_n + 1)
                        ACTV(vtok.rearrange("p j c -> p (j c)"), aux[:], ACT.Copy).then_inc(aux_free, 1)
                    if current and k in (5, 11):
                        weights(k // 6)
                    if following:
                        raw_norm(0, k, 4, 6)
                        raw_norm(1, k, 8, 10)

            def sb_high(p):
                a.wait_ge(sbo_taken, p + 2)
                ACTV(mid_hi[:, 0, ds(p, 1)], sb_orow, ACT.Copy).then_inc(sbo_hi, 1)

            z = [sc[0], sc[1], tp[0]]
            a.sem_inc(w_ready, 1)
            inv_rms(A_SB, D)
            sb_pair(0, -1, current=False)
            sb_pair(0, 0, previous=False)
            sb_pair(0, 1)
            with a.Fori(1, PAIRS // 2 - 1) as pp:
                steps.enter(pp - 1, SB_ACT_STEPS)
                sb_pair(pp, 0)
                sb_pair(pp, 1)
                steps.leave(PAIRS // 2 - 2)
            sb_pair(PAIRS // 2 - 1, 0)
            sb_pair(PAIRS // 2 - 1, 1, following=False)
            sb_high(PAIRS - 1)

            def mlp(i_mlp):
                for kind, c, u in MLP_UNITS:
                    if kind == "up":
                        with a.Fori(0, KD) as j:
                            a.wait_ge(hid_ready, MID1 + i_mlp * (FF2 // P) + 8 * c + j + 1)
                            ACTV(mid_hi[:, c % 2, ds(j, 1)], hid, ACT.Copy).then_inc(mid_hi_ready, 1)

            pre_norm2(1, U_SBO)
            inv_rms(A_M1, D)
            mlp(0)

            pre_norm2(2, U_M1 + 56)
            a.wait_ge(lb_step, 1)
            ACTV(lower[:, 1], lower[:, 0], ACT.Exp).then_inc(lb_step, 1)
            lb = lower[:, 2]

            def log_sigmoid_part(t, src, done):
                steps(ACTV(t, src, ACT.Abs))
                steps.wait()
                steps(ACTV(t, t, ACT.Exp, scale=-1.0))
                steps.wait()
                ACTV(t, t, ACT.Ln, bias=1.0).then_inc(done, 1)

            def hg_head(pp, par, current=True, following=True, previous=True, first=False):
                i = 2 * pp + par
                j = i + 1
                half = U_HG // 2 + 2 * i
                b_ = hb[par % 2]
                for k in range(HG_SLOTS):
                    if current:
                        if k == 1:
                            a.wait_ge(aux_done, a_hgv(i, first) + 1)
                            ACTV(hvtok.rearrange("p j c -> p (j c)"), aux[:], ACT.Copy).then_inc(aux_free, 1)
                        if 1 <= k < 8:
                            lv = k - 1
                            a.wait_ge(hg_sub, 7 * i + lv + 1)
                            ACTV(hx[lv % 3], hx[lv % 3], ACT.Exp).then_inc(hg_exp, 1)
                        if k == 9:
                            a.wait_ge(evacuated[1], half + 2)
                            if not first:
                                a.wait_ge(hg_on, i)
                            log_sigmoid_part(hgsig, hgraw, hg_glog)
                        if k == 12:
                            a.wait_ge(hg_gls, i + 1)
                            ACTV(hgsig, hgraw, ACT.Exp).then_inc(hg_gsig, 1)
                        if k == 10:
                            a.wait_ge(hg_b, i + 1)
                            a.wait_ge(hg_bias, i + 1)
                            if not first:
                                a.wait_ge(hg_offmm, i)
                            end = [b_[:, b * P + P - 1:b * P + P] for b in range(NB)]
                            blk = [slice(b * P, b * P + P) for b in range(NB)]
                            for b in (1, 3):
                                ACTV(hx128[:, blk[b]], b_[:, blk[b]], ACT.Exp)
                            for b in (0, 2):
                                ACTV(hx128[:, blk[b]], b_[:, blk[b]], ACT.Exp, bias=end[b], scale=-1.0)
                            ACTV(hx256[:, blk[2]], b_[:, blk[2]], ACT.Exp)
                            ACTV(hx256[:, blk[3]], b_[:, blk[3]], ACT.Exp, bias=end[2])
                            ACTV(hx256[:, blk[1]], b_[:, blk[1]], ACT.Exp, bias=end[1], scale=-1.0)
                            ACTV(hx256[:, blk[0]], b_[:, blk[0]], ACT.Exp, bias=hg_col[:, 0:1],
                                 scale=-1.0).then_inc(hg_offexp, 1)
                        if k == 12:
                            a.wait_ge(hg_offmm, i + 1)
                            if not first:
                                a.wait_ge(hg_pv, i)
                            ACTV(hoff[:, 0:S], tp[0][:], ACT.Copy)
                            ACTV(hoff[:, S:S + 2 * P], tp[1][:, 0:2 * P], ACT.Copy).then_inc(hg_offtaken, 1)
                        if k == 15:
                            hg_square(i)
                    if current and previous and k == 2:
                        hg_inv_rms(i - 1)
                    if current and previous and k == 4:
                        hg_high(i - 1)
                    if following:
                        if k == 4:
                            a.wait_ge(evacuated[0], half + 3)
                            log_sigmoid_part(ht1, hraw, hg_flog)
                        if k == 8:
                            a.wait_ge(hg_fm, j + 1)
                            steps(ACTV(ht2, ht2, ACT.Exp))
                            steps.wait()
                            ACTV(ht2, ht2, ACT.Ln, bias=1.0, scale=lb[:, ds(j, 1)]).then_inc(hg_flb, 1)
                        if k == 6:
                            a.wait_ge(hg_fd, j + 1)
                            ACTV(hfd, hfd, ACT.Exp).then_inc(hg_fexp, 1)
                        if k == 10:
                            a.wait_ge(evacuated[1], half + 3)
                            a.wait_ge(hg_b, j + 1)
                            log_sigmoid_part(ht1, hraw, hg_qlog)
                        if k == 11:
                            a.wait_ge(hg_qls, j + 1)
                            ACTV(ht1, ht1, ACT.Exp).then_inc(hg_qsig, 1)

            def hg_square(i):
                a.wait_ge(hg_pv, i + 1)
                ACTV(horow, po[:], ACT.Copy).then_inc(hg_otaken, 1)
                a.wait_ge(hg_otaken, i + 1)
                ACTV(hosq, horow, ACT.Square).then_inc(hg_osq, 1)

            def hg_inv_rms(i, last=False):
                n = a_hgv(i + 1) + (0 if last else 1)
                a.wait_ge(aux_done, n + 1)
                ACTV(hors, aux[:], ACT.Ln, bias=eps_col[:, 0:1], scale=1.0 / P).then_inc(aux_free, 1)
                a.wait_ge(aux_free, n + 1)
                ACTV(hors, hors, ACT.Exp, scale=-0.5).then_inc(hg_ors, 1)

            def hg_high(i):
                a.wait_ge(hg_on, i + 1)
                ACTV(mid_hi[:, 0, ds(i, 1)], horow, ACT.Copy).then_inc(hg_ohi, 1)

            inv_rms(A_HG, D)
            hg_head(0, -1, current=False)
            hg_head(0, 0, previous=False, first=True)
            hg_head(0, 1)
            with a.Fori(1, KD // 2 - 1) as pp:
                steps.enter(pp - 1, HG_ACT_STEPS)
                hg_head(pp, 0)
                hg_head(pp, 1)
                steps.leave(KD // 2 - 2)
            hg_head(KD // 2 - 1, 0)
            hg_head(KD // 2 - 1, 1, following=False)
            hg_inv_rms(KD - 1, last=True)
            hg_high(KD - 1)
            pre_norm2(3, U_HGO)
            inv_rms(A_M2, D)
            mlp(1)


_INPUTS = ["x", "positions", "attn_pre_g", "w_in", "forget_bias", "lam_q1", "lam_k1", "lam_q2", "lam_k2", "diff_sub_g",
           "w_out", "attn_post_g", "ffn_pre_g", "w_gate", "w_up", "w_down", "ffn_post_g", "norm_gains_2",
           "sb_w_qkv_2", "sb_q_gain_2", "sb_k_gain_2", "sb_w_o_2", "hg_w_in_2", "hg_lb_logits_2", "hg_norm_gain_2",
           "hg_w_o_2", "mlp_w1_2", "mlp_w2_2"]


def kernel(**inputs):
    import numpy as _np
    import concourse.bacc as _bacc
    from concourse import mybir as _mybir
    from concourse.bass_utils import run_bass_kernel_spmd as _run

    nc = _bacc.Bacc("TRN2", target_bir_lowering=False, num_devices=1)
    arrays, args = {}, []
    for name in _INPUTS:
        a = _np.ascontiguousarray(inputs[name])
        arrays[f"in_{name}_dram"] = a
        args.append(nc.dram_tensor(f"in_{name}_dram", a.shape, _mybir.dt.from_np(a.dtype), kind="ExternalInput").ap())
    out = nc.dram_tensor("out_dram", inputs["x"].shape, _mybir.dt.float32, kind="ExternalOutput").ap()
    two_blocks(nc, *args, out)
    result = _run(nc, [arrays], core_ids=[0])
    return result.results[0]["out_dram"]
```

```python
import math
from contextlib import ExitStack

import numpy as np
import concourse.bass as bass
from concourse import mybir

F32 = mybir.dt.float32
F32R = mybir.dt.float32r
I32 = mybir.dt.int32
ALU = mybir.AluOpType
ACT = mybir.ActivationFunctionType
AX_X = mybir.AxisListType.X
ds = bass.ds

P = 128
S = 512
D = 1024
KD = D // P
NB = S // P
LAYERS = 2
HD = 64
DIFF_W = 512
FOX_W = 512
FF1 = 2816
FF2 = 4096
EPS = 1e-6
NEG = -1e30
ROT_HALF = 8
THETA = 500000.0

FF1_CHUNKS = [(0, 8), (8, 8), (16, 6)]
FF1_TILES = FF1 // P
FF2_CHUNKS = [(0, 8), (8, 8), (16, 8), (24, 8)]
U_ATT, U_OUT, U_GU0, U_GU1, U_D0, U_GU2, U_D1, U_D2, U_LAYER = 0, 24, 32, 48, 64, 72, 84, 92, 100
FFN_ORDER = [("gu", 0, U_GU0), ("gu", 1, U_GU1), ("down", 0, U_D0), ("gu", 2, U_GU2), ("down", 1, U_D1),
             ("down", 2, U_D2)]
PAIRS = 8
NDIFF = 4
SLOTS = 12
HEAD_TILES = 8
T_OF = [4 if p < NDIFF else 8 for p in range(PAIRS)]
T_BASE = [sum(T_OF[:p]) for p in range(PAIRS + 1)]
LAM_INIT = [0.8 - 0.6 * math.exp(-0.3 * l) for l in range(LAYERS)]

G_ATT_PRE, G_B2, G_ATT_POST, G_FFN_PRE, G_FFN_POST, G_LB, G_DIFF, G_HG, G_SBQ, G_SBK, G_ROWS = (
    0, 16, 48, 64, 80, 96, 104, 106, 107, 108, 109)


def aux_uses():
    uses = []
    for p in range(-1, PAIRS):
        for k in range(SLOTS):
            if p == -1 and k == 3:
                uses.append("norm_att")
            if k == 1 and p >= 0:
                uses.append(("v", p))
            if k == 4 and 0 <= p - 1 < NDIFF:
                uses.append(("o_norm", p - 1))
            if k == 6 and p + 1 < NDIFF:
                uses.append(("rot_q", p + 1))
            if k == 9 and p + 1 < NDIFF:
                uses.append(("rot_k", p + 1))
    uses += ["norm_att_post", "norm_ffn", "norm_ffn_post"]
    return {u: i for i, u in enumerate(uses)}


AUX = aux_uses()
A_LAYER = len(AUX)

U2 = LAYERS * U_LAYER
U_SB, U_SBO, U_M1 = U2, U2 + 24, U2 + 32
U_HG = U_M1 + 64
U_HGO, U_M2 = U_HG + 32, U_HG + 40
U_END = U_M2 + 64
MLP_ORDER = [("up", 0), ("up", 1), ("down", 0), ("up", 2), ("down", 1), ("up", 3), ("down", 2), ("down", 3)]
MLP_UNITS = [(kind, c, 8 * i) for i, (kind, c) in enumerate(MLP_ORDER)]
Z_AT = [0, 512, 896, 1152]
Z_N = [512, 384, 256, 128]
Z_W = 1280
Z_BANK = [(0, 0), (1, 0), (2, 0), (2, 256)]
Z_PARTS = [(2, (2, 3), 896, 384), (1, (1,), 512, 384), (0, (0,), 0, 512)]
A_SB = LAYERS * A_LAYER
A_M1 = A_SB + 3 * PAIRS + 1
MID1 = LAYERS * FF1_TILES
A_HG = A_M1 + 1
A_M2 = A_HG + 17
U_LAST = U_END
LAG = 3
EARLY = 9
OUT_PARTS = [(0, 4), (4, 2), (6, 2)]
TAIL = 6
HG_SLOTS = 16
HALVES = [64, 32, 16, 8, 4, 2, 1]


def a_hgv(i, first=False):
    return A_HG + 1 if first else A_HG + 2 * i


def added_base(n):
    return 2 + KD * n


def block2_norm(i):
    return KD * (2 * LAYERS + i), KD * (4 * LAYERS + i), added_base(2 * LAYERS + i - 1)


VEC_STEPS_LAYER = 93
SB_STEPS = 40
SB_ACT_STEPS = 24
HG_STEPS = 6
HG_ACT_STEPS = 14
ACT_STEPS_LAYER = 46


class Steps:

    def __init__(self, engine, sem):
        self.engine, self.sem, self.base, self.n, self.outer = engine, sem, 0, 0, []

    def __call__(self, instruction):
        instruction.then_inc(self.sem, 1)
        self.n += 1

    def wait(self):
        self.engine.wait_ge(self.sem, self.base + self.n)

    def enter(self, i, per):
        self.outer.append((self.base, self.n, per))
        self.base, self.n = self.base + self.n + i * per, 0

    def leave(self, times):
        base, n, per = self.outer.pop()
        assert self.n == per, (self.n, per)
        self.base, self.n = base, n + times * per


def two_blocks(nc, x, positions, attn_pre_g, w_in, forget_bias, lam_q1, lam_k1, lam_q2, lam_k2, diff_sub_g,
               w_out, attn_post_g, ffn_pre_g, w_gate, w_up, w_down, ffn_post_g, norm_gains_2, sb_w_qkv_2,
               sb_q_gain_2, sb_k_gain_2, sb_w_o_2, hg_w_in_2, hg_lb_logits_2, hg_norm_gain_2, hg_w_o_2,
               mlp_w1_2, mlp_w2_2, out):
    with ExitStack() as ctx:
        def sb(name, shape, dt=F32):
            return ctx.enter_context(nc.sbuf_tensor(name, shape, dt))

        def sem(name):
            return ctx.enter_context(nc.semaphore(name))

        xT = sb("xT", [P, KD, S])
        h_hi = sb("h_hi", [P, KD, S], F32R)
        h_lo = sb("h_lo", [P, KD, S], F32R)
        mid_hi = sb("mid_hi", [P, 2, HEAD_TILES, S], F32R)
        mid_lo = sb("mid_lo", [P, 2, HEAD_TILES, S], F32R)
        yT = sb("yT", [P, KD, S])
        w_raw = sb("w_raw", [P, 2, 8, P])
        w_hi = sb("w_hi", [P, 2, 8, P], F32R)
        w_lo = sb("w_lo", [P, 2, 8, P], F32R)
        scratch = sb("scratch", [P, 6144])
        rstd = sb("rstd", [P, S])
        ident = sb("ident", [P, P])
        ident_r = sb("ident_r", [P, P], F32R)
        mask_r = sb("mask_r", [P, P], F32R)
        ones = sb("ones", [P, S])
        rotT = sb("rotT", [P, P])
        cosT = sb("cosT", [P, S])
        sinT = sb("sinT", [P, S])
        gains = sb("gains", [P, G_ROWS])
        layer_gain = sb("layer_gain", [P, 4, KD])
        lconst = sb("lconst", [P, LAYERS, 4])
        lcur = sb("lcur", [P, 4])
        eps_col = sb("eps_col", [P, 1])
        neg_incl_r = sb("neg_incl_r", [P, P], F32R)
        neg_ones_r = sb("neg_ones_r", [P, P], F32R)
        mask_sb_r = sb("mask_sb_r", [P, P], F32R)
        before01 = sb("before01", [P, P])
        head_ones = sb("head_ones", [P, P])
        sb_gain = sb("sb_gain", [P, 2])
        hdiag_t = sb("hdiag_t", [P, S])
        hoff_t = sb("hoff_t", [P, 768])
        lower = sb("lower", [P, 4, KD])
        hg_col = sb("hg_col", [P, 1])
        level_mask = sb("level_mask", [P, len(HALVES), NB * HD], mybir.dt.uint8)
        same_mask = sb("same_mask", [P, NB * P], mybir.dt.uint8)
        stat = sb("stat", [P, 16])
        sel_r = sb("sel_r", [P, 8, P], F32R)

        def part(a, n):
            return yT.rearrange("p a b -> p (a b)")[:, a:a + n] if a < KD * S else scratch[:, a - KD * S:a - KD * S + n]

        wf_raw = sb("wf_raw", [P, 8, P])
        wf_flat = wf_raw.rearrange("p k c -> p (k c)")
        negc = sb("negc", [P, S])
        raw = part(0, 512)
        vraw = part(512, 512)
        vtok = part(1024, 512).rearrange("p (j c) -> p j c", j=NB)
        rcos = part(1536, 512)
        rsin = part(2048, 512)
        orow = part(2560, 512)
        osq = part(3072, 512)
        onrm = part(3584, 512)
        qT = [part(4096 + 512 * i, 512) for i in range(2)]
        kT = [part(5120 + 512 * i, 512) for i in range(2)]
        prob = [part(6144 + 512 * i, 512) for i in range(4)]
        probT = [part(8192 + 512 * i, 512) for i in range(2)]
        ologs = part(9216, 512)
        raw_f, ologs_f = osq, orow
        logs = part(9728, 512)
        square = [part(4096 + 512 * i, 512) for i in range(2)]
        square_sum = part(5120, 512)
        pair_sum = [square_sum, part(5632, 512)]
        gate = part(5632, 512)
        gate_t = part(6144, 512)
        gate_t2 = part(6656, 512)
        up = part(7168, 512)
        hid = part(7680, 512)
        sb_orow = part(1536, 512)
        sb_sq = part(2048, 512)
        sb_logs = part(2560, 512)
        sb_log = part(4096, Z_W)
        sb_stay = part(4096 + Z_W, Z_W)
        sb_w = part(4096 + 2 * Z_W, Z_W)
        sqT = [part(7936 + 512 * i, 512) for i in range(2)]
        skT = [part(8960 + 512 * i, 512) for i in range(2)]
        stay_hi = mid_hi[:, 1].rearrange("p a b -> p (a b)")[:, 0:Z_W]
        stay_lo = mid_lo[:, 1].rearrange("p a b -> p (a b)")[:, 0:Z_W]
        tile_of = [part(512 * i, 512) for i in range(20)] + [cosT[:], sinT[:], negc[:], wf_flat[:, 0:512], wf_flat[:, 512:1024]]
        hq, hk, hb = tile_of[0:2], tile_of[2:4], tile_of[4:6]
        hvraw, hvtok, hgraw, hgsig = tile_of[6], tile_of[7].rearrange("p (j c) -> p j c", j=NB), tile_of[11], tile_of[12]
        horow, hosq, hors = tile_of[13:16]
        hraw, ht1, ht2, hfd = tile_of[16:20]
        hx = tile_of[20:23]
        hx128, hx256 = tile_of[23], tile_of[24]
        hdiag = hdiag_t[:]
        hoff = hoff_t[:]
        decay_r = mid_lo[:, 1, 0:2]
        wf_hi = mid_hi[:, 1].rearrange("p a b -> p (a b)")[:, 0:1024].rearrange("p (k c) -> p k c", k=8)
        wf_lo = mid_hi[:, 1].rearrange("p a b -> p (a b)")[:, 1024:2048].rearrange("p (k c) -> p k c", k=8)

        def psum(name):
            return ctx.enter_context(nc.psum_tensor(name, [P, S], F32))

        acc = [psum("acc0"), psum("acc1")]
        sc = [psum("sc0"), psum("sc1")]
        tp = [psum("tp0"), psum("tp1")]
        po = psum("po")
        aux = psum("aux")

        consts_in = sem("consts_in")
        x_in = sem("x_in")
        w_landed = [sem("w_landed0"), sem("w_landed1")]
        w_split = sem("w_split")
        unit_done = sem("unit_done")
        load_turn = sem("load_turn")
        split_turn = sem("split_turn")
        pred_turn = sem("pred_turn")
        evacuated = [sem("evacuated0"), sem("evacuated1")]
        pool_consts = sem("pool_consts")
        pool_step = sem("pool_step")
        vec_consts = sem("vec_consts")
        vec_step = sem("vec_step")
        act_step = sem("act_step")
        act_consts = sem("act_consts")
        pre_pe = sem("pre_pe")
        gains_ready = sem("gains_ready")
        x_ready = sem("x_ready")
        h_hi_ready = sem("h_hi_ready")
        h_ready = sem("h_ready")
        square_ready = sem("square_ready")
        square_added = sem("square_added")
        pair_added = sem("pair_added")
        square_summed = sem("square_summed")
        y_scaled = sem("y_scaled")
        rstd_ready = sem("rstd_ready")
        layer_const = sem("layer_const")
        aux_done = sem("aux_done")
        aux_free = sem("aux_free")
        qk_ready = sem("qk_ready")
        score_done = sem("score_done")
        max_done = sem("max_done")
        exp_done = sem("exp_done")
        p_ready = sem("p_ready")
        t_done = sem("t_done")
        t_taken = sem("t_taken")
        pv_done = sem("pv_done")
        po_taken = sem("po_taken")
        o_square = sem("o_square")
        o_rstd = sem("o_rstd")
        o_normed = sem("o_normed")
        o_hi_ready = sem("o_hi_ready")
        o_ready = sem("o_ready")
        wf_landed = sem("wf_landed")
        wf_split = sem("wf_split")
        wf_done = sem("wf_done")
        f_taken = sem("f_taken")
        f_ready = sem("f_ready")
        f_log = sem("f_log")
        decay_ready = sem("decay_ready")
        gate_log = sem("gate_log")
        raw_square = sem("raw_square")
        hg_f_negated = sem("hg_f_negated")
        hg_f_log = sem("hg_f_log")
        hg_bound_log = sem("hg_bound_log")
        hg_key_log = sem("hg_key_log")
        hg_key_exp = sem("hg_key_exp")
        hg_key_ready = sem("hg_key_ready")
        hg_q_log = sem("hg_q_log")
        hg_q_logsig = sem("hg_q_logsig")
        hg_q_sigmoid = sem("hg_q_sigmoid")
        hg_query_ready = sem("hg_query_ready")
        hg_g_log = sem("hg_g_log")
        hg_g_logsig = sem("hg_g_logsig")
        hg_g_sigmoid = sem("hg_g_sigmoid")
        level_sub = sem("level_sub")
        level_exp = sem("level_exp")
        level_mul = sem("level_mul")
        level_scored = sem("level_scored")
        level_taken = sem("level_taken")
        cross_exp = sem("cross_exp")
        cross_mul = sem("cross_mul")
        cross_scored = sem("cross_scored")
        cross_taken = sem("cross_taken")
        hg_col_ready = sem("hg_col_ready")
        hg_pv_done = sem("hg_pv_done")
        hg_o_taken = sem("hg_o_taken")
        hg_o_square = sem("hg_o_square")
        hg_o_rstd = sem("hg_o_rstd")
        hg_o_normed = sem("hg_o_normed")
        hg_o_hi = sem("hg_o_hi")
        hg_o_ready = sem("hg_o_ready")
        hg_decay_ready = sem("hg_decay_ready")
        lb_step = sem("lb_step")
        raw_rstd = sem("raw_rstd")
        sb_qk_ready = sem("sb_qk_ready")
        z_done = sem("z_done")
        z_log = sem("z_log")
        stay_ready = sem("stay_ready")
        logw_done = sem("logw_done")
        w_ready = sem("w_ready")
        sb_pv_done = sem("sb_pv_done")
        sb_o_taken = sem("sb_o_taken")
        sb_o_hi = sem("sb_o_hi")
        sb_o_ready = sem("sb_o_ready")
        gate_ls = sem("gate_ls")
        gate_sig = sem("gate_sig")
        gu_done = sem("gu_done")
        hid_ready = sem("hid_ready")
        mid_hi_ready = sem("mid_hi_ready")
        mid_ready = sem("mid_ready")
        out_ready = sem("out_ready")
        out_stored = sem("out_stored")

        def tiles(w):
            return w.rearrange("l (k p) c -> p (l k) c", p=P)

        w_in_t, w_out_t, w_gate_t, w_up_t, w_down_t = map(tiles, (w_in, w_out, w_gate, w_up, w_down))
        sb_qkv_t, sb_o_t, hg_in_t, hg_o_t, w1_t, w2_t = map(
            tiles, (sb_w_qkv_2, sb_w_o_2, hg_w_in_2, hg_w_o_2, mlp_w1_2, mlp_w2_2))
        x_rows = x.rearrange("b (t p) d -> p (b t) d", p=P)
        out_rows = out.rearrange("b (t p) d -> p (b t) d", p=P)
        x_tok = yT.rearrange("p a b -> p (a b)").rearrange("p (t d) -> p t d", t=NB)
        grow = scratch[:, 0:128]
        lam_in = sinT[:, 0:4 * LAYERS * HD].rearrange("p (v l c) -> p v l c", v=4, l=LAYERS)
        pos_i = scratch[:, 2048:2560].bitcast(I32)
        ang = cosT[:]
        turn = scratch[:, 2048:2560]
        red = scratch[:, 2560:3072]
        inv_row = scratch[:, 3072:3200]
        inv_col = scratch[:, 3200:3201]
        lam_p = scratch[:, 3264:3264 + 2 * LAYERS * HD].rearrange("p (v l c) -> p v l c", v=2, l=LAYERS)
        lam_s = scratch[:, 3584:3584 + 2 * LAYERS]
        lam_e = scratch[:, 3600:3600 + 2 * LAYERS]
        mask_f = scratch[:, 3712:3840]
        neg_incl_f = scratch[:, 3840:3968]
        mask_sb_f = scratch[:, 3968:4096]
        sel_f = scratch[:, 4096:5120].rearrange("p (h c) -> p h c", h=8)
        level_f = scratch[:, 5120:5120 + len(HALVES) * HD].rearrange("p (i q) -> p i q", i=len(HALVES))
        N_CONSTS = 14 + 4

        block = ctx.enter_context(nc.Block())

        @block.sync
        def _(sp):
            for t in range(NB):
                sp.dma_start(x_tok[:, t], x_rows[:, t]).then_inc(x_in, 16)

            def load(half, slot, w, row, k, col):
                sp.wait_ge(w_split, 2 * half + slot + 1)
                sp.sem_inc(load_turn, 1)
                sp.dma_start(w_raw[:, slot, 0:k], w[:, ds(row, k), ds(col, P)]).then_inc(w_landed[slot], 16)

            def load_wf(l):
                sp.wait_ge(wf_split, l + 1)
                sp.sem_inc(load_turn, 1)
                sp.dma_start(wf_raw[:], w_in_t[:, ds(l * KD, KD), w_in.shape[2] - P:w_in.shape[2]]).then_inc(wf_landed, 16)

            with sp.Fori(0, LAYERS) as l:
                for p in range(PAIRS):
                    q_col = p * P if p < NDIFF else 3 * DIFF_W + (p - NDIFF) * P
                    for i in range(3):
                        n = 3 * p + i
                        if n == 2:
                            load_wf(l)
                        load(l * (U_LAYER // 2) + n // 2, n % 2, w_in_t, l * KD, KD, q_col + i * DIFF_W)
                with sp.Fori(0, KD // 2) as m:
                    for i in range(2):
                        load(l * (U_LAYER // 2) + U_OUT // 2 + m, i, w_out_t, l * KD, KD, m * 2 * P + i * P)
                for kind, c, u in FFN_ORDER:
                    first, n = FF1_CHUNKS[c]
                    half = l * (U_LAYER // 2) + u // 2
                    if kind == "gu":
                        with sp.Fori(0, n) as j:
                            load(half + j, 0, w_gate_t, l * KD, KD, j * P + first * P)
                            load(half + j, 1, w_up_t, l * KD, KD, j * P + first * P)
                    else:
                        with sp.Fori(0, KD // 2) as m:
                            for i in range(2):
                                load(half + m, i, w_down_t, l * FF1_TILES + first, n, m * 2 * P + i * P)
            def load_square(u, w):
                with sp.Fori(0, KD // 2) as m:
                    for i in range(2):
                        load(u // 2 + m, i, w, 0, KD, m * 2 * P + i * P)

            def load_mlp(mlp, u0):
                for kind, c, u in MLP_UNITS:
                    with sp.Fori(0, KD // 2) as m:
                        for i in range(2):
                            col = m * 2 * P + i * P
                            if kind == "up":
                                load((u0 + u) // 2 + m, i, w1_t, mlp * KD, KD, col + c * D)
                            else:
                                load((u0 + u) // 2 + m, i, w2_t, mlp * (FF2 // P) + c * 8, 8, col)

            with sp.Fori(0, PAIRS // 2) as pp:
                for par in range(2):
                    for i in range(3):
                        u = 3 * par + i
                        load(U_SB // 2 + 3 * pp + u // 2, u % 2, sb_qkv_t, 0, KD, pp * 2 * P + par * P + i * D)
            load_square(U_SBO, sb_o_t)
            load_mlp(0, U_M1)
            with sp.Fori(0, KD) as i:
                for n, which in enumerate((1, 0, 2, 3)):
                    load(U_HG // 2 + 2 * i + n // 2, n % 2, hg_in_t, 0, KD, i * P + which * D)
            load_square(U_HGO, hg_o_t)
            load_mlp(1, U_M2)
            for first, n in OUT_PARTS:
                sp.wait_ge(out_ready, first + n)
                c = slice(first * P, (first + n) * P)
                sp.dma_start(out_rows[:, :, c], x_tok[:, :, c]).then_inc(out_stored, 16)
            sp.wait_ge(out_stored, 16 * len(OUT_PARTS))

        @block.gpsimd
        def _(pool):
            steps = Steps(pool, pool_step)
            steps(nc.gpsimd.memset(ident[:], 0.0))
            steps(nc.gpsimd.memset(rotT[:], 0.0))
            steps(nc.gpsimd.memset(mask_f, 0.0))
            steps(nc.gpsimd.memset(sel_f, 0.0))
            steps(nc.gpsimd.memset(neg_incl_f, -1.0))
            steps(nc.gpsimd.memset(mask_sb_f, NEG))
            steps(nc.gpsimd.memset(before01[:], 1.0))
            steps(nc.gpsimd.memset(level_f, 1.0))
            steps.wait()
            nc.gpsimd.affine_select(out=ident[:], in_=ident[:], compare_op=ALU.not_equal, fill=1.0, base=0,
                                    pattern=[[-1, P]], channel_multiplier=1).then_inc(pool_consts, 1)
            nc.gpsimd.affine_select(out=mask_f, in_=mask_f, compare_op=ALU.is_ge, fill=NEG, base=0,
                                    pattern=[[-1, P]], channel_multiplier=1).then_inc(pool_consts, 1)
            heads = rotT[:].rearrange("p (b c) -> p b c", b=2)
            lower, upper = heads[:, :, 0:ROT_HALF], heads[:, :, ROT_HALF:2 * ROT_HALF]
            nc.gpsimd.affine_select(out=lower, in_=lower, compare_op=ALU.not_equal, fill=-1.0, base=-ROT_HALF,
                                    pattern=[[-HD, 2], [-1, ROT_HALF]], channel_multiplier=1).then_inc(pool_consts, 1)
            nc.gpsimd.affine_select(out=upper, in_=upper, compare_op=ALU.not_equal, fill=1.0, base=0,
                                    pattern=[[-HD, 2], [-1, ROT_HALF]], channel_multiplier=1).then_inc(pool_consts, 1)
            nc.gpsimd.affine_select(out=sel_f, in_=sel_f, compare_op=ALU.not_equal, fill=1.0, base=-120,
                                    pattern=[[-1, 8], [0, P]], channel_multiplier=1).then_inc(pool_consts, 1)
            for t in (neg_incl_f, mask_sb_f):
                nc.gpsimd.affine_select(out=t, in_=t, compare_op=ALU.is_ge, fill=0.0, base=0,
                                        pattern=[[-1, P]], channel_multiplier=1).then_inc(pool_consts, 1)
            nc.gpsimd.affine_select(out=before01[:], in_=before01[:], compare_op=ALU.is_ge, fill=0.0, base=-1,
                                    pattern=[[1, P]], channel_multiplier=-1).then_inc(pool_consts, 1)
            for i, h in enumerate(HALVES):
                m = level_f[:, i].rearrange("p (n j) -> p n j", j=h)
                steps(nc.gpsimd.affine_select(out=m, in_=m, compare_op=ALU.is_ge, fill=0.0, base=0,
                                              pattern=[[-2 * h, HD // h], [0, h]], channel_multiplier=1))
            steps.wait()
            for i, h in enumerate(HALVES):
                m = level_f[:, i].rearrange("p (n j) -> p n j", j=h)
                nc.gpsimd.affine_select(out=m, in_=m, compare_op=ALU.is_ge, fill=0.0, base=h - 1,
                                        pattern=[[2 * h, HD // h], [0, h]], channel_multiplier=-1).then_inc(pool_consts, 1)
            pool.wait_ge(pool_consts, 8 + len(HALVES))

            def split(half, slot, k):
                pool.wait_ge(w_landed[slot], 16 * half + 16)
                pool.wait_ge(unit_done, 2 * half + slot + 1)
                pool.sem_inc(split_turn, 1)
                steps(nc.gpsimd.tensor_scalar(w_hi[:, slot, 0:k], w_raw[:, slot, 0:k], 1.0, 1.0, ALU.mult, ALU.mult))
                steps.wait()
                nc.gpsimd.tensor_tensor(w_lo[:, slot, 0:k], w_raw[:, slot, 0:k], w_hi[:, slot, 0:k].bitcast(F32),
                                        ALU.subtract).then_inc(w_split, 1)

            def split_units(first_half, halves, k):
                if halves == 1:
                    split(first_half, 0, k)
                    split(first_half, 1, k)
                    return
                with pool.Fori(0, halves) as i:
                    steps.enter(i, 2)
                    split(first_half + i, 0, k)
                    split(first_half + i, 1, k)
                    steps.leave(halves)

            def scale_y(l, si):
                for j in range(KD):
                    if j == 0:
                        pool.wait_ge(rstd_ready, l * 4 + si + 1)
                    nc.gpsimd.tensor_tensor(yT[:, j], yT[:, j], rstd[:], ALU.mult).then_inc(y_scaled, 1)

            pool.sem_inc(w_split, 2)
            pool.sem_inc(wf_split, 1)
            for dst, src in ((ident_r, ident[:]), (mask_r, mask_f), (sel_r, sel_f), (neg_incl_r, neg_incl_f),
                             (mask_sb_r, mask_sb_f)):
                nc.gpsimd.tensor_scalar(dst[:], src, 1.0, 1.0, ALU.mult, ALU.mult)
            split_units(0, 1, 8)
            for b in range(NB):
                nc.gpsimd.tensor_scalar(level_mask[:, :, b * HD:b * HD + HD], level_f, 1.0, 1.0, ALU.mult, ALU.mult)
                nc.gpsimd.tensor_scalar(same_mask[:, b * P:b * P + P], ident[:], 1.0, 1.0, ALU.mult, ALU.mult)
            with pool.Fori(0, LAYERS) as l:
                steps.enter(l, 1 + U_LAYER)
                pool.wait_ge(wf_landed, 16 * l + 16)
                pool.wait_ge(wf_done, l + 1)
                pool.sem_inc(split_turn, 1)
                steps(nc.gpsimd.tensor_scalar(wf_hi, wf_raw[:], 1.0, 1.0, ALU.mult, ALU.mult))
                steps.wait()
                nc.gpsimd.tensor_tensor(wf_lo, wf_raw[:], wf_hi.bitcast(F32), ALU.subtract).then_inc(wf_split, 1)
                half = l * (U_LAYER // 2)
                split_units(half + 1, U_GU0 // 2, 8)
                scale_y(l, 1)
                split_units(half + 1 + U_GU0 // 2, (U_D2 - U_GU0) // 2 - 1, 8)
                split_units(half + U_D2 // 2, KD // 2, FF1_CHUNKS[2][1])
                split_units(half + U_LAYER // 2, 1, 8)
                scale_y(l, 3)
                steps.leave(LAYERS)
            split_units(U2 // 2 + 1, (U_LAST - U2) // 2 - 1, 8)

        @block.tensor
        def _(pe):
            pe.sem_inc(unit_done, 2)
            pe.sem_inc(wf_done, 1)

            def products(bank, hi, lo, w_hi_, w_lo_, k_tiles, done, before=None, after=None):
                ops = []
                for k in range(k_tiles):
                    for i, (w, r) in enumerate(((w_hi_, hi), (w_hi_, lo), (w_lo_, hi))):
                        def issue(k=k, i=i, w=w, r=r):
                            if i == 0 and before is not None:
                                before(k)
                            mm = pe.matmul(bank[:], w[:, k], r[:, k], start=(k == 0 and i == 0),
                                           stop=(k == k_tiles - 1 and i == 2))
                            if k == k_tiles - 1 and i == 2:
                                mm.then_inc(done, 1)
                            if i == 2 and after is not None:
                                after(k)
                        ops.append(issue)
                return ops

            def sum_pair(n, q):
                pe.wait_ge(pair_added, n + q + 1)
                last = q == KD // 2 - 1
                pe.matmul(aux[:], ones[:, 0:P], pair_sum[q % 2], start=(q == 0),
                          stop=last).then_inc(aux_done if last else square_summed, 1)

            def unit(half, slot, hi, lo, k_tiles=8, ready=None, base=0, fresh=False, squares=None):
                def before(k):
                    if k == 0:
                        pe.wait_ge(w_split, 2 * half + slot + 3)
                        if not fresh:
                            pe.wait_ge(evacuated[slot], half)
                    if ready is not None:
                        pe.wait_ge(ready, base + k + 1)

                def after(k):
                    if k % 2:
                        sum_pair(squares, k // 2)
                return products(acc[slot], hi, lo, w_hi[:, slot], w_lo[:, slot], k_tiles, unit_done, before,
                                None if squares is None else after)

            def early_output(half, ready, base):
                a, b = (unit(half, i, mid_hi[:, 0], mid_lo[:, 0], ready=ready, base=base) for i in range(2))
                n = 3 * (KD - 1)
                return a[:n] + b[:EARLY], a[n:] + b[EARLY:]

            def side_by_side(half, base, n):
                both = [unit(half, i, h_hi, h_lo, ready=h_ready, base=base, fresh=True) for i in range(2)]
                for k in range(KD + LAG):
                    if k in (2, 4, 6, KD - 1):
                        sum_pair(n * (KD // 2), (k - 1) // 2)
                    for ops, at in zip(both, (k, k - LAG)):
                        if 0 <= at < KD:
                            run(ops[3 * at:3 * at + 3])

            def share(work, k, n):
                run(work[k * len(work) // n:(k + 1) * len(work) // n])

            def run(ops):
                for op in ops:
                    op()

            def sum_squares(added, a):
                pe.wait_ge(square_added, added + KD)
                pe.wait_ge(aux_free, a)
                pe.matmul(aux[:], ones[:, 0:P], square_sum, start=True, stop=True).then_inc(aux_done, 1)

            pe.wait_ge(pool_consts, 1)
            pe.wait_ge(x_in, 16 * NB)
            for j in range(KD):
                if j >= 2:
                    pe.wait_ge(x_ready, j - 1)
                for t in range(NB):
                    mm = pe.transpose(tp[j % 2][:, t * P:t * P + P], x_tok[:, t, j * P:j * P + P], ident[:])
                mm.then_inc(pre_pe, 1)
            pe.wait_ge(consts_in, 16 * N_CONSTS)
            pe.transpose(sc[0][:, 0:G_ROWS], grow[0:G_ROWS, :], ident[0:G_ROWS, 0:G_ROWS]).then_inc(pre_pe, 1)
            pe.wait_ge(vec_consts, 3)
            pe.matmul(sc[1][:, 0:1], inv_row[0:1, :], ones[0:1, 0:1], start=True, stop=True).then_inc(pre_pe, 1)

            with pe.Fori(0, LAYERS) as l:
                A = l * A_LAYER
                half0 = l * (U_LAYER // 2)

                def score(p, s):
                    t, m = s // 2, s % 2
                    bank, n = sc[s % 2], (t + 1) * P
                    if s == 0:
                        if p == 0:
                            pe.wait_ge(f_taken, l + 1)
                        if p < NDIFF:
                            pe.wait_ge(qk_ready, l * 2 * NDIFF + 2 * p + 2)
                        else:
                            for u in (3 * p, 3 * p + 1):
                                pe.wait_ge(evacuated[u % 2], half0 + u // 2 + 1)
                            if p == NDIFF:
                                pe.wait_ge(decay_ready, l + 1)
                    if p * 8 + s >= 2:
                        pe.wait_ge(exp_done, l * 64 + p * 8 + s - 1)
                    r = slice(HD * m, HD * m + HD)
                    pe.matmul(bank[:, 0:n], qT[p % 2][r, t * P:t * P + P], kT[p % 2][r, 0:n], start=True, stop=False)
                    if p >= NDIFF:
                        h = 2 * (p - NDIFF) + m
                        for i in range(2):
                            pe.matmul(bank[:, 0:n], sel_r[96:128, h, :], decay_r[96:128, i, 0:n], start=False, stop=False)
                    pe.matmul(bank[:, t * P:n], ident_r[:], mask_r[:], start=False, stop=True).then_inc(score_done, 1)

                def transpose_p(p, i):
                    ti = T_BASE[p] + i
                    t = i if p < NDIFF else i // 2
                    src = prob[(2 * i) % 4] if p < NDIFF else prob[i % 4]
                    pe.wait_ge(p_ready, l * T_BASE[PAIRS] + ti + 1)
                    if ti >= 2:
                        pe.wait_ge(t_taken, l * T_BASE[PAIRS] + ti - 1)
                    for j in range(t + 1):
                        mm = pe.transpose(tp[ti % 2][:, j * P:j * P + P], src[:, j * P:j * P + P], ident[:])
                    mm.then_inc(t_done, 1)

                def pv(p, i):
                    ti = T_BASE[p] + i
                    t = i if p < NDIFF else i // 2
                    r = slice(0, P) if p < NDIFF else slice(HD * (i % 2), HD * (i % 2) + HD)
                    if i == 0:
                        pe.wait_ge(aux_free, A + AUX[("v", p)] + 1)
                        if p >= 1:
                            pe.wait_ge(po_taken, l * PAIRS + p)
                    pe.wait_ge(t_taken, l * T_BASE[PAIRS] + ti + 1)
                    for j in range(t + 1):
                        mm = pe.matmul(po[r, t * P:t * P + P], vtok[:, j, r], probT[ti % 2][:, j * P:j * P + P],
                                       start=(j == 0), stop=(j == t))
                    mm.then_inc(pv_done, 1)

                def use_aux(name):
                    if AUX[name]:
                        pe.wait_ge(aux_free, A + AUX[name])

                for p in range(-1, PAIRS):
                    work = []
                    if p + 1 < PAIRS:
                        if p == -1:
                            side_by_side(half0, l * 16, 2 * l)
                        for u in range(max(3 * (p + 1), 2), 3 * (p + 1) + 3):
                            work += unit(half0 + u // 2, u % 2, h_hi, h_lo)
                        if p == -1:
                            work += products(sc[0], h_hi, h_lo, wf_hi, wf_lo, 8, wf_done,
                                             lambda k: pe.wait_ge(wf_split, l + 2) if k == 0 else None)
                    else:
                        work, rest = early_output(half0 + U_OUT // 2, o_ready, l * PAIRS)
                    for k in range(SLOTS):
                        if p >= 0 and k < 8:
                            score(p, k)
                        share(work, k, SLOTS if p + 1 < PAIRS else SLOTS + TAIL)
                        if p >= 0 and k == 1:
                            use_aux(("v", p))
                            pe.wait_ge(evacuated[(3 * p + 2) % 2], half0 + (3 * p + 2) // 2 + 1)
                            for j in range(NB):
                                mm = pe.transpose(aux[:, j * P:j * P + P], vraw[:, j * P:j * P + P], ident[:])
                            mm.then_inc(aux_done, 1)
                        if k == 4 and 0 <= p - 1 < NDIFF:
                            use_aux(("o_norm", p - 1))
                            pe.wait_ge(o_square, l * NDIFF + p)
                            pe.matmul(aux[:], ones[:, 0:P], osq, start=True, stop=True).then_inc(aux_done, 1)
                        for slot, name, i in ((6, "rot_q", 0), (9, "rot_k", 1)):
                            if k == slot and p + 1 < NDIFF:
                                u = 3 * (p + 1) + i
                                use_aux((name, p + 1))
                                pe.wait_ge(evacuated[u % 2], half0 + u // 2 + 1)
                                pe.matmul(aux[:], rotT[:], raw, start=True, stop=True).then_inc(aux_done, 1)
                        if p >= 0 and p < NDIFF:
                            if k >= 3 and k % 2 == 1 and (k - 3) // 2 < 4:
                                transpose_p(p, (k - 3) // 2)
                            if k >= 4 and k % 2 == 0 and (k - 4) // 2 < 4:
                                pv(p, (k - 4) // 2)
                        elif p >= NDIFF:
                            if 2 <= k < 10:
                                transpose_p(p, k - 2)
                            if 3 <= k < 11:
                                pv(p, k - 3)
                for k in range(SLOTS, SLOTS + TAIL):
                    share(work, k, SLOTS + TAIL)
                run(rest)
                with pe.Fori(1, KD // 2) as m:
                    for i in range(2):
                        run(unit(half0 + U_OUT // 2 + m, i, mid_hi[:, 0], mid_lo[:, 0]))
                sum_squares(added_base(2 * l), A + AUX["norm_att_post"])

                def gate_up(half):
                    run(unit(half, 0, h_hi, h_lo))
                    run(unit(half, 1, h_hi, h_lo))

                for kind, c, u in FFN_ORDER:
                    first, n = FF1_CHUNKS[c]
                    half = half0 + u // 2
                    if kind == "gu":
                        if c == 0:
                            side_by_side(half, l * 16 + 8, 2 * l + 1)
                            with pe.Fori(1, n) as j:
                                gate_up(half + j)
                        else:
                            with pe.Fori(0, n) as j:
                                gate_up(half + j)
                    else:
                        with pe.Fori(0, KD // 2) as m:
                            pe.wait_ge(mid_ready, l * FF1_TILES + first + n)
                            for i in range(2):
                                run(unit(half + m, i, mid_hi[:, c % 2], mid_lo[:, c % 2], n))
                sum_squares(added_base(2 * l + 1), A + AUX["norm_ffn_post"])

            def sb_pair(pp, par, current=True, following=True, previous=True, work=()):
                p = 2 * pp + par
                aux_n = A_SB + 3 + 3 * p
                if following:
                    work = []
                    for u in range(3 * (par + 1), 3 * (par + 1) + 3):
                        first = u == 0
                        work += unit(U_SB // 2 + 3 * pp + u // 2, u % 2, h_hi, h_lo, ready=h_ready if first else None,
                                     base=block2_norm(0)[0], squares=2 * LAYERS * (KD // 2) if first else None)

                def scores(m):
                    if m == 0:
                        pe.wait_ge(sb_qk_ready, 2 * p + 2)
                    pe.wait_ge(w_ready, 2 * p + m + 1)
                    r = slice(HD * m, HD * m + HD)
                    for bank, blocks, _, _ in Z_PARTS:
                        for b in blocks:
                            at = Z_BANK[b][1]
                            mm = pe.matmul(z[bank][:, at:at + Z_N[b]], skT[par % 2][r, b * P:b * P + P],
                                           sqT[par % 2][r, b * P:S], start=(b < 3), stop=True, skip_group_check=True)
                        mm.then_inc(z_done, 1)

                def log_weights(m):
                    for i, (bank, blocks, _, _) in enumerate(Z_PARTS):
                        pe.wait_ge(stay_ready, 6 * p + 3 * m + i + 1)
                        for b in blocks:
                            at = Z_BANK[b][1]
                            pe.matmul(z[bank][:, at:at + P], ident_r[:], mask_sb_r[:], start=False, stop=False,
                                      skip_group_check=True)
                            for c in range(b, NB):
                                lhs = neg_incl_r if c == b else neg_ones_r
                                for part_ in (stay_hi, stay_lo):
                                    mm = pe.matmul(z[bank][:, at + (c - b) * P:at + Z_N[b]], lhs[:],
                                                   part_[:, Z_AT[c]:Z_AT[c] + Z_N[c]], start=False,
                                                   stop=(c == NB - 1), skip_group_check=True)
                        mm.then_inc(logw_done, 1)

                def sb_pv(m, p_):
                    r = slice(HD * m, HD * m + HD)
                    pe.wait_ge(w_ready, 2 * p_ + m + 2)
                    if m == 0:
                        pe.wait_ge(aux_free, aux_n + 1)
                        pe.wait_ge(sb_o_taken, p_ + 1)
                    for b in range(NB):
                        mm = pe.matmul(po[r, b * P:S], vtok[:, b, r], sb_w[:, Z_AT[b]:Z_AT[b] + Z_N[b]],
                                       start=(b == 0), stop=(b == NB - 1), skip_group_check=True)
                    mm.then_inc(sb_pv_done, 1)

                for k in range(SLOTS):
                    if current:
                        if k in (0, 6):
                            scores(k // 6)
                        if k == 1 and previous:
                            last_pv(p - 1)
                        if k == 7:
                            sb_pv(0, p)
                        if k in (5, 11):
                            log_weights(k // 6)
                    share(work, k, SLOTS if following else SLOTS + TAIL)
                    if current and k == 2:
                        pe.wait_ge(aux_free, aux_n)
                        u = 3 * par + 2
                        pe.wait_ge(evacuated[u % 2], U_SB // 2 + 3 * pp + u // 2 + 1)
                        for j in range(NB):
                            mm = pe.transpose(aux[:, j * P:j * P + P], vraw[:, j * P:j * P + P], ident[:])
                        mm.then_inc(aux_done, 1)
                    for i, at in ((0, 6), (1, 10)):
                        if following and k == at:
                            pe.wait_ge(aux_free, aux_n + 1 + i)
                            pe.wait_ge(raw_square, 2 * p + 2 + i + 1)
                            pe.matmul(aux[:], head_ones[:], sb_sq, start=True, stop=True).then_inc(aux_done, 1)

            def last_pv(p_):
                pe.wait_ge(w_ready, 2 * p_ + 3)
                r = slice(HD, 2 * HD)
                for b in range(NB):
                    mm = pe.matmul(po[r, b * P:S], vtok[:, b, r], sb_w[:, Z_AT[b]:Z_AT[b] + Z_N[b]],
                                   start=(b == 0), stop=(b == NB - 1), skip_group_check=True)
                mm.then_inc(sb_pv_done, 1)

            z = [sc[0], sc[1], tp[0]]
            pe.sem_inc(sb_pv_done, 1)
            sb_pair(0, -1, current=False)
            sb_pair(0, 0, previous=False)
            sb_pair(0, 1)
            with pe.Fori(1, PAIRS // 2 - 1) as pp:
                sb_pair(pp, 0)
                sb_pair(pp, 1)
            sb_pair(PAIRS // 2 - 1, 0)
            work, rest = early_output(U_SBO // 2, sb_o_ready, 0)
            sb_pair(PAIRS // 2 - 1, 1, following=False, work=work)
            last_pv(PAIRS - 1)
            for k in range(SLOTS, SLOTS + TAIL):
                share(work, k, SLOTS + TAIL)

            def square_matrix(u, rest):
                run(rest)
                with pe.Fori(1, KD // 2) as m:
                    for i in range(2):
                        run(unit(u // 2 + m, i, mid_hi[:, 0], mid_lo[:, 0]))

            def result_back(j, half):
                pe.wait_ge(evacuated[j % 2], half + j // 2 + 1)
                if j >= 2:
                    pe.wait_ge(out_ready, j - 1)
                for t in range(NB):
                    mm = pe.transpose(tp[j % 2][:, t * P:t * P + P], xT[:, j, t * P:t * P + P], ident[:])
                mm.then_inc(pre_pe, 1)

            def mlp_products(i_mlp, u0, norm, a_n):
                for kind, c, u in MLP_UNITS:
                    half = (u0 + u) // 2
                    if kind == "up":
                        first = 0
                        if c == 0:
                            h_base, _, added = block2_norm(norm)
                            run(unit(half, 0, h_hi, h_lo, ready=h_ready, base=h_base))
                            ops = unit(half, 1, h_hi, h_lo)
                            run(ops[:3])
                            sum_squares(added, a_n)
                            run(ops[3:])
                            first = 1
                        with pe.Fori(first, KD // 2) as m:
                            for i in range(2):
                                run(unit(half + m, i, h_hi, h_lo))
                    elif i_mlp == 1 and c == 3:
                        for j in range(KD):
                            if j == 0:
                                pe.wait_ge(mid_ready, MID1 + (i_mlp + 1) * (FF2 // P))
                            run(unit(half + j // 2, j % 2, mid_hi[:, c % 2], mid_lo[:, c % 2]))
                            if j >= 1:
                                result_back(j - 1, half)
                        result_back(KD - 1, half)
                    else:
                        with pe.Fori(0, KD // 2) as m:
                            pe.wait_ge(mid_ready, MID1 + i_mlp * (FF2 // P) + 8 * c + 8)
                            for i in range(2):
                                run(unit(half + m, i, mid_hi[:, c % 2], mid_lo[:, c % 2]))

            square_matrix(U_SBO, rest)
            mlp_products(0, U_M1, 1, A_M1)

            def hg_head(pp, par, current=True, following=True, previous=True, first=False, work=()):
                i = 2 * pp + par
                half = U_HG // 2 + 2 * i
                if following:
                    work = []
                    for n in range(4):
                        work += unit(half + 2 + n // 2, n % 2, h_hi, h_lo, 8,
                                     ready=h_ready if par == -1 and n == 0 else None, base=block2_norm(2)[0])
                for k in range(HG_SLOTS):
                    if current and k == 0:
                        pe.wait_ge(hg_key_ready, i + 1)
                        pe.wait_ge(hg_query_ready, i + 1)
                        if not first:
                            pe.wait_ge(level_taken, 8 * i)
                        for b in range(NB):
                            c = slice(b * P, b * P + P)
                            mm = pe.matmul(sc[1][:, c], hk[par % 2][:, c], hq[par % 2][:, c], start=True, stop=True)
                        mm.then_inc(level_scored, 1)
                    if current and 3 <= k < 3 + len(HALVES):
                        lv = k - 3
                        h = HALVES[lv]
                        x = hx[lv % 3]
                        pe.wait_ge(level_mul, 7 * i + lv + 1)
                        if lv or not first:
                            pe.wait_ge(level_taken, 8 * i + lv)
                        for b in range(NB):
                            right = x[:, b * P:b * P + P].rearrange("p (n e j) -> p n e j", e=2, j=h)[:, :, 1]
                            mm = pe.matmul(sc[lv % 2][:, b * HD:b * HD + HD], x[:, b * P:b * P + P], right,
                                           start=True, stop=True)
                        mm.then_inc(level_scored, 1)
                    if current and k == 12:
                        pe.wait_ge(cross_mul, i + 1)
                        if not first:
                            pe.wait_ge(cross_taken, i)
                        pe.matmul(tp[0][:, 0:P], hx128[:, 0:P], hx128[:, P:2 * P], start=True, stop=True)
                        pe.matmul(tp[0][:, P:2 * P], hx128[:, 2 * P:3 * P], hx128[:, 3 * P:S], start=True, stop=True)
                        pe.matmul(tp[0][:, 2 * P:S], hx256[:, 0:P], hx256[:, 2 * P:S], start=True, stop=True)
                        pe.matmul(tp[1][:, 0:2 * P], hx256[:, P:2 * P], hx256[:, 2 * P:S], start=True,
                                  stop=True).then_inc(cross_scored, 1)
                    if current and k == 15:
                        pe.wait_ge(aux_free, a_hgv(i, first) + 1)
                        pe.wait_ge(level_taken, 8 * i + 8)
                        pe.wait_ge(cross_taken, i + 1)
                        if not first:
                            pe.wait_ge(hg_o_taken, i)
                        for b in range(NB):
                            pe.matmul(po[:, b * P:b * P + P], hvtok[:, b], hdiag[:, b * P:b * P + P], start=(b == 0),
                                      stop=False, skip_group_check=True)
                        for b, c, n, at in ((0, 1, P, 0), (2, 3, P, P), (0, 2, 2 * P, 2 * P), (1, 2, 2 * P, S)):
                            mm = pe.matmul(po[:, c * P:c * P + n], hvtok[:, b], hoff[:, at:at + n], start=False,
                                           stop=True, skip_group_check=True)
                        mm.then_inc(hg_pv_done, 1)
                    share(work, k, HG_SLOTS if following else HG_SLOTS + TAIL)
                    if par == -1 and k == 3:
                        sum_squares(block2_norm(2)[2], A_HG)
                    if current and k == 1:
                        pe.wait_ge(evacuated[0], half + 2)
                        pe.wait_ge(aux_free, a_hgv(i, first))
                        for j in range(NB):
                            mm = pe.transpose(aux[:, j * P:j * P + P], hvraw[:, j * P:j * P + P], ident[:])
                        mm.then_inc(aux_done, 1)
                    if current and previous and k == 2:
                        hg_norm(i - 1)

            def hg_norm(i, last=False):
                pe.wait_ge(hg_o_square, i + 1)
                pe.wait_ge(aux_free, a_hgv(i + 1) + (0 if last else 1))
                pe.matmul(aux[:], ones[:, 0:P], hosq, start=True, stop=True).then_inc(aux_done, 1)

            hg_head(0, -1, current=False)
            hg_head(0, 0, previous=False, first=True)
            hg_head(0, 1)
            with pe.Fori(1, KD // 2 - 1) as pp:
                hg_head(pp, 0)
                hg_head(pp, 1)
            hg_head(KD // 2 - 1, 0)
            work, rest = early_output(U_HGO // 2, hg_o_ready, 0)
            hg_head(KD // 2 - 1, 1, following=False, work=work)
            for k in range(HG_SLOTS, HG_SLOTS + TAIL // 2):
                share(work, k, HG_SLOTS + TAIL)
            hg_norm(KD - 1, last=True)
            for k in range(HG_SLOTS + TAIL // 2, HG_SLOTS + TAIL):
                share(work, k, HG_SLOTS + TAIL)
            square_matrix(U_HGO, rest)
            mlp_products(1, U_M2, 3, A_M2)

        @block.vector
        def _(v):
            steps = Steps(v, vec_step)
            TT, TS, STT, COPY = v.tensor_tensor, v.tensor_scalar, v.scalar_tensor_tensor, v.tensor_copy

            v.memset(lconst[:], 0.0).then_inc(vec_consts, 1)
            v.memset(ones[:], 1.0)
            v.memset(eps_col[:], EPS).then_inc(vec_consts, 1)
            steps(v.memset(inv_row[0:1, :], 0.0))
            steps.wait()
            by_head = inv_row[0:1, :].rearrange("p (b q) -> p b q", b=2)[:, :, 0:2 * ROT_HALF].rearrange(
                "p b (e d) -> p b e d", e=2)
            inv_freq = 1.0 / (np.float32(THETA) ** (np.arange(0, 2 * ROT_HALF, 2, dtype=np.float32) / np.float32(2 * ROT_HALF)))
            for d in range(ROT_HALF):
                last = v.memset(by_head[:, :, :, d], float(inv_freq[d]))
            last.then_inc(vec_consts, 1)
            for j in range(KD):
                v.wait_ge(pre_pe, j + 1)
                COPY(xT[:, j], tp[j % 2][:]).then_inc(x_ready, 1)
            v.wait_ge(pre_pe, KD + 1)
            COPY(gains[:], sc[0][:, 0:G_ROWS]).then_inc(gains_ready, 1)
            v.wait_ge(pre_pe, KD + 2)
            steps(COPY(inv_col, sc[1][:, 0:1]))
            v.wait_ge(gains_ready, 1)
            def add_square(n, added, j, i):
                v.wait_ge(square_ready, n + j + 1)
                v.wait_ge(square_added, added + j)
                TT(square_sum, square_sum, square[i], ALU.add).then_inc(square_added, 1)

            def low_part(hi_n, j, gain):
                v.wait_ge(h_hi_ready, hi_n + j + 1)
                STT(h_lo[:, ds(j, 1)], xT[:, ds(j, 1)], gain, h_hi[:, ds(j, 1)].bitcast(F32), ALU.mult,
                    ALU.subtract).then_inc(h_ready, 1)

            def add_pair(n, norm, j):
                v.wait_ge(square_ready, n + j + 1)
                if j > 3:
                    v.wait_ge(square_summed, 3 * norm + j // 2 - 1)
                TT(pair_sum[j // 2 % 2], square[0], square[1], ALU.add).then_inc(pair_added, 1)

            v.sem_inc(square_added, 2)
            for j in range(KD):
                low_part(0, j, gains[:, G_ATT_PRE + j:G_ATT_PRE + j + 1])
                if j % 2:
                    add_pair(0, 0, j)
            TS(neg_ones_r[:], ones[:, 0:P], -1.0, None, ALU.mult)
            steps(v.memset(head_ones[:], 0.0))
            steps.wait()
            for m in range(2):
                v.memset(head_ones[HD * m:HD * m + HD, HD * m:HD * m + HD], 1.0)
            TS(sb_gain[:, 0:1], gains[:, G_SBQ:G_SBQ + 1], HD ** -0.5, None, ALU.mult)
            COPY(sb_gain[:, 1:2], gains[:, G_SBK:G_SBK + 1])
            v.wait_ge(consts_in, 16 * N_CONSTS)
            steps(TT(lam_p, lam_in[:, 0:4:2], lam_in[:, 1:4:2], ALU.mult))
            steps.wait()
            v.reduce_sum(lam_s.rearrange("p (v l) -> p v l", v=2), lam_p, AX_X).then_inc(vec_consts, 1)
            big = 1.5 * 2.0 ** 23
            c1, c2 = 6.28125, 0.0019350051879882812
            c3 = 2 * math.pi - c1 - c2
            pi_in = float(np.nextafter(np.float32(math.pi), np.float32(0)))
            steps(TS(ang, pos_i, inv_col, None, ALU.mult))
            steps.wait()
            steps(TS(turn, ang, 1 / (2 * math.pi), None, ALU.mult))
            steps.wait()
            steps(TS(turn, turn, big, None, ALU.add))
            steps.wait()
            steps(TS(turn, turn, -big, None, ALU.add))
            steps.wait()
            steps(STT(red, turn, -c1, ang, ALU.mult, ALU.add))
            steps.wait()
            steps(STT(red, turn, -c2, red, ALU.mult, ALU.add))
            steps.wait()
            steps(STT(red, turn, -c3, red, ALU.mult, ALU.add))
            steps.wait()
            TS(red, red, -pi_in, pi_in, ALU.max, ALU.min).then_inc(vec_consts, 1)
            v.wait_ge(act_consts, 1)
            for l in range(LAYERS):
                steps(TT(lconst[:, l, 0:1], lam_e[:, LAYERS + l:LAYERS + l + 1], lam_e[:, l:l + 1], ALU.subtract))
                steps(TS(lconst[:, l, 1:2], gains[:, G_DIFF + l:G_DIFF + l + 1], 1.0 - LAM_INIT[l], None, ALU.mult))
            steps.wait()
            for l in range(LAYERS):
                steps(TS(lconst[:, l, 0:1], lconst[:, l, 0:1], -LAM_INIT[l], None, ALU.add))
            v.wait_ge(act_consts, 4)
            steps(TS(cosT[:], cosT[:], -2.0, 1.0, ALU.mult, ALU.add))
            steps.wait()

            def take(half, slot):
                v.wait_ge(unit_done, 2 * half + slot + 3)

            with v.Fori(0, LAYERS) as l:
                steps.enter(l, VEC_STEPS_LAYER)
                A = l * A_LAYER
                half0 = l * (U_LAYER // 2)
                v.wait_ge(h_ready, l * 16 + KD)
                COPY(layer_gain[:, 0:3], gains[:, G_ATT_POST:G_ATT_POST + 6 * KD].rearrange(
                    "p (g l j) -> p g l j", g=3, l=LAYERS)[:, :, ds(l, 1)])
                COPY(layer_gain[:, 3], gains[:, ds(l * KD + KD, KD)])
                COPY(lcur[:], lconst[:, ds(l, 1)]).then_inc(layer_const, 1)
                v.wait_ge(layer_const, l + 1)
                def probabilities(p, i):
                    t = i if p < NDIFF else i // 2
                    n = (t + 1) * P
                    if p < NDIFF:
                        s, a = 2 * i, (2 * i) % 4
                        v.wait_ge(exp_done, l * 64 + p * 8 + s + 2)
                        steps(v.reciprocal(stat[:, 8 + a:10 + a], stat[:, 4 + a:6 + a]))
                        steps.wait()
                        steps(TT(stat[:, 12:13], stat[:, 9 + a:10 + a], lcur[:, 0:1], ALU.mult))
                        steps(TS(prob[a][:, 0:n], prob[a][:, 0:n], stat[:, 8 + a:9 + a], None, ALU.mult))
                        steps.wait()
                        STT(prob[a][:, 0:n], prob[a + 1][:, 0:n], stat[:, 12:13], prob[a][:, 0:n],
                            ALU.mult, ALU.add).then_inc(p_ready, 1)
                    else:
                        a = i % 4
                        v.wait_ge(exp_done, l * 64 + p * 8 + i + 1)
                        steps(v.reciprocal(stat[:, 8 + a:9 + a], stat[:, 4 + a:5 + a]))
                        steps.wait()
                        TS(prob[a][:, 0:n], prob[a][:, 0:n], stat[:, 8 + a:9 + a], None, ALU.mult).then_inc(p_ready, 1)

                def take_qk(p, i):
                    u = 3 * p + i
                    take(half0 + u // 2, u % 2)
                    dst = raw if p < NDIFF else (qT, kT)[i][p % 2]
                    STT(dst, acc[u % 2][:], (HD ** -0.5, 1.0)[i], rstd[:], ALU.mult, ALU.mult).then_inc(evacuated[u % 2], 1)

                def rotate(p, i):
                    a = AUX[(("rot_q", "rot_k")[i], p)]
                    v.wait_ge(aux_done, A + a + 1)
                    TT(rsin, aux[:], sinT[:], ALU.mult).then_inc(aux_free, 1)
                    steps(TT(rcos, raw, cosT[:], ALU.mult))
                    steps.wait()
                    v.wait_ge(aux_free, A + a + 1)
                    TT((qT, kT)[i][p % 2], rcos, rsin, ALU.add).then_inc(qk_ready, 1)

                def low_output(p):
                    v.wait_ge(o_hi_ready, l * PAIRS + p + 1)
                    src = onrm if p < NDIFF else orow
                    TT(mid_lo[:, 0, p], src, mid_hi[:, 0, p].bitcast(F32), ALU.subtract).then_inc(o_ready, 1)

                for p in range(-1, PAIRS):
                    for k in range(SLOTS):
                        if k == 0 and p >= 0:
                            u = 3 * p + 2
                            take(half0 + u // 2, u % 2)
                            TT(vraw, acc[u % 2][:], rstd[:], ALU.mult).then_inc(evacuated[u % 2], 1)
                        if p >= 0 and k < 8:
                            n = (k // 2 + 1) * P
                            v.wait_ge(score_done, l * 64 + p * 8 + k + 1)
                            v.tensor_reduce(stat[:, k % 4:k % 4 + 1], sc[k % 2][:, 0:n], AX_X, ALU.max,
                                            negate=True).then_inc(max_done, 1)
                        if p >= 0 and p < NDIFF and k >= 2 and k % 2 == 0 and k <= 8:
                            probabilities(p, (k - 2) // 2)
                        if p >= NDIFF and 1 <= k <= 8:
                            probabilities(p, k - 1)
                        if k == 4 and p + 1 < PAIRS:
                            if p == -1:
                                v.wait_ge(rstd_ready, l * 4 + 1)
                            take_qk(p + 1, 0)
                        if k == 8 and p + 1 < PAIRS:
                            take_qk(p + 1, 1)
                        if p + 1 < NDIFF and k == 7:
                            rotate(p + 1, 0)
                        if p + 1 < NDIFF and k == 10:
                            rotate(p + 1, 1)
                        if k == 2 and p - 1 >= NDIFF:
                            low_output(p - 1)
                        if k == 6 and 0 <= p - 1 < NDIFF:
                            v.wait_ge(o_rstd, l * NDIFF + p)
                            STT(onrm, orow, lcur[:, 1:2], ologs, ALU.mult, ALU.mult).then_inc(o_normed, 1)
                        if k == 8 and 0 <= p - 1 < NDIFF:
                            low_output(p - 1)
                        if p == 0 and k == 9:
                            v.wait_ge(f_log, l + 1)
                            f = slice(96, P)
                            steps(STT(raw_f[f], raw_f[f], 0.0, ologs_f[f], ALU.min, ALU.subtract))
                            steps.wait()
                            steps(v.tensor_tensor_scan(negc[f], ones[f], raw_f[f], 0.0, ALU.mult, ALU.subtract))
                            steps.wait()
                            steps(COPY(decay_r[f, 0], negc[f]))
                            steps.wait()
                            TT(decay_r[f, 1], negc[f], decay_r[f, 0].bitcast(F32), ALU.subtract).then_inc(decay_ready, 1)
                        if k == 11 and p >= 0:
                            v.wait_ge(pv_done, l * T_BASE[PAIRS] + T_BASE[p + 1])
                            COPY(orow, po[:]).then_inc(po_taken, 1)
                    if p == -1:
                        v.wait_ge(wf_done, l + 2)
                        TT(raw_f[96:P], sc[0][96:P], rstd[96:P], ALU.mult).then_inc(f_taken, 1)
                        v.wait_ge(f_taken, l + 1)
                        TS(raw_f[96:P], raw_f[96:P], lcur[96:P, 2:3], None, ALU.add).then_inc(f_ready, 1)
                low_output(PAIRS - 1)

                def update_x(g, x_n, scaled, n, norm):
                    for j in range(KD + 1):
                        if j < KD:
                            v.wait_ge(y_scaled, scaled + j + 1)
                            STT(xT[:, j], yT[:, j], layer_gain[:, g, j:j + 1], xT[:, j], ALU.mult,
                                ALU.add).then_inc(x_ready, 1)
                        if j >= 1:
                            v.wait_ge(x_ready, x_n + j)
                            low_part(x_n, j - 1, layer_gain[:, g + 1, j - 1:j])
                            if j % 2 == 0:
                                add_pair(n, norm, j - 1)

                def take_y(half, slot, j, first):
                    take(half, slot)
                    dst = yT[:, ds(j, 1)]
                    if first:
                        COPY(dst, acc[slot][:]).then_inc(evacuated[slot], 1)
                    else:
                        TT(dst, dst, acc[slot][:], ALU.add).then_inc(evacuated[slot], 1)

                steps(v.memset(square_sum, 0.0))
                with v.Fori(0, KD // 2) as m:
                    steps.wait()
                    for i in range(2):
                        take_y(half0 + U_OUT // 2 + m, i, 2 * m + i, True)
                        add_square(l * 32 + 8, added_base(2 * l), 2 * m + i, i)
                update_x(0, l * 16 + 8, l * 16, l * 32 + 16, 2 * l + 1)
                for kind, c, u in FFN_ORDER:
                    first, n = FF1_CHUNKS[c]
                    half = half0 + u // 2
                    if kind == "gu":
                        with v.Fori(0, n) as j:
                            g = l * FF1_TILES + first + j
                            v.wait_ge(rstd_ready, l * 4 + 3)
                            take(half + j, 0)
                            TT(gate, acc[0][:], rstd[:], ALU.mult).then_inc(evacuated[0], 1)
                            v.wait_ge(gate_log, g + 1)
                            STT(gate_t, gate, 0.0, gate_t2, ALU.min, ALU.subtract).then_inc(gate_ls, 1)
                            take(half + j, 1)
                            TT(up, acc[1][:], rstd[:], ALU.mult).then_inc(evacuated[1], 1)
                            v.wait_ge(evacuated[1], half + j + 1)
                            TT(up, gate, up, ALU.mult).then_inc(gu_done, 1)
                            v.wait_ge(gate_sig, g + 1)
                            v.wait_ge(gu_done, g + 1)
                            TT(hid, up, gate_t2, ALU.mult).then_inc(hid_ready, 1)
                            v.wait_ge(mid_hi_ready, g + 1)
                            TT(mid_lo[:, c % 2, ds(j, 1)], hid, mid_hi[:, c % 2, ds(j, 1)].bitcast(F32),
                               ALU.subtract).then_inc(mid_ready, 1)
                    else:
                        if c == 2:
                            steps(v.memset(square_sum, 0.0))
                        with v.Fori(0, KD // 2) as m:
                            if c == 2:
                                steps.wait()
                            for i in range(2):
                                take_y(half + m, i, 2 * m + i, c == 0)
                                if c == 2:
                                    add_square(l * 32 + 24, added_base(2 * l + 1), 2 * m + i, i)
                update_x(2, l * 16 + 16, l * 16 + 8, l * 32 + 32, 2 * l + 2)
                steps.leave(LAYERS)

            def sb_pair(pp, par, current=True, following=True, previous=True):
                p = 2 * pp + par
                half = U_SB // 2 + 3 * pp
                aux_n = A_SB + 3 + 3 * p

                def stay(m):
                    for i, (bank, blocks, at, n) in enumerate(Z_PARTS):
                        c = slice(at, at + n)
                        v.wait_ge(z_log, 6 * p + 3 * m + i + 1)
                        steps(STT(sb_stay[:, c], z[bank][:, 0:n], 0.0, sb_log[:, c], ALU.max, ALU.add))
                        steps.wait()
                        for b in blocks:
                            d = sb_stay[:, Z_AT[b]:Z_AT[b] + P]
                            steps(TT(d, d, before01[:], ALU.mult))
                        steps.wait()
                        steps(COPY(stay_hi[:, c], sb_stay[:, c]))
                        steps.wait()
                        TT(stay_lo[:, c], sb_stay[:, c], stay_hi[:, c].bitcast(F32), ALU.subtract).then_inc(stay_ready, 1)

                def take_raw(i):
                    u = 3 * (par + 1) + i
                    if par >= 0 or i:
                        v.wait_ge(sb_qk_ready, 2 * p + 2 + i)
                    take(half + u // 2, u % 2)
                    TT(raw, acc[u % 2][:], rstd[:], ALU.mult).then_inc(evacuated[u % 2], 1)

                def normed(i):
                    v.wait_ge(raw_rstd, 2 * p + 2 + i + 1)
                    dst = (sqT, skT)[i][(par + 1) % 2]
                    STT(dst, raw, sb_gain[:, i:i + 1], sb_logs, ALU.mult, ALU.mult).then_inc(sb_qk_ready, 1)

                for k in range(SLOTS):
                    if current and k == 0:
                        u = 3 * par + 2
                        take(half + u // 2, u % 2)
                        TT(vraw, acc[u % 2][:], rstd[:], ALU.mult).then_inc(evacuated[u % 2], 1)
                        stay(0)
                    if current and k == 6:
                        stay(1)
                    if current and previous and k == 3:
                        sb_output(p - 1)
                    if following and k == 4:
                        if par == -1:
                            v.wait_ge(rstd_ready, 4 * LAYERS + 1)
                        take_raw(0)
                    if following and k == 7:
                        normed(0)
                    if following and k == 8:
                        take_raw(1)
                    if following and k == 11:
                        normed(1)

            def sb_output(p):
                v.wait_ge(sb_pv_done, 2 * p + 3)
                COPY(sb_orow, po[:]).then_inc(sb_o_taken, 1)
                v.wait_ge(sb_o_hi, p + 1)
                TT(mid_lo[:, 0, ds(p, 1)], sb_orow, mid_hi[:, 0, ds(p, 1)].bitcast(F32), ALU.subtract).then_inc(sb_o_ready, 1)

            z = [sc[0], sc[1], tp[0]]
            v.sem_inc(sb_o_taken, 1)
            sb_pair(0, -1, current=False)
            sb_pair(0, 0, previous=False)
            sb_pair(0, 1)
            with v.Fori(1, PAIRS // 2 - 1) as pp:
                steps.enter(pp - 1, SB_STEPS)
                sb_pair(pp, 0)
                sb_pair(pp, 1)
                steps.leave(PAIRS // 2 - 2)
            sb_pair(PAIRS // 2 - 1, 0)
            sb_pair(PAIRS // 2 - 1, 1, following=False)
            sb_output(PAIRS - 1)

            def add_x(half, slot, j):
                take(half, slot)
                v.wait_ge(evacuated[slot], half)
                dst = xT[:, ds(j, 1)]
                TT(dst, dst, acc[slot][:], ALU.add).then_inc(evacuated[slot], 1)

            def add_matrix(u, norm=None):
                if norm is not None:
                    steps(v.memset(square_sum, 0.0))
                with v.Fori(0, KD // 2) as m:
                    if norm is not None:
                        steps.wait()
                    for i in range(2):
                        j = 2 * m + i
                        add_x(u // 2 + m, i, j)
                        if norm is not None:
                            h_base, squares, added = block2_norm(norm)
                            low_part(h_base, j, gains[:, ds(j + (G_B2 + norm * KD), 1)])
                            add_square(squares, added, j, i)

            def mlp(i_mlp, u0, i_norm):
                for kind, c, u in MLP_UNITS:
                    half = (u0 + u) // 2
                    if kind == "down":
                        add_matrix(u0 + u, norm=2 if i_mlp == 0 and c == 3 else None)
                        continue
                    with v.Fori(0, KD // 2) as m:
                        for i in range(2):
                            g = MID1 + i_mlp * (FF2 // P) + 8 * c + 2 * m + i
                            v.wait_ge(rstd_ready, 4 * LAYERS + i_norm + 1)
                            take(half + m, i)
                            TT(gate, acc[i][:], rstd[:], ALU.mult).then_inc(evacuated[i], 1)
                            v.wait_ge(evacuated[i], half + m + 1)
                            STT(hid, gate, 0.0, gate, ALU.max, ALU.mult).then_inc(hid_ready, 1)
                            v.wait_ge(mid_hi_ready, g + 1)
                            TT(mid_lo[:, c % 2, ds(2 * m + i, 1)], hid, mid_hi[:, c % 2, ds(2 * m + i, 1)].bitcast(F32),
                               ALU.subtract).then_inc(mid_ready, 1)

            add_matrix(U_SBO, norm=1)
            mlp(0, U_M1, 1)

            low, ex, lb, rest = (lower[:, n] for n in range(4))
            logits = gains[:, G_LB:G_LB + KD]
            steps(COPY(low, logits))
            steps.wait()
            TT(low, logits, low, ALU.subtract).then_inc(lb_step, 1)
            v.wait_ge(lb_step, 2)
            steps(v.reciprocal(low, ex))
            steps.wait()
            steps(TT(low, ex, low, ALU.mult))
            steps.wait()
            steps(TT(lb, low, low, ALU.subtract))
            steps(v.memset(hdiag, 0.0))
            steps.wait()
            TS(rest, lb, -1.0, 1.0, ALU.mult, ALU.add).then_inc(lb_step, 1)
            v.wait_ge(lb_step, 3)

            def nodes(t, h):
                return t.rearrange("p (n e j) -> p n e j", e=2, j=h)

            def hg_head(pp, par, current=True, following=True, previous=True, first=False):
                i = 2 * pp + par
                j = i + 1
                half = U_HG // 2 + 2 * i
                q, kk, b_ = hq[par % 2], hk[par % 2], hb[par % 2]
                q1, k1, b1 = hq[(par + 1) % 2], hk[(par + 1) % 2], hb[(par + 1) % 2]

                def sub(lv):
                    x, b = nodes(hx[lv % 3], HALVES[lv]), nodes(b_, HALVES[lv])
                    h = HALVES[lv]
                    mid = b[:, :, 0, h - 1:h].broadcast_to([P, S // (2 * h), h])
                    if lv == 0:
                        v.wait_ge(hg_decay_ready, i + 1)
                    if lv >= 3 or not first:
                        v.wait_ge(level_scored, 8 * i + 1 + lv - 2)
                    TT(x[:, :, 1], b[:, :, 1], mid, ALU.subtract)
                    TT(x[:, :, 0], mid, b[:, :, 0], ALU.subtract).then_inc(level_sub, 1)

                def mul(lv):
                    x = nodes(hx[lv % 3], HALVES[lv])
                    v.wait_ge(level_exp, 7 * i + lv + 1)
                    TT(x[:, :, 1], x[:, :, 1], nodes(q, HALVES[lv])[:, :, 1], ALU.mult)
                    TT(x[:, :, 0], x[:, :, 0], nodes(kk, HALVES[lv])[:, :, 0], ALU.mult).then_inc(level_mul, 1)

                def pred(lv):
                    v.wait_ge(level_scored, 8 * i + 2 + lv)
                    v.wait_ge(level_taken, 8 * i + 1 + lv)
                    v.sem_inc(pred_turn, 1)
                    v.copy_predicated(nodes(hdiag, HALVES[lv])[:, :, 1],
                                      level_mask[:, lv].rearrange("p (n j) -> p n j", j=HALVES[lv]),
                                      sc[lv % 2][:, 0:NB * HD].rearrange("p (n j) -> p n j", j=HALVES[lv])).then_inc(level_taken, 1)

                for k in range(HG_SLOTS):
                    if current:
                        if k == 0:
                            if not first:
                                v.wait_ge(hg_g_sigmoid, i)
                            take(half + 1, 1)
                            TT(hgraw, acc[1][:], rstd[:], ALU.mult).then_inc(evacuated[1], 1)
                            v.wait_ge(level_scored, 8 * i + 1)
                            if not first:
                                v.wait_ge(hg_pv_done, i)
                            v.sem_inc(pred_turn, 1)
                            v.copy_predicated(hdiag, same_mask[:], sc[1][:]).then_inc(level_taken, 1)
                        if 1 <= k < 8:
                            sub(k - 1)
                        if 2 <= k < 9:
                            mul(k - 2)
                        if 3 <= k < 10:
                            pred(k - 3)
                        if k == 7:
                            if not first:
                                v.wait_ge(cross_exp, i)
                            TT(hg_col[:], b_[:, P - 1:P], b_[:, 2 * P - 1:2 * P], ALU.add).then_inc(hg_col_ready, 1)
                        if k == 10:
                            v.wait_ge(cross_exp, i + 1)
                            for x, h in ((hx128, P), (hx256, 2 * P)):
                                x, q_, k_ = nodes(x, h), nodes(q, h), nodes(kk, h)
                                TT(x[:, :, 1], x[:, :, 1], q_[:, :, 1], ALU.mult)
                                last = TT(x[:, :, 0], x[:, :, 0], k_[:, :, 0], ALU.mult)
                            last.then_inc(cross_mul, 1)
                        if k == 12:
                            v.wait_ge(hg_g_log, i + 1)
                            STT(hgraw, hgraw, 0.0, hgsig, ALU.min, ALU.subtract).then_inc(hg_g_logsig, 1)
                    if current and previous and k == 9:
                        hg_normed(i - 1)
                    if current and previous and k == 11:
                        hg_low(i - 1)
                    if following:
                        if k == 5:
                            if par == -1:
                                v.wait_ge(rstd_ready, 4 * LAYERS + 3)
                            take(half + 2, 0)
                            TT(hraw, acc[0][:], rstd[:], ALU.mult).then_inc(evacuated[0], 1)
                            v.wait_ge(evacuated[0], half + 3)
                            TS(ht2, hraw, -1.0, 80.0, ALU.mult, ALU.min).then_inc(hg_f_negated, 1)
                        if k == 8:
                            v.wait_ge(hg_f_log, j + 1)
                            steps(STT(ht1, hraw, 0.0, ht1, ALU.min, ALU.subtract))
                            steps.wait()
                            TT(hfd, ht1, hraw, ALU.subtract).then_inc(hg_key_log, 1)
                        if k == 9:
                            v.wait_ge(hg_key_exp, j + 1)
                            TS(k1, hfd, rest[:, ds(j, 1)], None, ALU.mult).then_inc(hg_key_ready, 1)
                        if k == 10:
                            take(half + 2, 1)
                            TT(hraw, acc[1][:], rstd[:], ALU.mult).then_inc(evacuated[1], 1)
                            v.wait_ge(hg_bound_log, j + 1)
                            steps(TT(ht2, ht1, ht2, ALU.add))
                            steps.wait()
                            for b in range(NB):
                                c = slice(b * P, b * P + P)
                                scan = v.tensor_tensor_scan(b1[:, c], ones[:, c], ht2[:, c], 0.0, ALU.mult, ALU.add)
                            scan.then_inc(hg_decay_ready, 1)
                        if k == 12:
                            v.wait_ge(hg_q_log, j + 1)
                            STT(ht1, hraw, 0.0, ht1, ALU.min, ALU.subtract).then_inc(hg_q_logsig, 1)
                        if k == 13:
                            v.wait_ge(hg_q_sigmoid, j + 1)
                            TT(q1, hraw, ht1, ALU.mult).then_inc(hg_query_ready, 1)
                        if k == 12:
                            take(half + 3, 0)
                            TT(hvraw, acc[0][:], rstd[:], ALU.mult).then_inc(evacuated[0], 1)

            def hg_normed(i):
                v.wait_ge(hg_o_rstd, i + 1)
                steps(STT(horow, horow, gains[:, G_HG:G_HG + 1], hors, ALU.mult, ALU.mult))
                steps.wait()
                v.wait_ge(hg_g_sigmoid, i + 1)
                TT(horow, horow, hgsig, ALU.mult).then_inc(hg_o_normed, 1)

            def hg_low(i):
                v.wait_ge(hg_o_hi, i + 1)
                TT(mid_lo[:, 0, ds(i, 1)], horow, mid_hi[:, 0, ds(i, 1)].bitcast(F32), ALU.subtract).then_inc(hg_o_ready, 1)

            hg_head(0, -1, current=False)
            hg_head(0, 0, previous=False, first=True)
            hg_head(0, 1)
            with v.Fori(1, KD // 2 - 1) as pp:
                steps.enter(pp - 1, HG_STEPS)
                hg_head(pp, 0)
                hg_head(pp, 1)
                steps.leave(KD // 2 - 2)
            hg_head(KD // 2 - 1, 0)
            hg_head(KD // 2 - 1, 1, following=False)
            hg_normed(KD - 1)
            hg_low(KD - 1)
            add_matrix(U_HGO, norm=3)
            mlp(1, U_M2, 3)

        @block.scalar
        def _(a):
            steps = Steps(a, act_step)
            ACTV = a.activation
            for i, g in ((G_ATT_PRE, attn_pre_g), (G_ATT_POST, attn_post_g), (G_FFN_PRE, ffn_pre_g), (G_FFN_POST, ffn_post_g)):
                a.dma_start(grow[i:i + 16, :], g.rearrange("l (j c) -> (l j) c", c=P)).then_inc(consts_in, 16)
            a.dma_start(grow[G_B2:G_B2 + 32, :], norm_gains_2.rearrange("l w (j c) -> (l w j) c", c=P)).then_inc(consts_in, 16)
            a.dma_start(grow[G_LB:G_LB + 8, :], hg_lb_logits_2.rearrange("l (j c) -> (l j) c", c=P)).then_inc(consts_in, 16)
            a.dma_start(grow[G_DIFF:G_DIFF + LAYERS, :], diff_sub_g).then_inc(consts_in, 16)
            a.dma_start(grow[G_HG:G_HG + 1, :], hg_norm_gain_2).then_inc(consts_in, 16)
            for i in range(2):
                a.dma_start(grow[G_SBQ:G_SBQ + 1, i * HD:i * HD + HD], sb_q_gain_2).then_inc(consts_in, 16)
                a.dma_start(grow[G_SBK:G_SBK + 1, i * HD:i * HD + HD], sb_k_gain_2).then_inc(consts_in, 16)
            for i, w in enumerate((lam_q1, lam_k1, lam_q2, lam_k2)):
                a.dma_start(lam_in[:, i], w.partition_broadcast(P)).then_inc(consts_in, 16)
            a.dma_start(pos_i, positions.rearrange("b s -> (b s)").partition_broadcast(P)).then_inc(consts_in, 16)
            a.wait_ge(vec_consts, 1)
            with nc.allow_non_contiguous_dma(reason="16 words"):
                a.dma_start(lconst[120:P, :, 2], forget_bias.rearrange("l h -> h l")).then_inc(consts_in, 16)
            def high_part(x_n, j, gain):
                a.wait_ge(x_ready, x_n + j + 1)
                ACTV(h_hi[:, j], xT[:, j], ACT.Identity, scale=gain).then_inc(h_hi_ready, 1)

            def square_of(src, i):
                ACTV(square[i], src, ACT.Square).then_inc(square_ready, 1)

            def inv_rms(a_n, width):
                a.wait_ge(aux_done, a_n + 1)
                ACTV(logs, aux[:], ACT.Ln, bias=eps_col[:, 0:1], scale=1.0 / width).then_inc(aux_free, 1)
                a.wait_ge(aux_free, a_n + 1)
                ACTV(rstd[:], logs, ACT.Exp, scale=-0.5).then_inc(rstd_ready, 1)

            def pre_norm(x_n, n, gain_of):
                for j in range(KD):
                    high_part(x_n, j, gain_of(j))
                    if j >= 2:
                        a.wait_ge(pair_added, n * (KD // 2) + j // 2)
                    square_of(xT[:, j], j % 2)

            a.preload_act_table_set("natural_log_exp_and_others")
            a.wait_ge(gains_ready, 1)
            pre_norm(0, 0, lambda j: gains[:, G_ATT_PRE + j:G_ATT_PRE + j + 1])
            inv_rms(0, D)
            a.wait_ge(vec_consts, 4)
            ACTV(lam_e, lam_s, ACT.Exp).then_inc(act_consts, 1)
            a.wait_ge(vec_consts, 5)
            ACTV(sinT[:], red, ACT.Sin).then_inc(act_consts, 1)
            ACTV(cosT[:], red, ACT.Sin, scale=0.5).then_inc(act_consts, 1)
            a.wait_ge(act_consts, 3)
            ACTV(cosT[:], cosT[:], ACT.Square).then_inc(act_consts, 1)
            a.preload_act_table_set("natural_log_exp_and_others")

            with a.Fori(0, LAYERS) as l:
                steps.enter(l, ACT_STEPS_LAYER)
                A = l * A_LAYER
                half0 = l * (U_LAYER // 2)
                a.wait_ge(layer_const, l + 1)

                def take_t(p, i):
                    ti = T_BASE[p] + i
                    t = i if p < NDIFF else i // 2
                    a.wait_ge(t_done, l * T_BASE[PAIRS] + ti + 1)
                    ACTV(probT[ti % 2][:, 0:(t + 1) * P], tp[ti % 2][:, 0:(t + 1) * P], ACT.Copy).then_inc(t_taken, 1)

                def high_output(p):
                    if p < NDIFF:
                        a.wait_ge(o_normed, l * NDIFF + p + 1)
                        src = onrm
                    else:
                        a.wait_ge(po_taken, l * PAIRS + p + 1)
                        src = orow
                    ACTV(mid_hi[:, 0, p], src, ACT.Copy).then_inc(o_hi_ready, 1)

                for p in range(-1, PAIRS):
                    for k in range(SLOTS):
                        if p == -1:
                            continue
                        if k == 0 and 0 <= p - 1 < NDIFF:
                            a.wait_ge(po_taken, l * PAIRS + p)
                            ACTV(osq, orow, ACT.Square).then_inc(o_square, 1)
                        if k == 0 and p - 1 >= NDIFF:
                            high_output(p - 1)
                        if k < 8:
                            n = (k // 2 + 1) * P
                            a.wait_ge(max_done, l * 64 + p * 8 + k + 1)
                            ACTV(prob[k % 4][:, 0:n], sc[k % 2][:, 0:n], ACT.Exp, bias=stat[:, k % 4:k % 4 + 1],
                                 accum_out=stat[:, 4 + k % 4:5 + k % 4]).then_inc(exp_done, 1)
                        if k == 1:
                            v_use = AUX[("v", p)]
                            a.wait_ge(aux_done, A + v_use + 1)
                            ACTV(vtok.rearrange("p j c -> p (j c)"), aux[:], ACT.Copy).then_inc(aux_free, 1)
                        if k == 5 and 0 <= p - 1 < NDIFF:
                            n = AUX[("o_norm", p - 1)]
                            a.wait_ge(aux_done, A + n + 1)
                            ACTV(ologs, aux[:], ACT.Ln, bias=eps_col[:, 0:1], scale=1.0 / (2 * HD)).then_inc(aux_free, 1)
                            a.wait_ge(aux_free, A + n + 1)
                            ACTV(ologs, ologs, ACT.Exp, scale=-0.5).then_inc(o_rstd, 1)
                        if k == 7 and 0 <= p - 1 < NDIFF:
                            high_output(p - 1)
                        if p < NDIFF and k >= 3 and k % 2 == 1 and (k - 3) // 2 < 4:
                            take_t(p, (k - 3) // 2)
                        if p >= NDIFF and 2 <= k < 10:
                            take_t(p, k - 2)
                    if p == -1:
                        f = slice(96, P)
                        a.wait_ge(f_ready, l + 1)
                        steps(ACTV(ologs_f[f], raw_f[f], ACT.Abs))
                        steps.wait()
                        steps(ACTV(ologs_f[f], ologs_f[f], ACT.Exp, scale=-1.0))
                        steps.wait()
                        ACTV(ologs_f[f], ologs_f[f], ACT.Ln, bias=1.0).then_inc(f_log, 1)
                high_output(PAIRS - 1)

                def square_loop(half, added):
                    with a.Fori(0, KD // 2) as m:
                        for i in range(2):
                            a.wait_ge(evacuated[i], half + m + 1)
                            a.wait_ge(square_added, added + 2 * m + i - 1)
                            square_of(yT[:, ds(2 * m + i, 1)], i)

                square_loop(half0 + U_OUT // 2, added_base(2 * l))
                inv_rms(A + AUX["norm_att_post"], D)
                pre_norm(l * 16 + 8, 2 * l + 1, lambda j: layer_gain[:, 1, j:j + 1])
                inv_rms(A + AUX["norm_ffn"], D)
                for kind, c, u in FFN_ORDER:
                    first, n = FF1_CHUNKS[c]
                    half = half0 + u // 2
                    if kind == "gu":
                        with a.Fori(0, n) as j:
                            steps.enter(j, 2)
                            g = l * FF1_TILES + first + j
                            a.wait_ge(evacuated[0], half + j + 1)
                            steps(ACTV(gate_t, gate, ACT.Abs))
                            steps.wait()
                            steps(ACTV(gate_t2, gate_t, ACT.Exp, scale=-1.0))
                            steps.wait()
                            ACTV(gate_t2, gate_t2, ACT.Ln, bias=1.0).then_inc(gate_log, 1)
                            a.wait_ge(gate_ls, g + 1)
                            ACTV(gate_t2, gate_t, ACT.Exp).then_inc(gate_sig, 1)
                            a.wait_ge(hid_ready, g + 1)
                            ACTV(mid_hi[:, c % 2, ds(j, 1)], hid, ACT.Copy).then_inc(mid_hi_ready, 1)
                            steps.leave(n)
                    elif c == 2:
                        square_loop(half, added_base(2 * l + 1))
                inv_rms(A + AUX["norm_ffn_post"], D)
                pre_norm(l * 16 + 16, 2 * l + 2, lambda j: layer_gain[:, 3, j:j + 1])
                inv_rms(A + A_LAYER, D)
                steps.leave(LAYERS)

            def pre_norm2(norm, u):
                added = block2_norm(norm)[2]
                for j in range(KD):
                    gain = G_B2 + norm * KD + j
                    a.wait_ge(evacuated[j % 2], u // 2 + j // 2 + 1)
                    ACTV(h_hi[:, j], xT[:, j], ACT.Identity, scale=gains[:, gain:gain + 1]).then_inc(h_hi_ready, 1)
                    a.wait_ge(square_added, added + j - 1)
                    square_of(xT[:, j], j % 2)

            def sb_pair(pp, par, current=True, following=True, previous=True):
                p = 2 * pp + par
                half = U_SB // 2 + 3 * pp
                aux_n = A_SB + 3 + 3 * p

                def softplus_log(m):
                    parts = [sb_log[:, at:at + n] for _, _, at, n in Z_PARTS]

                    def magnitude(i):
                        a.wait_ge(z_done, 6 * p + 3 * m + i + 1)
                        steps(ACTV(parts[i], z[Z_PARTS[i][0]][:, 0:Z_PARTS[i][3]], ACT.Abs))

                    magnitude(0)
                    magnitude(1)
                    steps.wait()
                    steps(ACTV(parts[0], parts[0], ACT.Exp, scale=-1.0))
                    magnitude(2)
                    steps.wait()
                    ACTV(parts[0], parts[0], ACT.Ln, bias=1.0).then_inc(z_log, 1)
                    for i in (1, 2):
                        steps(ACTV(parts[i], parts[i], ACT.Exp, scale=-1.0))
                        steps.wait()
                        ACTV(parts[i], parts[i], ACT.Ln, bias=1.0).then_inc(z_log, 1)

                def weights(m):
                    for i, (bank, _, at, n) in enumerate(Z_PARTS):
                        a.wait_ge(logw_done, 6 * p + 3 * m + i + 1)
                        e = ACTV(sb_w[:, at:at + n], z[bank][:, 0:n], ACT.Exp)
                    e.then_inc(w_ready, 1)

                def raw_norm(i, k, first, last):
                    u = 3 * (par + 1) + i
                    if k == first:
                        a.wait_ge(evacuated[u % 2], half + u // 2 + 1)
                        ACTV(sb_sq, raw, ACT.Square).then_inc(raw_square, 1)
                    if k == last:
                        a.wait_ge(aux_done, aux_n + 2 + i)
                        ACTV(sb_logs, aux[:], ACT.Ln, bias=eps_col[:, 0:1], scale=1.0 / HD).then_inc(aux_free, 1)
                        a.wait_ge(aux_free, aux_n + 2 + i)
                        ACTV(sb_logs, sb_logs, ACT.Exp, scale=-0.5).then_inc(raw_rstd, 1)

                for k in range(SLOTS):
                    if current and k in (0, 6):
                        softplus_log(k // 6)
                    if current and previous and k == 3:
                        sb_high(p - 1)
                    if current and k == 2:
                        a.wait_ge(aux_done, aux_n + 1)
                        ACTV(vtok.rearrange("p j c -> p (j c)"), aux[:], ACT.Copy).then_inc(aux_free, 1)
                    if current and k in (5, 11):
                        weights(k // 6)
                    if following:
                        raw_norm(0, k, 4, 6)
                        raw_norm(1, k, 8, 10)

            def sb_high(p):
                a.wait_ge(sb_o_taken, p + 2)
                ACTV(mid_hi[:, 0, ds(p, 1)], sb_orow, ACT.Copy).then_inc(sb_o_hi, 1)

            z = [sc[0], sc[1], tp[0]]
            a.sem_inc(w_ready, 1)
            sb_pair(0, -1, current=False)
            sb_pair(0, 0, previous=False)
            sb_pair(0, 1)
            with a.Fori(1, PAIRS // 2 - 1) as pp:
                steps.enter(pp - 1, SB_ACT_STEPS)
                sb_pair(pp, 0)
                sb_pair(pp, 1)
                steps.leave(PAIRS // 2 - 2)
            sb_pair(PAIRS // 2 - 1, 0)
            sb_pair(PAIRS // 2 - 1, 1, following=False)
            sb_high(PAIRS - 1)

            def mlp(i_mlp):
                for kind, c, u in MLP_UNITS:
                    if kind == "up":
                        with a.Fori(0, KD) as j:
                            a.wait_ge(hid_ready, MID1 + i_mlp * (FF2 // P) + 8 * c + j + 1)
                            ACTV(mid_hi[:, c % 2, ds(j, 1)], hid, ACT.Copy).then_inc(mid_hi_ready, 1)

            pre_norm2(1, U_SBO)
            inv_rms(A_M1, D)
            mlp(0)

            pre_norm2(2, U_M1 + 56)
            a.wait_ge(lb_step, 1)
            ACTV(lower[:, 1], lower[:, 0], ACT.Exp).then_inc(lb_step, 1)
            lb = lower[:, 2]

            def log_sigmoid_part(t, src, done):
                steps(ACTV(t, src, ACT.Abs))
                steps.wait()
                steps(ACTV(t, t, ACT.Exp, scale=-1.0))
                steps.wait()
                ACTV(t, t, ACT.Ln, bias=1.0).then_inc(done, 1)

            def hg_head(pp, par, current=True, following=True, previous=True, first=False):
                i = 2 * pp + par
                j = i + 1
                half = U_HG // 2 + 2 * i
                b_ = hb[par % 2]
                for k in range(HG_SLOTS):
                    if current:
                        if k == 1:
                            a.wait_ge(aux_done, a_hgv(i, first) + 1)
                            ACTV(hvtok.rearrange("p j c -> p (j c)"), aux[:], ACT.Copy).then_inc(aux_free, 1)
                        if 1 <= k < 8:
                            lv = k - 1
                            a.wait_ge(level_sub, 7 * i + lv + 1)
                            ACTV(hx[lv % 3], hx[lv % 3], ACT.Exp).then_inc(level_exp, 1)
                        if k == 11:
                            a.wait_ge(evacuated[1], half + 2)
                            if not first:
                                a.wait_ge(hg_o_normed, i)
                            log_sigmoid_part(hgsig, hgraw, hg_g_log)
                        if k == 13:
                            a.wait_ge(hg_g_logsig, i + 1)
                            ACTV(hgsig, hgraw, ACT.Exp).then_inc(hg_g_sigmoid, 1)
                        if k == 9:
                            a.wait_ge(hg_decay_ready, i + 1)
                            a.wait_ge(hg_col_ready, i + 1)
                            if not first:
                                a.wait_ge(cross_scored, i)
                            end = [b_[:, b * P + P - 1:b * P + P] for b in range(NB)]
                            blk = [slice(b * P, b * P + P) for b in range(NB)]
                            for b in (1, 3):
                                ACTV(hx128[:, blk[b]], b_[:, blk[b]], ACT.Exp)
                            for b in (0, 2):
                                ACTV(hx128[:, blk[b]], b_[:, blk[b]], ACT.Exp, bias=end[b], scale=-1.0)
                            ACTV(hx256[:, blk[2]], b_[:, blk[2]], ACT.Exp)
                            ACTV(hx256[:, blk[3]], b_[:, blk[3]], ACT.Exp, bias=end[2])
                            ACTV(hx256[:, blk[1]], b_[:, blk[1]], ACT.Exp, bias=end[1], scale=-1.0)
                            ACTV(hx256[:, blk[0]], b_[:, blk[0]], ACT.Exp, bias=hg_col[:, 0:1],
                                 scale=-1.0).then_inc(cross_exp, 1)
                        if k == 12:
                            a.wait_ge(cross_scored, i + 1)
                            if not first:
                                a.wait_ge(hg_pv_done, i)
                            ACTV(hoff[:, 0:S], tp[0][:], ACT.Copy)
                            ACTV(hoff[:, S:S + 2 * P], tp[1][:, 0:2 * P], ACT.Copy).then_inc(cross_taken, 1)
                        if k == 15:
                            hg_square(i)
                    if current and previous and k == 2:
                        hg_inv_rms(i - 1)
                    if current and previous and k == 10:
                        hg_high(i - 1)
                    if following:
                        if k == 5:
                            a.wait_ge(evacuated[0], half + 3)
                            log_sigmoid_part(ht1, hraw, hg_f_log)
                        if k == 9:
                            a.wait_ge(hg_f_negated, j + 1)
                            steps(ACTV(ht2, ht2, ACT.Exp))
                            steps.wait()
                            ACTV(ht2, ht2, ACT.Ln, bias=1.0, scale=lb[:, ds(j, 1)]).then_inc(hg_bound_log, 1)
                        if k == 8:
                            a.wait_ge(hg_key_log, j + 1)
                            ACTV(hfd, hfd, ACT.Exp).then_inc(hg_key_exp, 1)
                        if k == 11:
                            a.wait_ge(evacuated[1], half + 3)
                            a.wait_ge(hg_decay_ready, j + 1)
                            log_sigmoid_part(ht1, hraw, hg_q_log)
                        if k == 12:
                            a.wait_ge(hg_q_logsig, j + 1)
                            ACTV(ht1, ht1, ACT.Exp).then_inc(hg_q_sigmoid, 1)

            def hg_square(i):
                a.wait_ge(hg_pv_done, i + 1)
                ACTV(horow, po[:], ACT.Copy).then_inc(hg_o_taken, 1)
                a.wait_ge(hg_o_taken, i + 1)
                ACTV(hosq, horow, ACT.Square).then_inc(hg_o_square, 1)

            def hg_inv_rms(i, last=False):
                n = a_hgv(i + 1) + (0 if last else 1)
                a.wait_ge(aux_done, n + 1)
                ACTV(hors, aux[:], ACT.Ln, bias=eps_col[:, 0:1], scale=1.0 / P).then_inc(aux_free, 1)
                a.wait_ge(aux_free, n + 1)
                ACTV(hors, hors, ACT.Exp, scale=-0.5).then_inc(hg_o_rstd, 1)

            def hg_high(i):
                a.wait_ge(hg_o_normed, i + 1)
                ACTV(mid_hi[:, 0, ds(i, 1)], horow, ACT.Copy).then_inc(hg_o_hi, 1)

            inv_rms(A_HG, D)
            hg_head(0, -1, current=False)
            hg_head(0, 0, previous=False, first=True)
            hg_head(0, 1)
            with a.Fori(1, KD // 2 - 1) as pp:
                steps.enter(pp - 1, HG_ACT_STEPS)
                hg_head(pp, 0)
                hg_head(pp, 1)
                steps.leave(KD // 2 - 2)
            hg_head(KD // 2 - 1, 0)
            hg_head(KD // 2 - 1, 1, following=False)
            hg_inv_rms(KD - 1, last=True)
            hg_high(KD - 1)
            pre_norm2(3, U_HGO)
            inv_rms(A_M2, D)
            mlp(1)
            for j in range(KD):
                a.wait_ge(pre_pe, KD + 2 + j + 1)
                ACTV(x_tok[:, :, j * P:j * P + P], tp[j % 2].rearrange("p (t c) -> p t c", t=NB),
                     ACT.Copy).then_inc(out_ready, 1)


_INPUTS = ["x", "positions", "attn_pre_g", "w_in", "forget_bias", "lam_q1", "lam_k1", "lam_q2", "lam_k2", "diff_sub_g",
           "w_out", "attn_post_g", "ffn_pre_g", "w_gate", "w_up", "w_down", "ffn_post_g", "norm_gains_2",
           "sb_w_qkv_2", "sb_q_gain_2", "sb_k_gain_2", "sb_w_o_2", "hg_w_in_2", "hg_lb_logits_2", "hg_norm_gain_2",
           "hg_w_o_2", "mlp_w1_2", "mlp_w2_2"]


def kernel(**inputs):
    import numpy as _np
    import concourse.bacc as _bacc
    from concourse import mybir as _mybir
    from concourse.bass_utils import run_bass_kernel_spmd as _run

    nc = _bacc.Bacc("TRN2", target_bir_lowering=False, num_devices=1)
    arrays, args = {}, []
    for name in _INPUTS:
        a = _np.ascontiguousarray(inputs[name])
        arrays[f"in_{name}_dram"] = a
        args.append(nc.dram_tensor(f"in_{name}_dram", a.shape, _mybir.dt.from_np(a.dtype), kind="ExternalInput").ap())
    out = nc.dram_tensor("out_dram", inputs["x"].shape, _mybir.dt.float32, kind="ExternalOutput").ap()
    two_blocks(nc, *args, out)
    result = _run(nc, [arrays], core_ids=[0])
    return result.results[0]["out_dram"]
```
